# Optimizing a Trainium2 kernel written in Bass

```python
import math
import jax, jax.numpy as jnp
from jax import lax
import numpy as np

D_MODEL = 1024
BATCH = 1
SEQ = 512
DEPTH = 2
DEC_BATCH = 8
DEC_SEQ = 4
PAST_LEN = 4096
PAGE_SIZE = 128

ML_HEADS = 4
ML_DK = 64
ML_DV = 64
ML_W = ML_HEADS * ML_DV
GD_HEADS = 4
GD_DK = 128
GD_DV = 128
GD_KW = GD_HEADS * GD_DK
GD_VW = GD_HEADS * GD_DV
GD_CONV = 4
GD_CONV_CH = 2 * GD_KW + GD_VW
HG_HEADS = 4
HG_DK = 64
HG_DV = 64
HG_W = HG_HEADS * HG_DV
MIX_W = ML_W + GD_VW + HG_W
D_FF = -(-8 * D_MODEL // (3 * 256)) * 256
CHUNK = 64
EPS = 1e-6
NEG = -1e30
IN_SIZES = (ML_HEADS * ML_DK, ML_HEADS * ML_DK, ML_W, ML_W, ML_HEADS, ML_HEADS,
            GD_KW, GD_KW, GD_VW, GD_VW, GD_HEADS, GD_HEADS,
            HG_HEADS * HG_DK, HG_HEADS * HG_DK, HG_W, HG_W)
IN_WIDTH = sum(IN_SIZES)

kernel_name = 'hymba_style_mlstm_gdn_hgrn2_step'

def _split_points():
    pts, acc = [], 0
    for s in IN_SIZES[:-1]:
        acc += s
        pts.append(acc)
    return pts

def _rmsnorm(x, w):
    xf = x.astype(jnp.float32)
    return xf * lax.rsqrt(jnp.mean(xf * xf, axis=-1, keepdims=True) + EPS) * w.astype(jnp.float32)

def _head_norm(o, w):
    return o * lax.rsqrt(jnp.mean(o * o, axis=-1, keepdims=True) + EPS) * w.astype(jnp.float32)

def _l2norm(x):
    return x * lax.rsqrt(jnp.sum(x * x, axis=-1, keepdims=True) + EPS)

def _heads(a, h):
    b, t, _ = a.shape
    return jnp.transpose(a.reshape(b, t, h, -1), (0, 2, 1, 3))

def _merge(a):
    b, h, t, d = a.shape
    return jnp.transpose(a, (0, 2, 1, 3)).reshape(b, t, h * d)

def _chunk_len(t):
    return CHUNK if t % CHUNK == 0 else t

def _to_chunks(a, L):
    b, h, t = a.shape[:3]
    return jnp.moveaxis(a.reshape((b, h, t // L, L) + a.shape[3:]), 2, 0)

def _from_chunks(a):
    a = jnp.moveaxis(a, 0, 2)
    b, h, nc, L, d = a.shape
    return a.reshape(b, h, nc * L, d)

def _masked_exp(mask, logw):
    return jnp.where(mask, jnp.exp(jnp.where(mask, logw, 0.0)), 0.0)

def _mlstm_scan(q, k, v, logi, logf, C0, n0, m0):
    L = _chunk_len(q.shape[2])
    causal = jnp.tril(jnp.ones((L, L), bool))

    def step(carry, inp):
        C, n, m = carry
        qc, kc, vc, li, lf = inp
        b = jnp.cumsum(lf, axis=-1)
        inter = b + m[..., None]
        draw = b[..., :, None] - b[..., None, :] + li[..., None, :]
        mt = jnp.maximum(inter, jnp.max(jnp.where(causal, draw, NEG), axis=-1))
        w_inter = jnp.exp(inter - mt)
        qk = jnp.einsum('bhtd,bhsd->bhts', qc, kc) * _masked_exp(causal, draw - mt[..., None])
        num = w_inter[..., None] * jnp.einsum('bhtd,bhde->bhte', qc, C) + jnp.einsum('bhts,bhse->bhte', qk, vc)
        den = w_inter * jnp.einsum('bhtd,bhd->bht', qc, n) + jnp.sum(qk, axis=-1)
        h = num / jnp.maximum(jnp.abs(den), jnp.exp(-mt))[..., None]
        m_new = mt[..., -1]
        bl = b[..., -1]
        w_c = jnp.exp(bl + m - m_new)
        ks = kc * jnp.exp(bl[..., None] - b + li - m_new[..., None])[..., None]
        C_new = w_c[..., None, None] * C + jnp.einsum('bhsd,bhse->bhde', ks, vc)
        n_new = w_c[..., None] * n + jnp.sum(ks, axis=2)
        return (C_new, n_new, m_new), h

    xs = tuple(_to_chunks(a, L) for a in (q, k, v, logi, logf))
    (C, n, m), h = lax.scan(step, (C0, n0, m0), xs)
    return _from_chunks(h), C, n, m

def _gdn_scan(q, k, v, g, beta, S0):
    L = _chunk_len(q.shape[2])
    incl = jnp.tril(jnp.ones((L, L), bool))
    strict = jnp.tril(jnp.ones((L, L), bool), -1)
    eye = jnp.eye(L, dtype=jnp.float32)

    def step(S, inp):
        qc, kc, vc, gc, bc = inp
        d = jnp.cumsum(gc, axis=-1)
        gam = _masked_exp(incl, d[..., :, None] - d[..., None, :])
        a = jnp.where(strict, bc[..., :, None] * jnp.einsum('bhtd,bhsd->bhts', kc, kc) * gam, 0.0)
        rhs = jnp.concatenate([vc * bc[..., None], kc * (bc * jnp.exp(d))[..., None]], axis=-1)
        sol = lax.linalg.triangular_solve(a + eye, rhs, left_side=True, lower=True)
        w_v, w_k = sol[..., :GD_DV], sol[..., GD_DV:]
        u = w_v - jnp.einsum('bhld,bhde->bhle', w_k, S)
        attn = jnp.einsum('bhtd,bhsd->bhts', qc, kc) * gam
        o = jnp.einsum('bhtd,bhde->bhte', qc * jnp.exp(d)[..., None], S) + jnp.einsum('bhts,bhse->bhte', attn, u)
        dl = d[..., -1]
        S_new = jnp.exp(dl)[..., None, None] * S + jnp.einsum(
            'bhsd,bhse->bhde', kc * jnp.exp(dl[..., None] - d)[..., None], u)
        return S_new, o

    xs = tuple(_to_chunks(a, L) for a in (q, k, v, g, beta))
    S, o = lax.scan(step, S0, xs)
    return _from_chunks(o), S

def _hgrn_scan(q, logf, k, i, S0):
    L = _chunk_len(q.shape[2])
    incl = jnp.tril(jnp.ones((L, L), bool))[:, :, None]

    def step(S, inp):
        qc, lfc, kc, ic = inp
        bc = jnp.cumsum(lfc, axis=2)
        dec = _masked_exp(incl, bc[:, :, :, None, :] - bc[:, :, None, :, :])
        attn = jnp.einsum('bhtc,bhsc,bhtsc->bhts', qc, kc, dec)
        o = jnp.einsum('bhtc,bhce->bhte', qc * jnp.exp(bc), S) + jnp.einsum('bhts,bhse->bhte', attn, ic)
        bl = bc[:, :, -1]
        S_new = jnp.exp(bl)[..., None] * S + jnp.einsum('bhsc,bhse->bhce', kc * jnp.exp(bl[:, :, None] - bc), ic)
        return S_new, o

    xs = tuple(_to_chunks(a, L) for a in (q, logf, k, i))
    S, o = lax.scan(step, S0, xs)
    return _from_chunks(o), S

def _block(x, C0, n0, m0, S_gd0, buf0, S_hg0, lb, norm1_w, w_in, ml_i_bias, ml_f_bias, ml_norm_w,
           gd_conv_w, gd_A_log, gd_dt_bias, gd_norm_w, hg_norm_w, w_out, norm2_w, w_gate_up, w_down):
    f32 = jnp.float32
    dt = x.dtype
    T = x.shape[1]
    h = _rmsnorm(x, norm1_w).astype(dt)
    proj = jnp.einsum('btd,de->bte', h, w_in).astype(f32)
    (ml_q, ml_k, ml_v, ml_o, ml_i, ml_f,
     gd_q, gd_k, gd_v, gd_g, gd_a, gd_b,
     hg_q, hg_f, hg_i, hg_g) = jnp.split(proj, _split_points(), axis=-1)

    q = _heads(ml_q, ML_HEADS)
    k = _heads(ml_k, ML_HEADS) * (ML_DK ** -0.5)
    v = _heads(ml_v, ML_HEADS)
    logi = jnp.swapaxes(ml_i + ml_i_bias.astype(f32), 1, 2)
    logf = jnp.swapaxes(jax.nn.log_sigmoid(ml_f + ml_f_bias.astype(f32)), 1, 2)
    h_ml, C, n, m = _mlstm_scan(q, k, v, logi, logf, C0.astype(f32), n0.astype(f32), m0.astype(f32))
    h_ml = jax.nn.sigmoid(_heads(ml_o, ML_HEADS)) * h_ml
    y_ml = _merge(_head_norm(h_ml, ml_norm_w))

    conv_in = jnp.concatenate([gd_q, gd_k, gd_v], axis=-1)
    full = jnp.concatenate([buf0.astype(f32), conv_in], axis=1)
    cw = gd_conv_w.astype(f32)
    conv = jax.nn.silu(sum(full[:, j:j + T] * cw[j] for j in range(GD_CONV)))
    new_buf = full[:, T:]
    cq, ck, cv = jnp.split(conv, [GD_KW, 2 * GD_KW], axis=-1)
    q = _l2norm(_heads(cq, GD_HEADS)) * (GD_DK ** -0.5)
    k = _l2norm(_heads(ck, GD_HEADS))
    v = _heads(cv, GD_HEADS)
    g = -jnp.exp(gd_A_log.astype(f32)) * jax.nn.softplus(gd_a + gd_dt_bias.astype(f32))
    beta = jax.nn.sigmoid(gd_b)
    o_gd, S_gd = _gdn_scan(q, k, v, jnp.swapaxes(g, 1, 2), jnp.swapaxes(beta, 1, 2), S_gd0.astype(f32))
    y_gd = _merge(_head_norm(o_gd, gd_norm_w) * jax.nn.silu(_heads(gd_g, GD_HEADS)))

    lbh = lb.reshape(HG_HEADS, 1, HG_DK)
    z = _heads(hg_f, HG_HEADS)
    sz = jax.nn.sigmoid(z)
    logf_hg = jnp.log(lbh + (1.0 - lbh) * sz)
    k_hg = (1.0 - lbh) * (1.0 - sz)
    q_hg = jax.nn.silu(_heads(hg_q, HG_HEADS))
    i_hg = _heads(hg_i, HG_HEADS)
    o_hg, S_hg = _hgrn_scan(q_hg, logf_hg, k_hg, i_hg, S_hg0.astype(f32))
    y_hg = _merge(_head_norm(o_hg, hg_norm_w) * jax.nn.silu(_heads(hg_g, HG_HEADS)))

    mix = jnp.concatenate([y_ml, y_gd, y_hg], axis=-1).astype(dt)
    x = x + jnp.einsum('bte,ed->btd', mix, w_out)

    h2 = _rmsnorm(x, norm2_w).astype(dt)
    gate, up = jnp.split(jnp.einsum('btd,df->btf', h2, w_gate_up), 2, axis=-1)
    x = x + jnp.einsum('btf,fd->btd', jax.nn.silu(gate) * up, w_down)
    return x, C, n, m, S_gd, new_buf, S_hg

def _trunk(x, states, lb, weights, final_norm_w):
    C, n, m, S_gd, buf, S_hg = states
    (norm1_w, w_in, ml_i_bias, ml_f_bias, ml_norm_w, gd_conv_w, gd_A_log, gd_dt_bias, gd_norm_w,
     hg_norm_w, w_out, norm2_w, w_gate_up, w_down) = weights
    outs = []
    for l in range(DEPTH):
        x, *new = _block(x, C[l], n[l], m[l], S_gd[l], buf[l], S_hg[l], lb[l], norm1_w[l], w_in[l],
                         ml_i_bias[l], ml_f_bias[l], ml_norm_w[l], gd_conv_w[l], gd_A_log[l], gd_dt_bias[l],
                         gd_norm_w[l], hg_norm_w[l], w_out[l], norm2_w[l], w_gate_up[l], w_down[l])
        outs.append(new)
    y = _rmsnorm(x, final_norm_w).astype(x.dtype)
    st = [jnp.stack([o[i] for o in outs]).astype(x.dtype) for i in range(6)]
    return (y, *st)

def setup_inputs(seed: int = 0) -> dict:
    key = jax.random.key(seed)
    ks = jax.random.split(key, 24)
    f32 = jnp.float32

    def nrm(k, shape, scale):
        return jax.random.normal(k, shape, f32) * scale

    dt = jnp.exp(jax.random.uniform(ks[14], (DEPTH, GD_HEADS), f32, math.log(1e-3), math.log(0.1)))
    return {
        'x_prompt': nrm(ks[0], (BATCH, SEQ, D_MODEL), 1.0),
        'x_sample': nrm(ks[1], (DEC_BATCH, DEC_SEQ, D_MODEL), 1.0),
        'state_mlstm_C': nrm(ks[2], (DEPTH, DEC_BATCH, ML_HEADS, ML_DK, ML_DV), 0.1),
        'state_mlstm_n': jnp.abs(nrm(ks[3], (DEPTH, DEC_BATCH, ML_HEADS, ML_DK), 0.1)),
        'state_mlstm_m': nrm(ks[4], (DEPTH, DEC_BATCH, ML_HEADS), 0.5),
        'state_gdn_S': nrm(ks[5], (DEPTH, DEC_BATCH, GD_HEADS, GD_DK, GD_DV), 0.1),
        'state_gdn_conv': nrm(ks[6], (DEPTH, DEC_BATCH, GD_CONV - 1, GD_CONV_CH), 1.0),
        'state_hgrn_S': nrm(ks[7], (DEPTH, DEC_BATCH, HG_HEADS, HG_DK, HG_DV), 0.3),
        'norm1_w': 1.0 + nrm(ks[8], (DEPTH, D_MODEL), 0.02),
        'w_in': nrm(ks[9], (DEPTH, D_MODEL, IN_WIDTH), D_MODEL ** -0.5),
        'ml_i_bias': nrm(ks[10], (DEPTH, ML_HEADS), 0.1),
        'ml_f_bias': 3.0 + 3.0 * jax.random.uniform(ks[11], (DEPTH, ML_HEADS), f32),
        'ml_norm_w': 1.0 + nrm(ks[12], (DEPTH, ML_DV), 0.02),
        'gd_conv_w': nrm(ks[13], (DEPTH, GD_CONV, GD_CONV_CH), GD_CONV ** -0.5),
        'gd_A_log': jnp.log(jax.random.uniform(ks[15], (DEPTH, GD_HEADS), f32, 1.0, 16.0)),
        'gd_dt_bias': dt + jnp.log(-jnp.expm1(-dt)),
        'gd_norm_w': 1.0 + nrm(ks[16], (DEPTH, GD_DV), 0.02),
        'hg_lower_bounds': nrm(ks[17], (DEPTH, HG_HEADS * HG_DK), 0.1),
        'hg_norm_w': 1.0 + nrm(ks[18], (DEPTH, HG_DV), 0.02),
        'w_out': nrm(ks[19], (DEPTH, MIX_W, D_MODEL), MIX_W ** -0.5),
        'norm2_w': 1.0 + nrm(ks[20], (DEPTH, D_MODEL), 0.02),
        'w_gate_up': nrm(ks[21], (DEPTH, D_MODEL, 2 * D_FF), D_MODEL ** -0.5),
        'w_down': nrm(ks[22], (DEPTH, D_FF, D_MODEL), D_FF ** -0.5),
        'final_norm_w': 1.0 + nrm(ks[23], (D_MODEL,), 0.02),
    }

def reference(x_prompt, x_sample, state_mlstm_C, state_mlstm_n, state_mlstm_m, state_gdn_S, state_gdn_conv,
              state_hgrn_S, norm1_w, w_in, ml_i_bias, ml_f_bias, ml_norm_w, gd_conv_w, gd_A_log, gd_dt_bias,
              gd_norm_w, hg_lower_bounds, hg_norm_w, w_out, norm2_w, w_gate_up, w_down, final_norm_w):
    f32 = jnp.float32
    probs = jax.nn.softmax(hg_lower_bounds.astype(f32), axis=0)
    lb = jnp.cumsum(probs, axis=0) - probs[0]
    weights = (norm1_w, w_in, ml_i_bias, ml_f_bias, ml_norm_w, gd_conv_w, gd_A_log, gd_dt_bias, gd_norm_w,
               hg_norm_w, w_out, norm2_w, w_gate_up, w_down)
    B = x_prompt.shape[0]
    zero_states = (jnp.zeros((DEPTH, B, ML_HEADS, ML_DK, ML_DV), f32),
                   jnp.zeros((DEPTH, B, ML_HEADS, ML_DK), f32),
                   jnp.zeros((DEPTH, B, ML_HEADS), f32),
                   jnp.zeros((DEPTH, B, GD_HEADS, GD_DK, GD_DV), f32),
                   jnp.zeros((DEPTH, B, GD_CONV - 1, GD_CONV_CH), f32),
                   jnp.zeros((DEPTH, B, HG_HEADS, HG_DK, HG_DV), f32))
    y_prompt, p_C, p_n, p_m, p_S, p_conv, p_H = _trunk(x_prompt, zero_states, lb, weights, final_norm_w)
    sample_states = (state_mlstm_C, state_mlstm_n, state_mlstm_m, state_gdn_S, state_gdn_conv, state_hgrn_S)
    y_sample, s_C, s_n, s_m, s_S, s_conv, s_H = _trunk(x_sample, sample_states, lb, weights, final_norm_w)
    return (y_prompt, y_sample, p_C, p_n, p_m, p_S, p_conv, p_H, s_C, s_n, s_m, s_S, s_conv, s_H)


_drawn_inputs = setup_inputs


def setup_inputs(seed=0):
    import zlib

    import numpy as np

    out = dict(_drawn_inputs(seed))
    spreads = {}
    factors = {'ml_norm_w': 13.414,
     'gd_norm_w': 12.957,
     'hg_norm_w': 7.52,
     'norm2_w': 2.942,
     'final_norm_w': 8.462}
    for name, (base, spread) in spreads.items():
        noise = np.random.default_rng([zlib.crc32(name.encode()), seed]).standard_normal(out[name].shape)
        drawn = base * np.exp(spread * noise) if base else spread * noise
        out[name] = __import__('jax').numpy.asarray(drawn.astype(out[name].dtype))
    for name, factor in factors.items():
        out[name] = (out[name] * factor).astype(out[name].dtype)
    return out
```

```python
from contextlib import ExitStack, contextmanager

import numpy as np

import concourse.bass as bass
from concourse import mybir

F32 = mybir.dt.float32
ALU = mybir.AluOpType
ACT = mybir.ActivationFunctionType
AX = mybir.AxisListType

P = 128
D, SEQ, DEPTH, NSEQ, DSEQ = 1024, 512, 2, 8, 4
SAMP = NSEQ * DSEQ
TOK = SEQ + SAMP
HALF = TOK // 2
NT = SEQ // P + 1
H = 4
DKM, DKG, DKH = 64, 128, 64
CONV = 4
GT = 3 * H * DKG // P
KT = D // P
FF = 2816
FT = FF // P
MIX = H * (DKM + DKG + DKH)
EPS = 1e-6
LEVELS = 7
TINY = 2.0 ** -63

ML_QK, ML_VO, GD_QKV, GD_G, HG_QF, HG_IG = 0, 512, 1032, 2568, 3088, 3600
GROUP = 520
V0, O0, I0, F0 = 0, 256, 512, 516
OG1, A1, B1 = 0, 512, 516
I2, OG2 = 0, 256
LI, LF, GG, BETA = 0, 4, 8, 12

SEM0 = 110
EXP_LN = "natural_log_exp_and_others"


def constants():
    s, t = np.meshgrid(np.arange(P), np.arange(P), indexing="ij")
    parts, at, n = [], {}, 0

    def put(name, a):
        nonlocal n
        at[name] = (n, a.shape[1])
        parts.append(a.astype(np.float32))
        n += a.shape[1]

    put("ident", s == t)
    put("ones", np.ones((P, P)))
    put("upto", s <= t)
    put("end", np.broadcast_to(t == P - 1, (P, P)))
    for l in range(LEVELS):
        block = (s >> (l + 1)) == (t >> (l + 1))
        put(f"low{l}", block & ((s >> l) & 1 == 1) & ((t >> l) & 1 == 0))
        put(f"up{l}", block & ((t >> l) & 1 == 1) & ((s >> l) & 1 == 0))
    same = (s // DSEQ) == (t // DSEQ)
    k = SAMP
    put("upto_s", (same & (s <= t))[:, :k])
    put("same_s", same[:, :k])
    put("end_s", (same & (t % DSEQ == DSEQ - 1))[:, :k])
    b, tt = np.meshgrid(np.arange(NSEQ), np.arange(k), indexing="ij")
    put("seq_of_column", np.broadcast_to((tt // DSEQ == b).reshape(1, -1), (P, NSEQ * k)))
    put("seq_of_row", (np.arange(P)[:, None] // DSEQ) == np.arange(NSEQ)[None])
    return np.concatenate(parts, axis=1), at


class Signals:

    def __init__(self, nc):
        self.nc, self.named = nc, {}

    def __getitem__(self, name):
        if name not in self.named:
            self.named[name] = self.nc.alloc_semaphore(name, num=SEM0 + len(self.named))
        return self.named[name]


@contextmanager
def phase(nc):
    sig = Signals(nc)
    with nc.Block(no_gpsimd_drain=True) as block:
        yield sig, block
    for s in sig.named.values():
        nc.release_semaphore(s)
    nc.all_engine_barrier(sems_to_clear=range(SEM0, SEM0 + len(sig.named)))


def bc(ap, *shape):
    return ap.broadcast_to(list(shape))


def tile_rows(i):
    return SAMP if i == NT - 1 else P


class Memory:

    def __init__(self, nc, stack, const_at, n_const):
        self.nc, self.stack = nc, stack
        self.words = nc.sbuf_bytes_remaining // 4 // 8 * 8 - 8
        self.all = stack.enter_context(nc.sbuf_tensor("sbuf", [P, self.words], F32))
        self.top = 0
        self.bank = [stack.enter_context(nc.psum_tensor(f"bank{i}", [P, 512], F32)) for i in range(8)]
        self.const = self.take(n_const)
        self.const_at = const_at
        self.x = self.take(NT, D)
        self.hT = self.take(KT, TOK)
        work = self.top
        self.mlF = self.take(4, TOK)
        self.gdF = self.take(GT, CONV - 1 + SEQ)
        self.gdS = self.take(GT, NSEQ, CONV - 1 + DSEQ)
        self.gdC = self.take(GT, SAMP)
        self.hgF = self.take(4, TOK)
        self.tokp_at = self.top
        self.tokp = self.take(NT, 3, GROUP)
        self.act = self.view(work, FT, TOK)
        self.h = self.view(self.top - NT * 3 * GROUP, NT, D)
        self.gates = self.take(NT, 16)
        self.colw = self.take(64)
        self.lb = self.take(DEPTH * 2)
        self.rows = self.take(16 + 64 + 64 + 128)
        self.rstd = self.take(8)
        self.lbl = self.take(2)
        self.mcol = self.take(4)
        self.ss = self.take(8)
        self.S_gd = self.take(H, 1, DKG)
        self.C_ml = self.take(2, 1, DKM + 1)
        self.S_hg = self.take(2, 1, DKH)
        self.m_ml = self.take(H, 1)
        self.arena = self.top
        self.slab = self.take(16, GROUP)

    def view(self, at, *shape):
        n = int(np.prod(shape))
        ap = self.all[:, at:at + n]
        if len(shape) == 1:
            return ap
        names = "abcd"[:len(shape)]
        sizes = dict(zip(names, shape))
        return ap.rearrange(f"p ({' '.join(names)}) -> p {' '.join(names)}", **sizes)

    def take(self, *shape):
        ap = self.view(self.top, *shape)
        self.top += int(np.prod(shape))
        assert self.top <= self.words, (self.top, self.words)
        return ap

    def c(self, name, rows=P):
        at, n = self.const_at[name]
        return self.const[0:rows, at:at + n]


def layer_rows(m):
    r = m.rows
    return {"ibias": r[:, 0:4], "fbias": r[:, 4:8], "negA": r[:, 8:12], "dtb": r[:, 12:16],
            "mlw": r[:, 16:80], "hgw": r[:, 80:144], "gdw": r[:, 144:272]}


def setup_phase(nc, m, d):
    m.top = m.arena + 16 * GROUP
    lbr = m.take(P)
    pr = m.take(DEPTH * 2)
    mx, sm = m.take(2), m.take(2)
    with phase(nc) as (sig, block):
        @block.sync
        def _(sp):
            sp.dma_start(m.const, d["consts"]).then_inc(sig["const_loaded"], 16)
            sp.dma_start(m.x[:, 0:NT - 1, :],
                         d["x_prompt"][0].rearrange("(i p) n -> p i n", p=P)).then_inc(sig["x_loaded"], 16)
            sp.dma_start(m.x[0:SAMP, NT - 1, :],
                         d["x_sample"].rearrange("b t n -> (b t) n")).then_inc(sig["x_loaded"], 16)
            sp.dma_start(lbr[0:2 * DEPTH, :],
                         d["hg_lower_bounds"].rearrange("l (j p) -> (l j) p", p=P)).then_inc(sig["bounds_loaded"], 16)
            sp.wait_ge(sig["x_loaded"], 32)

        @block.gpsimd
        def _(pool):
            pool.memset(m.tokp[:, NT - 1], 0.0)
            pool.memset(m.ss, 1.0)

        @block.tensor
        def _(pe):
            pe.wait_ge(sig["const_loaded"], 16)
            pe.wait_ge(sig["bounds_loaded"], 16)
            pe.transpose(m.bank[0][:, 0:2 * DEPTH], lbr[0:2 * DEPTH, :], m.c("ident", 2 * DEPTH)[:, 0:2 * DEPTH]
                         ).then_inc(sig["bounds_turned"], 1)

        @block.vector
        def _(dve):
            b = m.bank[0][:, 0:2 * DEPTH]
            dve.wait_ge(sig["bounds_turned"], 1)
            dve.tensor_copy(pr, b).then_inc(sig["bounds"], 1)
            dve.wait_ge(sig["bounds"], 1)
            dve.tensor_tensor(mx, pr[:, 0:2], pr[:, 2:4], ALU.max).then_inc(sig["bounds"], 1)
            dve.wait_ge(sig["bounds"], 2)
            for l in range(DEPTH):
                dve.tensor_tensor(m.lb[:, 2 * l:2 * l + 2], pr[:, 2 * l:2 * l + 2], mx, ALU.subtract
                                  ).then_inc(sig["bounds_shifted"], 1)
            dve.wait_ge(sig["bounds_exp"], 1)
            dve.tensor_tensor(sm, pr[:, 0:2], pr[:, 2:4], ALU.add).then_inc(sig["bounds"], 1)
            dve.wait_ge(sig["bounds"], 3)
            dve.reciprocal(mx, sm).then_inc(sig["bounds"], 1)
            dve.wait_ge(sig["bounds"], 4)
            dve.tensor_tensor(pr[:, 0:2], pr[:, 0:2], mx, ALU.mult).then_inc(sig["bounds"], 1)
            dve.tensor_tensor(pr[:, 2:4], pr[:, 2:4], mx, ALU.mult).then_inc(sig["bounds"], 1)
            dve.wait_ge(sig["bounds"], 6)
            dve.tensor_tensor(m.lb[:, 0:2], pr[:, 0:2], pr[:, 0:2], ALU.subtract)
            dve.tensor_tensor(sm, pr[:, 0:2], pr[:, 2:4], ALU.add).then_inc(sig["bounds"], 1)
            dve.wait_ge(sig["bounds"], 7)
            dve.tensor_tensor(m.lb[:, 2:4], sm, pr[:, 0:2], ALU.subtract)

        @block.scalar
        def _(act):
            nc.scalar.preload_act_table_set(EXP_LN)
            act.wait_ge(sig["bounds_shifted"], DEPTH)
            act.activation(pr, m.lb, ACT.Exp).then_inc(sig["bounds_exp"], 1)


def norm_phase(nc, m, d, l, which):
    m.top = m.arena + 16 * GROUP
    wrows = m.take(P)
    rows = layer_rows(m)
    wlast = m.take(D)
    y = m.take(NT, D) if which == 2 else None
    with phase(nc) as (sig, block):
        if which == 0:
            @block.sync
            def _(sp):
                one = bass.ds(l, 1)
                sp.dma_start(wrows[0:48, :], d["gd_conv_w"][one].rearrange("o j (t p) -> (o j t) p", p=P)
                             ).then_inc(sig["rows_loaded"], 16)
                for at, name in ((48, "norm1_w"), (56, "norm2_w")):
                    sp.dma_start(wrows[at:at + KT, :], d[name][one].rearrange("o (k p) -> (o k) p", p=P)
                                 ).then_inc(sig["rows_loaded"], 16)
                for key, name, n in (("ibias", "ml_i_bias", 4), ("fbias", "ml_f_bias", 4), ("negA", "gd_A_log", 4),
                                     ("dtb", "gd_dt_bias", 4), ("mlw", "ml_norm_w", 64), ("hgw", "hg_norm_w", 64),
                                     ("gdw", "gd_norm_w", 128)):
                    sp.dma_start(rows[key], bc(d[name][one, :], P, n)).then_inc(sig["small_loaded"], 16)
                sp.wait_ge(sig["small_loaded"], 7 * 16)
        if which == 2:
            @block.sync
            def _(sp):
                sp.dma_start(wlast, bc(d["final_norm_w"].rearrange("(o n) -> o n", o=1), P, D)
                             ).then_inc(sig["last_w_loaded"], 16)
                for i in range(NT):
                    sp.wait_ge(sig["y_ready"], i + 1)
                    dst = d["y_prompt"][0, i * P:(i + 1) * P, :] if i < NT - 1 else \
                        d["y_sample"].rearrange("b t n -> (b t) n")
                    sp.dma_start(dst, y[0:tile_rows(i), i, :]).then_inc(sig["y_stored"], 16)
                sp.wait_ge(sig["y_stored"], 16 * NT)

        if which == 0:
            @block.gpsimd
            def _(pool):
                pool.tensor_copy(m.lbl, m.lb[:, bass.ds(l * 2, 2)])

        @block.scalar
        def _(act):
            for i in range(NT):
                n = tile_rows(i)
                act.activation(m.h[0:n, i, :], m.x[0:n, i, :], ACT.Square,
                               accum_out=m.ss[0:n, i:i + 1]).then_inc(sig["squares"], 1)
            act.wait_ge(sig["squares"], NT)
            act.activation(m.rstd[:, 0:NT], m.ss[:, 0:NT], ACT.Ln, scale=1.0 / D, bias=EPS).then_inc(sig["rstd"], 1)
            act.wait_ge(sig["rstd"], 1)
            act.activation(m.rstd[:, 0:NT], m.rstd[:, 0:NT], ACT.Exp, scale=-0.5).then_inc(sig["rstd"], 1)
            if which == 0:
                act.wait_ge(sig["small_loaded"], 7 * 16)
                act.activation(rows["negA"], rows["negA"], ACT.Exp).then_inc(sig["decay_rates"], 1)

        if which == 2:
            @block.vector
            def _(dve):
                dve.wait_ge(sig["rstd"], 2)
                dve.wait_ge(sig["last_w_loaded"], 16)
                for i in range(NT):
                    n = tile_rows(i)
                    dve.scalar_tensor_tensor(out=y[0:n, i, :], in0=m.x[0:n, i, :], scalar=m.rstd[0:n, i:i + 1],
                                             in1=wlast[0:n, :], op0=ALU.mult, op1=ALU.mult).then_inc(sig["y_ready"], 1)
            return

        @block.vector
        def _(dve):
            dve.wait_ge(sig["rstd"], 2)
            for i in range(NT):
                n = tile_rows(i)
                dve.tensor_scalar(m.h[0:n, i, :], m.x[0:n, i, :], m.rstd[0:n, i:i + 1], None, ALU.mult
                                  ).then_inc(sig["h_ready"], 1)
            if which == 0:
                dve.wait_ge(sig["rows_turned"], 1)
                dve.tensor_copy(m.colw, m.bank[7][:, 0:64]).then_inc(sig["colw_ready"], 1)
                dve.wait_ge(sig["decay_rates"], 1)
                dve.tensor_scalar(rows["negA"], rows["negA"], -1.0, None, ALU.mult)
                dve.wait_ge(sig["colw_ready"], 1)
            w = m.colw[:, 48 + 8 * which:56 + 8 * which]
            for i in range(NT):
                n = tile_rows(i)
                for g in range(2):
                    u = 2 * i + g
                    dve.wait_ge(sig["h_turned"], u + 1)
                    src = m.bank[u % 6][:, 0:4 * n].rearrange("p (k t) -> p k t", k=4)
                    wk = bc(w[:, 4 * g:4 * g + 4].unsqueeze(2), P, 4, n)
                    dve.tensor_tensor(m.hT[:, 4 * g:4 * g + 4, i * P:i * P + n], src, wk, ALU.mult
                                      ).then_inc(sig["bank_read"], 1)

        @block.tensor
        def _(pe):
            if which == 0:
                pe.wait_ge(sig["rows_loaded"], 48)
                pe.transpose(m.bank[7][:, 0:64], wrows[0:64, :], m.c("ident", 64)[:, 0:64]
                             ).then_inc(sig["rows_turned"], 1)
            for i in range(NT):
                n = tile_rows(i)
                pe.wait_ge(sig["h_ready"], i + 1)
                for g in range(2):
                    u = 2 * i + g
                    if u >= 6:
                        pe.wait_ge(sig["bank_read"], u - 5)
                    for k in range(4):
                        kt = 4 * g + k
                        mm = pe.transpose(m.bank[u % 6][:, k * n:(k + 1) * n], m.h[0:n, i, kt * P:(kt + 1) * P],
                                          m.c("ident", n)[:, 0:n])
                    mm.then_inc(sig["h_turned"], 1)


def project_phase(nc, m, d, l):
    one = bass.ds(l, 1)

    def slab(slot, k, c0, n):
        src = d["w_in"][one, k * P:(k + 1) * P, c0] if not isinstance(c0, int) else \
            d["w_in"][one, k * P:(k + 1) * P, c0:c0 + n]
        return m.slab[:, slot, 0:n], src.rearrange("o p n -> (o p) n")

    NF = 5
    GROUPS = ((1, GD_G, 520, 8), (0, ML_VO, 520, 0), (2, HG_IG, 512, 8))
    with phase(nc) as (sig, block):
        @block.sync
        def _(sp):
            def free(k, n):
                if k < KT - 1:
                    sp.wait_ge(sig[f"slab{k}_used"], n + 1)
                else:
                    sp.wait_ge(sig["high_bank_done"], 4 * n + 4)

            with sp.Fori(0, 3) as j:
                for k in range(KT):
                    free(k, j)
                    dst, src = slab(k, k, bass.ds(j * 512 + GD_QKV, 512), 512)
                    sp.dma_start(dst, src).then_inc(sig[f"slab{k}_loaded"], 16)
            for k in range(KT):
                dst, src = slab(8 + k, k, GROUPS[0][1], GROUPS[0][2])
                sp.dma_start(dst, src).then_inc(sig[f"slab{8 + k}_loaded"], 16)
            for n, c0, width in ((3, ML_QK, 512), (4, HG_QF, 512), (5, ML_VO, 520)):
                for k in range(KT):
                    free(k, n)
                    dst, src = slab(k, k, c0, width)
                    sp.dma_start(dst, src).then_inc(sig[f"slab{k}_loaded"], 16)
            for k in range(KT):
                sp.wait_ge(sig["high_bank_done"], 4 * NF + NT + 4)
                dst, src = slab(8 + k, k, GROUPS[2][1], GROUPS[2][2])
                sp.dma_start(dst, src).then_inc(sig[f"slab{8 + k}_loaded"], 16)

        @block.tensor
        def _(pe):
            def features(n):
                for k in range(KT):
                    pe.wait_ge(sig[f"slab{k}_loaded"], 16 * n + 16)
                    for t in range(4):
                        if k == 0:
                            pe.wait_ge(sig["low_bank_read"], 4 * n + t + 1)
                            pe.wait_ge(sig["high_bank_read"], 4 * n + t + 1)
                        for half, done in enumerate(("low_bank_done", "high_bank_done")):
                            mm = pe.matmul(m.bank[2 * t + half][:, 0:HALF], m.slab[:, k, t * P:(t + 1) * P],
                                           m.hT[:, k, half * HALF:(half + 1) * HALF],
                                           start=(k == 0), stop=(k == KT - 1))
                            if k == KT - 1:
                                mm.then_inc(sig[done], 1)
                            elif t == 3 and half == 1:
                                mm.then_inc(sig[f"slab{k}_used"], 1)

            for k in range(KT - 1):
                pe.sem_inc(sig[f"slab{k}_used"], 1)
            pe.sem_inc(sig["low_bank_done"], 4)
            pe.sem_inc(sig["high_bank_done"], 4)
            with pe.Fori(0, 3) as j:
                features(j)
            features(3)
            features(4)
            u = 4 * NF
            for g, c0, width, slot in GROUPS:
                w2 = width // 2
                for i in range(NT):
                    n = tile_rows(i)
                    pe.wait_ge(sig["low_bank_read"], u + 1)
                    pe.wait_ge(sig["high_bank_read"], u + 1)
                    for k in range(KT):
                        if i == 0:
                            pe.wait_ge(sig[f"slab{slot + k}_loaded"], 16 * ((NF + 1) if slot == 0 else 1 + (g == 2)))
                        for half, done in enumerate(("low_bank_done", "high_bank_done")):
                            mm = pe.matmul(m.bank[2 * (u % 4) + half][0:n, 0:w2], m.hT[:, k, i * P:i * P + n],
                                           m.slab[:, slot + k, half * w2:(half + 1) * w2],
                                           start=(k == 0), stop=(k == KT - 1))
                            if k == KT - 1:
                                mm.then_inc(sig[done], 1)
                    u += 1

        def evacuate(eng, copy, half):
            done, read = (("low_bank_done", "low_bank_read"), ("high_bank_done", "high_bank_read"))[half]
            eng.sem_inc(sig[read], 4)

            def features(n, prompt, sample):
                for t in range(4):
                    eng.wait_ge(sig[done], 4 * n + t + 5)
                    b = m.bank[2 * t + half]
                    if half == 0:
                        copy(prompt(t)[:, 0:HALF], b[:, 0:HALF]).then_inc(sig[read], 1)
                    else:
                        copy(prompt(t)[:, HALF:SEQ], b[:, 0:SEQ - HALF])
                        copy(sample(t), b[:, SEQ - HALF:HALF]).then_inc(sig[read], 1)

            with eng.Fori(0, 3) as j:
                features(j, lambda t: m.gdF[:, bass.ds(4 * j + t, 1), CONV - 1:].rearrange("p a n -> p (a n)"),
                         lambda t: m.gdS[:, bass.ds(4 * j + t, 1), :, CONV - 1:].rearrange("p a b n -> p (a b) n"))
            features(3, lambda t: m.mlF[:, t, 0:SEQ], lambda t: m.mlF[:, t, SEQ:])
            features(4, lambda t: m.hgF[:, t, 0:SEQ], lambda t: m.hgF[:, t, SEQ:])
            u = 4 * NF
            for g, c0, width, slot in GROUPS:
                w2 = width // 2
                for i in range(NT):
                    n = tile_rows(i)
                    eng.wait_ge(sig[done], u + 5)
                    copy(m.tokp[0:n, i, g, half * w2:(half + 1) * w2],
                         m.bank[2 * (u % 4) + half][0:n, 0:w2]).then_inc(sig[read], 1)
                    u += 1

        @block.scalar
        def _(act):
            evacuate(act, act.copy, 0)

        @block.vector
        def _(dve):
            def copy(o, i):
                if len(o.shape) == 3:
                    i = i.rearrange("p (b n) -> p b n", b=NSEQ)
                return dve.tensor_copy(o, i)
            evacuate(dve, copy, 1)

        @block.gpsimd
        def _(pool):
            pool.memset(m.gdF[:, :, 0:CONV - 1], 0.0)


def prep_phase(nc, m, d, l):
    one = bass.ds(l, 1)
    m.top = m.arena + 16 * GROUP
    bufs = m.take(GT * P)
    last = m.take(GT, 27)
    lastT = m.take(GT * P)
    m.top = m.arena
    acc = [m.take(SEQ) for _ in range(2)]
    sacc = m.take(GT, NSEQ, DSEQ)
    stmp = m.take(GT, NSEQ, DSEQ)
    fy, ab = m.take(NT, 8), m.take(NT, 8)
    pos = m.take(NT, 4)
    rows = layer_rows(m)
    taps = m.colw[:, 0:48].rearrange("p (j t) -> p j t", j=CONV)
    OLD = NSEQ * (CONV - 1)
    with phase(nc) as (sig, block):
        @block.sync
        def _(sp):
            sp.dma_start(bufs[0:OLD, :], d["state_gdn_conv"][one].rearrange("o b j n -> (o b j) n")
                         ).then_inc(sig["rows_loaded"], 16)
            sp.wait_ge(sig["last_ready"], 3)
            sp.dma_start(d["p_conv"][one].rearrange("o b j n -> (o b j) n"), lastT[0:3, :]
                         ).then_inc(sig["last_stored"], 16)
            sp.dma_start(d["s_conv"][one].rearrange("o b j n -> (o b j) n"), lastT[3:27, :]
                         ).then_inc(sig["last_stored"], 16)
            sp.wait_ge(sig["last_stored"], 32)

        @block.tensor
        def _(pe):
            pe.wait_ge(sig["rows_loaded"], 16)
            for t in range(GT):
                mm = pe.transpose(m.bank[0][:, t * OLD:(t + 1) * OLD], bufs[0:OLD, t * P:(t + 1) * P],
                                  m.c("ident", OLD)[:, 0:OLD])
            mm.then_inc(sig["rows_turned"], 1)
            pe.wait_ge(sig["last_taken"], 2)
            for t in range(GT):
                mm = pe.transpose(m.bank[1 + t // 4][0:27, (t % 4) * P:(t % 4 + 1) * P], last[:, t, :], m.c("ident"))
                if t % 4 == 3:
                    mm.then_inc(sig["last_turned"], 1)

        @block.gpsimd
        def _(pool):
            pool.tensor_copy(last[:, :, 0:3], m.gdF[:, :, SEQ:SEQ + 3]).then_inc(sig["last_taken"], 1)
            for t in range(GT):
                cp = pool.tensor_copy(last[:, t, 3:27].rearrange("p (b j) -> p b j", b=NSEQ), m.gdS[:, t, :, DSEQ:])
            cp.then_inc(sig["last_taken"], 1)
            pool.wait_ge(sig["rows_placed"], 1)
            for j in range(CONV):
                wj = bc(taps[:, j, :].unsqueeze(2).unsqueeze(3), P, GT, NSEQ, DSEQ)
                dst = sacc if j == 0 else stmp
                if j > 1:
                    pool.wait_ge(sig["tap_added"], j - 1)
                pool.tensor_tensor(dst, m.gdS[:, :, :, j:j + DSEQ], wj, ALU.mult).then_inc(sig["tap_scaled"], 1)
                if j > 0:
                    pool.wait_ge(sig["tap_scaled"], j + 1)
                    if j > 1:
                        pool.wait_ge(sig["tap_added"], j - 1)
                    pool.tensor_tensor(sacc, sacc, stmp, ALU.add).then_inc(sig["tap_added"], 1)
            pool.wait_ge(sig["gates_silu"], 2)
            for i in range(NT):
                g = m.tokp[:, i, 1, 0:H * DKG].rearrange("p (h n) -> p h n", h=H)
                pool.tensor_tensor(g, g, bc(rows["gdw"].unsqueeze(1), P, H, DKG), ALU.mult)
                g = m.tokp[:, i, 2, OG2:OG2 + H * DKH].rearrange("p (h n) -> p h n", h=H)
                pool.tensor_tensor(g, g, bc(rows["hgw"].unsqueeze(1), P, H, DKH), ALU.mult)

        @block.vector
        def _(dve):
            dve.wait_ge(sig["rows_turned"], 1)
            dve.tensor_copy(m.gdS[:, :, :, 0:CONV - 1],
                            m.bank[0][:, 0:GT * OLD].rearrange("p (t b j) -> p t b j", t=GT, b=NSEQ)
                            ).then_inc(sig["rows_placed"], 1)
            dve.wait_ge(sig["last_turned"], 3)
            for g in range(3):
                dve.tensor_copy(lastT[0:27, g * 512:(g + 1) * 512], m.bank[1 + g][0:27, :]
                                ).then_inc(sig["last_ready"], 1)
            t0 = m.tokp
            dve.tensor_tensor(m.gates[:, :, LI:LI + 4], t0[:, :, 0, I0:I0 + 4],
                              bc(rows["ibias"].unsqueeze(1), P, NT, 4), ALU.add)
            dve.tensor_tensor(fy[:, :, 0:4], t0[:, :, 0, F0:F0 + 4], bc(rows["fbias"].unsqueeze(1), P, NT, 4),
                              ALU.add).then_inc(sig["fy_ready"], 1)
            dve.tensor_tensor(fy[:, :, 4:8], t0[:, :, 1, A1:A1 + 4], bc(rows["dtb"].unsqueeze(1), P, NT, 4),
                              ALU.add).then_inc(sig["fy_ready"], 1)
            dve.wait_ge(sig["fy_ready"], 2)
            dve.scalar_tensor_tensor(out=ab, in0=fy, scalar=-1.0, in1=fy, op0=ALU.mult, op1=ALU.max
                                     ).then_inc(sig["fy_abs"], 1)
            dve.tensor_scalar(m.gates[:, :, LF:LF + 4], fy[:, :, 0:4], 0.0, None, ALU.min).then_inc(sig["fy_clipped"], 1)
            dve.tensor_scalar(pos, fy[:, :, 4:8], 0.0, None, ALU.max).then_inc(sig["fy_clipped"], 1)
            with dve.Fori(0, GT // 2) as n:
                for tap in range(CONV):
                    for b in range(2):
                        t = bass.ds(2 * n + b, 1)
                        src = m.gdF[:, t, tap:tap + SEQ].rearrange("p a n -> p (a n)")
                        w = taps[:, tap, bass.ds(2 * n + b, 1)]
                        if tap == 0:
                            dve.wait_ge(sig[f"conv{b}_stored"], n + 1)
                            dve.tensor_scalar(acc[b], src, w, None, ALU.mult).then_inc(sig[f"conv{b}"], 1)
                        else:
                            dve.wait_ge(sig[f"conv{b}"], 4 * n + tap)
                            dve.scalar_tensor_tensor(out=acc[b], in0=src, scalar=w, in1=acc[b],
                                                     op0=ALU.mult, op1=ALU.add).then_inc(sig[f"conv{b}"], 1)
            dve.wait_ge(sig["fy_ln"], 2)
            dve.wait_ge(sig["fy_clipped"], 2)
            dve.tensor_tensor(m.gates[:, :, LF:LF + 4], m.gates[:, :, LF:LF + 4], ab[:, :, 0:4], ALU.subtract)
            dve.tensor_tensor(pos, pos, ab[:, :, 4:8], ALU.add).then_inc(sig["softplus"], 1)
            dve.wait_ge(sig["softplus"], 1)
            dve.tensor_tensor(m.gates[:, :, GG:GG + 4], pos, bc(rows["negA"].unsqueeze(1), P, NT, 4), ALU.mult)

        @block.scalar
        def _(act):
            g1 = m.tokp[:, :, 1, 0:H * DKG]
            g2 = m.tokp[:, :, 2, OG2:OG2 + H * DKH]
            act.activation(g1, g1, ACT.Silu).then_inc(sig["gates_silu"], 1)
            act.activation(g2, g2, ACT.Silu).then_inc(sig["gates_silu"], 1)
            for b in range(2):
                act.sem_inc(sig[f"conv{b}_stored"], 1)
            q = m.hgF[:, 0:2, :]
            act.activation(q, q, ACT.Silu)
            with act.Fori(0, GT // 2) as n:
                for b in range(2):
                    act.wait_ge(sig[f"conv{b}"], 4 * n + 4)
                    act.activation(m.gdF[:, bass.ds(2 * n + b, 1), CONV - 1:].rearrange("p a n -> p (a n)"), acc[b],
                                   ACT.Silu).then_inc(sig[f"conv{b}_stored"], 1)
            act.wait_ge(sig["tap_added"], CONV - 1)
            act.activation(m.gdC.rearrange("p t n -> p (t n)"), sacc.rearrange("p t b n -> p (t b n)"), ACT.Silu)
            z = m.hgF[:, 2:4, :]
            act.activation(z, z, ACT.Sigmoid)
            o = m.tokp[:, :, 0, O0:O0 + H * DKM]
            act.activation(o, o, ACT.Sigmoid)
            act.activation(m.gates[:, :, BETA:BETA + 4], m.tokp[:, :, 1, B1:B1 + 4], ACT.Sigmoid)
            nc.scalar.preload_act_table_set(EXP_LN)
            act.wait_ge(sig["fy_abs"], 1)
            act.activation(ab, ab, ACT.Exp, scale=-1.0).then_inc(sig["fy_ln"], 1)
            act.wait_ge(sig["fy_ln"], 1)
            act.activation(ab, ab, ACT.Ln, bias=1.0).then_inc(sig["fy_ln"], 1)


def start_states(nc, m):
    with phase(nc) as (sig, block):
        @block.gpsimd
        def _(pool):
            for s in (m.S_gd, m.C_ml, m.S_hg, m.m_ml):
                pool.memset(s, 0.0)
            pool.memset(m.view(m.arena, 6 * H * P), 0.0)


def load_sample_states(nc, m, d, l):
    one = bass.ds(l, 1)
    m.top = m.arena
    st = {"S_gd": m.take(H, NSEQ, DKG), "C_ml": m.take(2, NSEQ, DKM + 1), "S_hg": m.take(2, NSEQ, DKH),
          "m_ml": m.take(H, NSEQ)}
    with phase(nc) as (sig, block):
        @block.gpsimd
        def _(pool):
            pool.memset(m.view(m.top, 6 * H * SAMP), 0.0)

        @block.sync
        def _(sp):
            for h in range(H):
                half, pair = slice(64 * (h % 2), 64 * (h % 2) + 64), h // 2
                sp.dma_start(st["S_gd"][:, h], d["state_gdn_S"][one, :, h].rearrange("o b k v -> k (o b) v")
                             ).then_inc(sig["state_loaded"], 16)
                sp.dma_start(st["C_ml"][half, pair, :, 0:DKM],
                             d["state_mlstm_C"][one, :, h].rearrange("o b k v -> k (o b) v")
                             ).then_inc(sig["state_loaded"], 16)
                sp.dma_start(st["C_ml"][half, pair, :, DKM:],
                             d["state_mlstm_n"][one, :, h].rearrange("o b (k x) -> k (o b) x", x=1)
                             ).then_inc(sig["state_loaded"], 16)
                sp.dma_start(st["S_hg"][half, pair], d["state_hgrn_S"][one, :, h].rearrange("o b k v -> k (o b) v")
                             ).then_inc(sig["state_loaded"], 16)
                sp.dma_start(st["m_ml"][:, h, :], bc(d["state_mlstm_m"][one, :, h], P, NSEQ)
                             ).then_inc(sig["state_loaded"], 16)
            sp.wait_ge(sig["state_loaded"], 16 * 5 * H)
    return st


def store_states(nc, m, d, l, st, who, nseq, mcol, rows):
    one = bass.ds(l, 1)
    with phase(nc) as (sig, block):
        @block.sync
        def _(sp):
            for h in range(H):
                half, pair = slice(64 * (h % 2), 64 * (h % 2) + 64), h // 2
                sp.dma_start(d[who + "_S"][one, :, h].rearrange("o b k v -> k (o b) v"), st["S_gd"][:, h]
                             ).then_inc(sig["state_stored"], 16)
                sp.dma_start(d[who + "_C"][one, :, h].rearrange("o b k v -> k (o b) v"),
                             st["C_ml"][half, pair, :, 0:DKM]).then_inc(sig["state_stored"], 16)
                sp.dma_start(d[who + "_n"][one, :, h].rearrange("o b (k x) -> k (o b) x", x=1),
                             st["C_ml"][half, pair, :, DKM:]).then_inc(sig["state_stored"], 16)
                sp.dma_start(d[who + "_H"][one, :, h].rearrange("o b k v -> k (o b) v"), st["S_hg"][half, pair]
                             ).then_inc(sig["state_stored"], 16)
            sp.dma_start(d[who + "_m"][one].rearrange("o b h -> (o b) h"), mcol[rows, :]
                         ).then_inc(sig["state_stored"], 16)
            sp.wait_ge(sig["state_stored"], 16 * (4 * H + 1))


HALVES = tuple((odd, slice(64 * odd, 64 * odd + 64)) for odd in range(2))


def sample_state_words():
    return (H * DKG + 2 * (DKM + 1) + 2 * DKH + H) * NSEQ


def chunk_phase(nc, m, st, nseq, c):
    sample = c is None
    L = DSEQ if sample else P
    T = nseq * L
    nl = 2 if sample else LEVELS
    W = H * T
    tile = NT - 1 if sample else None
    upto = m.c("upto_s" if sample else "upto", T)[:, 0:T]
    same = m.c("same_s" if sample else "ones", T)[:, 0:T]
    endsel = m.c("end_s" if sample else "end", T)[:, 0:T]
    ident = m.c("ident", T)[:, 0:T]
    ones = m.c("ones")
    rows = layer_rows(m)

    def low(lv):
        return m.c(f"low{lv}", T)[:, 0:T]

    def up(lv):
        return m.c(f"up{lv}", T)[:, 0:T]

    def heads(ap, n=None):
        return ap.rearrange("p (h n) -> p h n", h=H)

    def over_heads(mask):
        return bc(mask.unsqueeze(1), mask.shape[0], H, mask.shape[1])

    def per_head(col, n):
        return bc(col.unsqueeze(2), col.shape[0], H, n)

    m.top = m.arena if not sample else m.arena + sample_state_words()
    padded = m.take(6, H, T)
    mq, mqw, hq, hqe = (padded[:, i] for i in range(4))
    lq = [padded[:, 4], padded[:, 5]]
    t4 = lambda: m.take(H, T)
    tv = lambda: m.take(H, DKG)
    kn, qn, EA, EB, X, Y, kd, qd, edb = (t4() for _ in range(9))
    A = EA
    at = m.top
    AM = [t4(), t4()]
    first = m.top
    m.take(5, H * DKG)
    spot = lambda i, n: m.view(first + i * H * DKG, H, n)
    sqk, r = spot(0, T), spot(0, DKG)
    sqq, u = spot(1, T), spot(1, DKG)
    vS, p1 = spot(2, T), spot(2, T)
    ug, og = spot(3, T), m.view(first + 3 * H * DKG, H * DKG)
    Dg, kdec = spot(4, T), spot(4, DKG)
    vb = tv()
    gates = m.take(16)
    dcol, ddc, kfac, msg = m.take(12), m.take(4), m.take(4), m.take(4)
    hk, bH, hlf, hkd, mk = (m.take(2, T) for _ in range(5))
    hkdT, mks = (m.take(2 * P), m.take(2 * P)) if sample else \
        (a.rearrange("p x t -> p (x t)") for a in (hkd, mk))
    lev = m.take(nl, 2, T)
    lk = [m.take(2, T) for _ in range(2)]
    hacc, htmp = t4(), [t4(), t4()]
    hms, hog = m.take(4), m.take(H * DKH)
    vext = m.take(H, DKM + 1)
    ua, ma, M, mW = t4(), t4(), t4(), t4()
    wexp = t4()
    bcol, acol, gcol, gend, emt, den, mms, kw = (m.take(12 if i == 0 else 4) for i in range(8))
    mog = m.take(H * DKM)
    m_sq = m.take(H * DKM) if sample else hlf.rearrange("p x t -> p (x t)")
    lbm, lbn = m.take(2), m.take(2)
    mix = m.take(MIX) if sample else m.view(at, MIX)
    if sample:
        kx, qx = m.take(H, nseq, T), m.take(H, nseq, T)
        hqx, mqx = m.take(H, nseq, T), m.take(H, nseq, T)
        ux = [m.view(m.tokp_at + i * nseq * DKG, nseq, DKG) for i in range(2)]
        hx = m.view(m.tokp_at + 2 * nseq * DKG, H, nseq, DKH)
        vx = m.view(m.tokp_at + 2 * nseq * DKG + H * nseq * DKH, H, nseq, DKM + 1)
        seqcol = m.c("seq_of_column").rearrange("p (b t) -> p b t", b=nseq)
        seqrow = m.c("seq_of_row", T)
    else:
        kx, qx, hqx, mqx = kd, qd, hqe, mqw
    M0, M1, H0, H1, G0, G1, G2, G3 = m.bank

    if sample:
        gt = lambda a, z: m.gdC[:, a:z, :]
        mlF, hgF = (lambda a, z: m.mlF[:, a:z, SEQ:]), (lambda a, z: m.hgF[:, a:z, SEQ:])
        tk = lambda g, a, z: m.tokp[0:T, tile, g, a:z]
        gates_src = m.gates[0:T, tile, :]
        hTc = m.hT[:, :, SEQ:]
    else:
        gt = lambda a, z: m.gdF[:, a:z, bass.ds(c * P + (CONV - 1), P)]
        mlF = lambda a, z: m.mlF[:, a:z, bass.ds(c * P, P)]
        hgF = lambda a, z: m.hgF[:, a:z, bass.ds(c * P, P)]
        tk = lambda g, a, z: m.tokp[:, bass.ds(c, 1), g, a:z].rearrange("p o n -> p (o n)")
        gates_src = m.gates[:, bass.ds(c, 1), :].rearrange("p o n -> p (o n)")
        hTc = m.hT[:, :, bass.ds(c * P, P)]
    li, lf, gg, beta = (gates[0:T, a:a + 4] for a in (LI, LF, GG, BETA))
    pair_of = lambda h: (slice(64 * (h % 2), 64 * (h % 2) + 64), h // 2)

    def seqs(ap):
        return ap.rearrange("p x (b j) -> p x b j", b=nseq)

    with phase(nc) as (sig, block):
        @block.scalar
        def _(act):
            def rstd(ms, n, ready, name):
                act.wait_ge(sig[ready], 1)
                act.activation(ms, ms, ACT.Ln, scale=1.0 / n, bias=EPS).then_inc(sig[name], 1)
                act.wait_ge(sig[name], 1)
                act.activation(ms, ms, ACT.Exp, scale=-0.5).then_inc(sig[name], 1)

            nc.scalar.preload_act_table_set(EXP_LN)
            act.copy(gates[0:T, :], gates_src).then_inc(sig["gates_taken"], 1)
            act.activation(sqk, gt(4, 8), ACT.Square).then_inc(sig["squares"], 1)
            act.activation(sqq, gt(0, 4), ACT.Square).then_inc(sig["squares"], 1)
            act.wait_ge(sig["f_ready"], 1)
            act.activation(hlf, hlf, ACT.Ln).then_inc(sig["logf"], 1)
            act.mul(mk, mlF(2, 4), DKM ** -0.5).then_inc(sig["ml_k"], 1)
            for odd, half in HALVES:
                act.copy(hq[half, odd::2, :], hgF(0, 2)[half]).then_inc(sig["hg_q"], 1)
                act.copy(mq[half, odd::2, :], mlF(0, 2)[half]).then_inc(sig["ml_q"], 1)
            act.copy(vS, gt(8, 12)).then_inc(sig["v_taken"], 1)
            for i, (b, sq) in enumerate(((G0, sqk), (G1, sqq))):
                flat = sq.rearrange("p h t -> p (h t)")
                act.wait_ge(sig["norm_sums"], i + 1)
                act.activation(flat, b[:, 0:W], ACT.Ln, bias=EPS).then_inc(sig["norm_ln"], 1)
                act.wait_ge(sig["norm_ln"], i + 1)
                act.activation(flat, flat, ACT.Exp, scale=-0.5).then_inc(sig["norm_ready"], 1)
            act.wait_ge(sig["ml_arows"], 1)
            act.copy(ma.rearrange("p h t -> p (h t)"), M0[:, 0:W]).then_inc(sig["ml_a_taken"], 1)
            act.wait_ge(sig["gd_Dmax"], 1)
            act.activation(EA[0:T], EA[0:T], ACT.Exp, scale=-1.0).then_inc(sig["gd_EA"], 1)
            act.wait_ge(sig["gd_Dmin"], 1)
            act.activation(EB[0:T], EB[0:T], ACT.Exp).then_inc(sig["gd_EB"], 1)
            act.activation(edb.rearrange("p h t -> p (h t)"), G2[:, 0:W], ACT.Exp).then_inc(sig["gd_edb"], 1)
            act.wait_ge(sig["gd_dd"], 1)
            act.activation(kfac[0:T], ddc[0:T], ACT.Exp).then_inc(sig["gd_kfac"], 1)
            act.wait_ge(sig["lev_abs"], 1)
            act.activation(lev, lev, ACT.Exp, scale=-1.0).then_inc(sig["lev_ready"], 1)
            act.wait_ge(sig["hg_dl"], 1)
            act.activation(bH, bH, ACT.Exp).then_inc(sig["hg_eb"], 1)
            act.activation(hkd, hkd, ACT.Exp, scale=-1.0).then_inc(sig["hg_ekd"], 1)
            act.wait_ge(sig["ml_D"], 2)
            act.activation(mW[0:T], mW[0:T], ACT.Exp, scale=-1.0).then_inc(sig["ml_E"], 1)
            act.wait_ge(sig["ml_wD"], 1)
            act.activation(wexp, wexp, ACT.Exp, scale=-1.0).then_inc(sig["ml_wexp"], 1)
            act.wait_ge(sig["ml_kwD"], 1)
            act.activation(kw[0:T], kw[0:T], ACT.Exp).then_inc(sig["ml_kw"], 1)
            act.wait_ge(sig["ml_mt"], 1)
            act.activation(emt[0:T], m.mcol[0:T, :], ACT.Exp, scale=-1.0).then_inc(sig["ml_emt"], 1)
            act.wait_ge(sig["gd_X0"], 1)
            act.copy(X[0:T].rearrange("p h t -> p (h t)"), G2[0:T, 0:W]).then_inc(sig["X_ready"], 1)
            for lv in range(1, nl):
                act.wait_ge(sig["inv_p1"], lv)
                if lv > 1:
                    act.wait_ge(sig["inv_p2"], lv - 1)
                act.copy(p1[0:T].rearrange("p h t -> p (h t)"), G0[0:T, 0:W]).then_inc(sig["inv_p1_taken"], 1)
            act.wait_ge(sig["hg_k_turned"], 1)
            act.copy(hkdT[0:T, :], H1[0:T, 0:2 * P]).then_inc(sig["hg_kT"], 1)
            act.wait_ge(sig["ml_gated"], 1)
            act.activation(m_sq[0:T, :], mog[0:T, :], ACT.Square).then_inc(sig["ml_sq"], 1)
            rstd(mms[0:T], DKM, "ml_ms", "ml_rstd")
            act.wait_ge(sig["hg_o"], 1)
            act.activation(hog[0:T, :], H0[0:T, 0:H * DKH], ACT.Square).then_inc(sig["hg_sq"], 1)
            rstd(hms[0:T], DKH, "hg_ms", "hg_rstd")
            act.wait_ge(sig["gd_u"], 1)
            act.copy(u[0:T].rearrange("p h n -> p (h n)"), G1[0:T, :]).then_inc(sig["u_ready"], 1)
            act.wait_ge(sig["gd_o"], 1)
            act.activation(og[0:T, :], G2[0:T, :], ACT.Square).then_inc(sig["gd_sq"], 1)
            rstd(msg[0:T], DKG, "gd_ms", "gd_rstd")
            act.wait_ge(sig["mix_turned"], 2)
            act.copy(hTc[:, 4:8, :], M1[:, 0:W].rearrange("p (k t) -> p k t", k=4))

        @block.gpsimd
        def _(pool):
            def mul(out, a, b):
                return pool.tensor_tensor(out, a, b, ALU.mult)

            pool.wait_ge(sig["gates_taken"], 1)
            mul(ug[0:T], over_heads(upto), per_head(gg, T)).then_inc(sig["gd_ug"], 1)
            mul(ua[0:T], over_heads(ident), per_head(li, T)).then_inc(sig["ml_ua"], 1)
            mul(mW[0:T], over_heads(upto), per_head(lf, T)).then_inc(sig["ml_ua"], 1)
            pool.wait_ge(sig["ml_ua"], 2)
            pool.tensor_tensor(ua[0:T], ua[0:T], mW[0:T], ALU.subtract).then_inc(sig["ml_ua_ready"], 1)
            pool.tensor_copy(vext[0:T, :, 0:DKM], heads(tk(0, V0, V0 + H * DKM))).then_inc(sig["ml_v"], 1)
            pool.memset(vext[0:T, :, DKM:], 1.0).then_inc(sig["ml_v"], 1)
            pool.wait_ge(sig["gd_EA"], 1)
            mul(EA[0:T], EA[0:T], per_head(beta, T)).then_inc(sig["gd_EAb"], 1)
            pool.wait_ge(sig["gd_EB"], 1)
            mul(EB[0:T], EB[0:T], over_heads(upto)).then_inc(sig["gd_EBm"], 1)
            pool.wait_ge(sig["gd_edb"], 1)
            pool.wait_ge(sig["gd_kn"], 1)
            mul(kd, kn, edb).then_inc(sig["gd_kd"], 1)
            pool.wait_ge(sig["gd_qn"], 1)
            mul(qd, qn, edb).then_inc(sig["gd_qd"], 1)
            if sample:
                pool.wait_ge(sig["gd_kd"], 1)
                pool.wait_ge(sig["gd_qd"], 1)
                for h in range(H):
                    mul(kx[:, h], bc(kd[:, h].unsqueeze(1), P, nseq, T), seqcol)
                    x = mul(qx[:, h], bc(qd[:, h].unsqueeze(1), P, nseq, T), seqcol)
                x.then_inc(sig["gd_x"], 1)
            pool.wait_ge(sig["ml_E"], 1)
            mul(mW[0:T], mW[0:T], over_heads(upto)).then_inc(sig["ml_W"], 1)

            def blocks(lv):
                pool.wait_ge(sig["gd_A"], 1)
                if lv > 2:
                    pool.wait_ge(sig["inv_p1"], lv - 2)
                mul(AM[lv % 2][0:T], A[0:T], over_heads(low(lv))).then_inc(sig["AM_ready"], 1)

            blocks(1)
            for s in range(1, nl + 1):
                if s + 1 < nl:
                    blocks(s + 1)
                pool.wait_ge(sig["hg_masked"], s + 1)
                if s > 1:
                    pool.wait_ge(sig["hg_sum"], s - 1)
                pool.tensor_tensor(hacc[0:T], hacc[0:T], htmp[s % 2][0:T], ALU.add).then_inc(sig["hg_sum"], 1)
            if sample:
                pool.wait_ge(sig["hg_qe"], 2)
                pool.wait_ge(sig["ml_qw"], 2)
                for j in range(H):
                    mul(hqx[:, j], bc(hqe[:, j].unsqueeze(1), P, nseq, T), seqcol)
                    x = mul(mqx[:, j], bc(mqw[:, j].unsqueeze(1), P, nseq, T), seqcol)
                x.then_inc(sig["qx_ready"], 1)
                pool.wait_ge(sig["ml_v"], 2)
                for h in range(H):
                    mul(hx[0:T, h], bc(tk(2, I2 + h * DKH, I2 + (h + 1) * DKH).unsqueeze(1), T, nseq, DKH),
                        bc(seqrow.unsqueeze(2), T, nseq, DKH))
                    x = mul(vx[0:T, h], bc(vext[0:T, h].unsqueeze(1), T, nseq, DKM + 1),
                            bc(seqrow.unsqueeze(2), T, nseq, DKM + 1))
                x.then_inc(sig["values_spread"], 1)
                pool.wait_ge(sig["ml_num"], 1)
                pool.wait_ge(sig["hg_o"], 1)
                for h in range(H):
                    half, j = pair_of(h)
                    e = seqs(wexp)[half, h, :, L - 1]
                    mul(st["C_ml"][half, j], st["C_ml"][half, j], bc(e.unsqueeze(2), 64, nseq, DKM + 1))
                    e = seqs(bH)[half, j, :, L - 1]
                    x = mul(st["S_hg"][half, j], st["S_hg"][half, j], bc(e.unsqueeze(2), 64, nseq, DKH))
                x.then_inc(sig["states_decayed"], 1)

                def spread(h):
                    if h > 1:
                        pool.wait_ge(sig["gd_delta"], 2 * h - 2)
                    mul(ux[h % 2][0:T], bc(u[0:T, h].unsqueeze(1), T, nseq, DKG),
                        bc(seqrow.unsqueeze(2), T, nseq, DKG)).then_inc(sig["u_spread"], 1)

                pool.wait_ge(sig["u_ready"], 1)
                spread(0)
                spread(1)
                pool.wait_ge(sig["gd_o"], 1)
                for h in range(H):
                    e = seqs(edb)[:, h, :, L - 1]
                    mul(st["S_gd"][:, h], st["S_gd"][:, h], bc(e.unsqueeze(2), P, nseq, DKG)
                        ).then_inc(sig["gd_decayed"], 1)
                spread(2)
                spread(3)

        @block.vector
        def _(dve):
            def tt(out, a, b, op):
                return dve.tensor_tensor(out, a, b, op)

            def mul(out, a, b):
                return dve.tensor_tensor(out, a, b, ALU.mult)

            def head_squares(sq, ms, name):
                dve.wait_ge(sig[name + "_sq"], 1)
                dve.tensor_reduce(ms, sq, AX.X, ALU.add).then_inc(sig[name + "_ms"], 1)

            dve.tensor_scalar(lbm, m.lbl, -1.0, 1.0, ALU.mult, ALU.add).then_inc(sig["lb_rest"], 1)
            dve.tensor_scalar(lbn, m.lbl, 1.0, None, ALU.subtract).then_inc(sig["lb_rest"], 1)
            dve.wait_ge(sig["lb_rest"], 2)
            for j in range(2):
                z = hgF(2 + j, 3 + j).rearrange("p a t -> p (a t)")
                dve.tensor_scalar(hlf[:, j], z, lbm[:, j:j + 1], m.lbl[:, j:j + 1], ALU.mult, ALU.add
                                  ).then_inc(sig["f_raw"], 1)
                dve.tensor_scalar(hk[:, j], z, lbn[:, j:j + 1], lbm[:, j:j + 1], ALU.mult, ALU.add
                                  ).then_inc(sig["hg_k"], 1)
            dve.wait_ge(sig["f_raw"], 2)
            dve.tensor_scalar(hlf, hlf, TINY, None, ALU.max).then_inc(sig["f_ready"], 1)
            dve.wait_ge(sig["gd_dcols"], 1)
            dve.tensor_copy(dcol[0:T, 0:8], G3[0:T, 0:8]).then_inc(sig["dcol_taken"], 1)
            dve.wait_ge(sig["dcol_taken"], 1)
            dve.wait_ge(sig["gd_drows"], 1)
            tt(Dg[0:T], G2[0:T, 0:W].rearrange("p (h t) -> p h t", h=H), per_head(dcol[0:T, 0:4], T), ALU.subtract
               ).then_inc(sig["gd_D"], 1)
            tt(ddc[0:T], dcol[0:T, 4:8], dcol[0:T, 0:4], ALU.subtract).then_inc(sig["gd_dd"], 1)
            dve.wait_ge(sig["gd_D"], 1)
            dve.tensor_scalar(EA[0:T], Dg[0:T], 0.0, None, ALU.max).then_inc(sig["gd_Dmax"], 1)
            dve.tensor_scalar(EB[0:T], Dg[0:T], 0.0, None, ALU.min).then_inc(sig["gd_Dmin"], 1)
            dve.wait_ge(sig["norm_ready"], 1)
            mul(kn, gt(4, 8), sqk).then_inc(sig["gd_kn"], 1)
            dve.wait_ge(sig["norm_ready"], 2)
            dve.scalar_tensor_tensor(out=qn, in0=gt(0, 4), scalar=DKG ** -0.5, in1=sqq, op0=ALU.mult, op1=ALU.mult
                                     ).then_inc(sig["gd_qn"], 1)
            dve.wait_ge(sig["logf"], 1)
            if sample:
                dve.tensor_copy(seqs(bH)[:, :, :, 0], seqs(hlf)[:, :, :, 0]).then_inc(sig["hg_b"], 1)
                for t in range(1, L):
                    dve.wait_ge(sig["hg_b"], t)
                    tt(seqs(bH)[:, :, :, t], seqs(bH)[:, :, :, t - 1], seqs(hlf)[:, :, :, t], ALU.add
                       ).then_inc(sig["hg_b"], 1)
                dve.wait_ge(sig["hg_b"], L)
            else:
                for j in range(2):
                    dve.tensor_tensor_scan(bH[:, j], ones[:, 0:T], hlf[:, j], 0.0, ALU.mult, ALU.add
                                           ).then_inc(sig["hg_b"], 1)
                dve.wait_ge(sig["hg_b"], 2)
            for lv in range(nl):
                n = 1 << (lv + 1)
                v = bH.rearrange("p x (k n) -> p x k n", n=n)
                mid = bc(v[:, :, :, n // 2 - 1:n // 2], P, 2, T // n, n)
                tt(lev[:, lv].rearrange("p x (k n) -> p x k n", n=n), v, mid, ALU.subtract).then_inc(sig["lev"], 1)
            tt(seqs(hkd), seqs(bH), bc(seqs(bH)[:, :, :, L - 1:L], P, 2, nseq, L), ALU.subtract
               ).then_inc(sig["hg_dl"], 1)
            dve.wait_ge(sig["lev"], nl)
            dve.scalar_tensor_tensor(out=lev, in0=lev, scalar=-1.0, in1=lev, op0=ALU.mult, op1=ALU.max
                                     ).then_inc(sig["lev_abs"], 1)
            dve.wait_ge(sig["gd_kk"], 1)
            dve.wait_ge(sig["gd_EAb"], 1)
            mul(A[0:T], heads(G0[0:T, 0:W]), EA[0:T]).then_inc(sig["gd_A"], 1)
            dve.wait_ge(sig["gd_kq"], 1)
            dve.wait_ge(sig["gd_EBm"], 1)
            mul(EB[0:T], heads(G1[0:T, 0:W]), EB[0:T]).then_inc(sig["gd_att"], 1)
            dve.wait_ge(sig["gd_A"], 1)
            mul(Dg[0:T], A[0:T], over_heads(low(0))).then_inc(sig["gd_A0"], 1)
            dve.wait_ge(sig["gd_A0"], 1)
            tt(Y[0:T], over_heads(ident), Dg[0:T], ALU.subtract).then_inc(sig["Y_ready"], 1)
            dve.wait_ge(sig["v_turned"], 1)
            mul(vb[0:T], heads(G3[0:T, :]), per_head(beta, DKG)).then_inc(sig["gd_vb"], 1)
            dve.wait_ge(sig["ml_bcols"], 1)
            dve.tensor_copy(bcol[0:T, 0:4], M1[0:T, 0:4]).then_inc(sig["ml_b"], 1)
            dve.tensor_copy(bcol[:, 8:12], M1[:, 8:12]).then_inc(sig["ml_b"], 1)
            dve.wait_ge(sig["ml_b"], 2)
            tt(acol[0:T], li, bcol[0:T, 0:4], ALU.subtract).then_inc(sig["ml_acol"], 1)
            dve.wait_ge(sig["ml_a_taken"], 1)
            mp = st["m_ml"]
            if sample:
                tt(seqs(M)[:, :, :, 0], seqs(ma)[:, :, :, 0], mp, ALU.max).then_inc(sig["ml_M"], 1)
                for t in range(1, L):
                    dve.wait_ge(sig["ml_M"], t)
                    tt(seqs(M)[:, :, :, t], seqs(M)[:, :, :, t - 1], seqs(ma)[:, :, :, t], ALU.max
                       ).then_inc(sig["ml_M"], 1)
            else:
                for h in range(H):
                    dve.tensor_tensor_scan(M[:, h], ma[:, h], ma[:, h], mp[:, h], ALU.max, ALU.max
                                           ).then_inc(sig["ml_M"], 1)
            dve.wait_ge(sig["ml_M"], 4)
            dve.wait_ge(sig["ml_acol"], 1)
            tt(mW[0:T], M[0:T], per_head(acol[0:T], T), ALU.subtract).then_inc(sig["ml_D"], 1)
            dve.wait_ge(sig["ml_D"], 1)
            dve.tensor_scalar(mW[0:T], mW[0:T], 0.0, None, ALU.max).then_inc(sig["ml_D"], 1)
            tt(seqs(wexp), seqs(M), bc(mp.unsqueeze(3), P, H, nseq, L), ALU.subtract).then_inc(sig["ml_wD"], 1)
            mul(ua[0:T], M[0:T], over_heads(ident)).then_inc(sig["ml_pick"], 1)
            mul(ma[0:T], M[0:T], over_heads(endsel)).then_inc(sig["ml_pick"], 1)
            dve.wait_ge(sig["ml_pick"], 2)
            dve.tensor_reduce(gcol[0:T], ua[0:T], AX.X, ALU.add).then_inc(sig["ml_cols"], 1)
            dve.tensor_reduce(gend[0:T], ma[0:T], AX.X, ALU.add).then_inc(sig["ml_cols"], 1)
            dve.wait_ge(sig["ml_cols"], 2)
            tt(kw[0:T], acol[0:T], gend[0:T], ALU.subtract).then_inc(sig["ml_kwD"], 1)
            tt(m.mcol[0:T, :], bcol[0:T, 0:4], gcol[0:T], ALU.add).then_inc(sig["ml_mt"], 1)
            if not sample:
                tt(mp.rearrange("p h b -> p (h b)"), bcol[:, 8:12], M[:, :, T - 1], ALU.add
                   ).then_inc(sig["m_next"], 1)
            dve.wait_ge(sig["ml_wexp"], 1)
            dve.wait_ge(sig["ml_q"], 2)
            for odd, half in HALVES:
                mul(mqw[half, odd::2, :], mq[half, odd::2, :], wexp[half, odd::2, :]).then_inc(sig["ml_qw"], 1)
            dve.wait_ge(sig["ml_scores"], 1)
            dve.wait_ge(sig["ml_W"], 1)
            mul(mW[0:T], heads(M0[0:T, 0:W]), mW[0:T]).then_inc(sig["ml_P"], 1)
            dve.wait_ge(sig["ml_k_turned"], 1)
            dve.wait_ge(sig["ml_kw"], 1)
            mul(heads(mks[0:T, :]), heads(M0[0:T, 0:2 * P]), per_head(kw[0:T], DKM)).then_inc(sig["ml_ks"], 1)
            dve.wait_ge(sig["hg_q"], 2)
            dve.wait_ge(sig["hg_k"], 2)
            dve.wait_ge(sig["hg_eb"], 1)
            for odd, half in HALVES:
                mul(hqe[half, odd::2, :], hq[half, odd::2, :], bH[half]).then_inc(sig["hg_qe"], 1)
            dve.wait_ge(sig["hg_ekd"], 1)
            mul(hkd, hk, hkd).then_inc(sig["hg_kd"], 1)
            dve.wait_ge(sig["k_turned"], 1)
            dve.wait_ge(sig["gd_kfac"], 1)
            mul(kdec[0:T], heads(G3[0:T, :]), per_head(kfac[0:T], DKG)).then_inc(sig["gd_kdec"], 1)

            def inverse(lv):
                dve.wait_ge(sig["inv_p2"], lv)
                tt(X[0:T], X[0:T], heads(G1[0:T, 0:W]), ALU.subtract).then_inc(sig["X_ready"], 1)
                if lv < nl - 1:
                    dve.wait_ge(sig["inv_p2t"], lv)
                    tt(Y[0:T], Y[0:T], heads(G2[0:T, 0:W]), ALU.subtract).then_inc(sig["Y_ready"], 1)

            def masked(s):
                dve.wait_ge(sig["hg_scores"], s + 1)
                dst = hacc if s == 0 else htmp[s % 2]
                if s > 2:
                    dve.wait_ge(sig["hg_sum"], s - 2)
                mul(dst[0:T], heads((H0, H1)[s % 2][0:T, 0:W]), over_heads(ident if s == 0 else up(s - 1))
                    ).then_inc(sig["hg_masked"], 1)

            def level_operands(lv):
                dve.wait_ge(sig["lev_ready"], 1)
                if lv >= 2:
                    dve.wait_ge(sig["hg_scores"], lv)
                for odd, half in HALVES:
                    mul(lq[lv % 2][half, odd::2, :], hq[half, odd::2, :], lev[half, lv]).then_inc(sig["lq"], 1)
                mul(lk[lv % 2], hk, lev[:, lv]).then_inc(sig["lq"], 1)

            for lv in range(nl):
                level_operands(lv)
                masked(lv)
                if lv > 0:
                    inverse(lv)
            masked(nl)
            dve.wait_ge(sig["ml_num"], 1)
            num = M1[0:T, 0:H * (DKM + 1)].rearrange("p (h n) -> p h n", h=H)
            dve.tensor_copy(den[0:T], num[:, :, DKM]).then_inc(sig["ml_den"], 1)
            dve.wait_ge(sig["ml_den"], 1)
            dve.scalar_tensor_tensor(out=den[0:T], in0=den[0:T], scalar=-1.0, in1=den[0:T], op0=ALU.mult, op1=ALU.max
                                     ).then_inc(sig["ml_den"], 1)
            dve.wait_ge(sig["ml_den"], 2)
            dve.wait_ge(sig["ml_emt"], 1)
            tt(den[0:T], den[0:T], emt[0:T], ALU.max).then_inc(sig["ml_den"], 1)
            dve.wait_ge(sig["ml_den"], 3)
            dve.reciprocal(den[0:T], den[0:T]).then_inc(sig["ml_den"], 1)
            dve.wait_ge(sig["ml_den"], 4)
            mul(heads(mog[0:T, :]), num[:, :, 0:DKM], per_head(den[0:T], DKM)).then_inc(sig["ml_h"], 1)
            dve.wait_ge(sig["ml_h"], 1)
            mul(mog[0:T, :], mog[0:T, :], tk(0, O0, O0 + H * DKM)).then_inc(sig["ml_gated"], 1)
            head_squares(heads(m_sq[0:T, :]), mms[0:T], "ml")
            dve.wait_ge(sig["ml_delta"], 1)
            C = st["C_ml"]
            if not sample:
                for h in range(H):
                    half, j = pair_of(h)
                    dve.scalar_tensor_tensor(out=C[half, j, 0], in0=C[half, j, 0], scalar=wexp[half, h, T - 1:T],
                                             in1=M0[half, h * (DKM + 1):(h + 1) * (DKM + 1)],
                                             op0=ALU.mult, op1=ALU.add).then_inc(sig["ml_state"], 1)
            else:
                dve.wait_ge(sig["states_decayed"], 1)
                for h in range(H):
                    half, j = pair_of(h)
                    for q in range(2):
                        i = 2 * h + q
                        dve.wait_ge(sig["ml_delta"], i + 1)
                        b = (M0, H1)[i % 2]
                        tt(C[half, j, 4 * q:4 * q + 4], C[half, j, 4 * q:4 * q + 4],
                           b[half, 0:4 * (DKM + 1)].rearrange("p (b n) -> p b n", b=4), ALU.add
                           ).then_inc(sig["ml_state"], 1)
            dve.wait_ge(sig["ml_rstd"], 2)
            mul(heads(mog[0:T, :]), heads(mog[0:T, :]), per_head(mms[0:T], DKM)).then_inc(sig["ml_normed"], 1)
            dve.wait_ge(sig["ml_normed"], 1)
            mul(heads(mix[0:T, 0:H * DKM]), heads(mog[0:T, :]),
                bc(rows["mlw"][0:T].unsqueeze(1), T, H, DKM)).then_inc(sig["mix"], 1)
            head_squares(heads(hog[0:T, :]), hms[0:T], "hg")
            dve.wait_ge(sig["hg_rstd"], 2)
            hm = mix[0:T, H * (DKM + DKG):]
            mul(heads(hog[0:T, :]), heads(H0[0:T, 0:H * DKH]), per_head(hms[0:T], DKH)).then_inc(sig["hg_normed"], 1)
            dve.wait_ge(sig["hg_normed"], 1)
            mul(hm, hog[0:T, :], tk(2, OG2, OG2 + H * DKH)).then_inc(sig["mix"], 1)
            Sh = st["S_hg"]
            for h in range(H):
                half, j = pair_of(h)
                if not sample:
                    dve.wait_ge(sig["hg_delta"], 1)
                    dve.scalar_tensor_tensor(out=Sh[half, j, 0], in0=Sh[half, j, 0], scalar=bH[half, j, T - 1:T],
                                             in1=H1[half, h * DKH:(h + 1) * DKH], op0=ALU.mult, op1=ALU.add
                                             ).then_inc(sig["hg_state"], 1)
                else:
                    dve.wait_ge(sig["hg_delta"], h + 1)
                    tt(Sh[half, j], Sh[half, j], (H1, M0)[h % 2][half, :].rearrange("p (b n) -> p b n", b=nseq),
                       ALU.add).then_inc(sig["hg_state"], 1)
            dve.wait_ge(sig["gd_kS"], 1)
            dve.wait_ge(sig["gd_vb"], 1)
            mul(r[0:T], heads(G0[0:T, :]), per_head(beta, DKG)).then_inc(sig["gd_r"], 1)
            dve.wait_ge(sig["gd_r"], 1)
            tt(r[0:T], vb[0:T], r[0:T], ALU.subtract).then_inc(sig["gd_r"], 1)
            head_squares(heads(og[0:T, :]), msg[0:T], "gd")
            S = st["S_gd"]
            if not sample:
                dve.wait_ge(sig["gd_delta"], 1)
                for h in range(H):
                    dve.scalar_tensor_tensor(out=S[:, h, 0], in0=S[:, h, 0], scalar=edb[:, h, T - 1:T],
                                             in1=G3[:, h * DKG:(h + 1) * DKG], op0=ALU.mult, op1=ALU.add)
            else:
                for h in range(H):
                    dve.wait_ge(sig["gd_decayed"], h + 1)
                    for q in range(2):
                        i = 2 * h + q
                        dve.wait_ge(sig["gd_delta"], i + 1)
                        tt(S[:, h, 4 * q:4 * q + 4], S[:, h, 4 * q:4 * q + 4],
                           (G3, G0)[i % 2][:, :].rearrange("p (b n) -> p b n", b=4), ALU.add
                           ).then_inc(sig["gd_state"], 1)
            dve.wait_ge(sig["gd_rstd"], 2)
            mul(heads(og[0:T, :]), heads(G2[0:T, :]), per_head(msg[0:T], DKG)).then_inc(sig["gd_normed"], 1)
            dve.wait_ge(sig["gd_normed"], 1)
            mul(mix[0:T, H * DKM:H * (DKM + DKG)], og[0:T, :], tk(1, OG1, OG1 + H * DKG)).then_inc(sig["mix"], 1)
            dve.wait_ge(sig["mix_turned"], 1)
            dve.tensor_copy(hTc[:, 0:4, :], M0[:, 0:W].rearrange("p (k t) -> p k t", k=4))

        @block.tensor
        def _(pe):
            def per_h(bank, width, lhs, rhs, done, n=T):
                for h in range(H):
                    mm = pe.matmul(bank[0:n, h * width:(h + 1) * width], lhs(h), rhs(h), start=True, stop=True)
                return mm.then_inc(sig[done], 1)

            def flat(ap):
                return ap.rearrange("p h t -> p (h t)")

            for i, (b, sq) in enumerate(((G0, sqk), (G1, sqq))):
                pe.wait_ge(sig["squares"], i + 1)
                pe.matmul(b[:, 0:W], ones, flat(sq), start=True, stop=True).then_inc(sig["norm_sums"], 1)
            pe.wait_ge(sig["gd_ug"], 1)
            pe.matmul(G2[:, 0:W], ones[0:T, :], flat(ug[0:T]), start=True, stop=True).then_inc(sig["gd_drows"], 1)
            pe.matmul(G3[0:T, 0:4], upto, gg, start=True, stop=True)
            pe.matmul(G3[0:T, 4:8], same, gg, start=True, stop=True).then_inc(sig["gd_dcols"], 1)
            pe.wait_ge(sig["ml_ua_ready"], 1)
            pe.matmul(M0[:, 0:W], ones[0:T, :], flat(ua[0:T]), start=True, stop=True).then_inc(sig["ml_arows"], 1)
            pe.matmul(M1[:, 8:12], ones[0:T, :], lf, start=True, stop=True)
            pe.matmul(M1[0:T, 0:4], upto, lf, start=True, stop=True).then_inc(sig["ml_bcols"], 1)

            def turn(bank, src, n, done):
                for k in range(n):
                    mm = pe.transpose(bank[0:T, k * P:(k + 1) * P], src[:, k, :], m.c("ident"))
                mm.then_inc(sig[done], 1)

            pe.wait_ge(sig["v_taken"], 1)
            pe.wait_ge(sig["dcol_taken"], 1)
            turn(G3, vS, H, "v_turned")
            pe.wait_ge(sig["gd_kn"], 1)
            per_h(G0, T, lambda h: kn[:, h], lambda h: kn[:, h], "gd_kk")
            pe.wait_ge(sig["gd_qn"], 1)
            per_h(G1, T, lambda h: kn[:, h], lambda h: qn[:, h], "gd_kq")
            pe.wait_ge(sig["ml_a_taken"], 1)
            pe.wait_ge(sig["ml_q"], 2)
            pe.wait_ge(sig["ml_k"], 1)

            def pairs(bank, a, b, done):
                for h in range(H):
                    mm = pe.matmul(bank[0:T, h * T:(h + 1) * T], a[:, h // 2], b[:, h], start=True, stop=True)
                mm.then_inc(sig[done], 1)

            pairs(M0, mk, mq, "ml_scores")
            pe.wait_ge(sig["gd_edb"], 1)
            pe.wait_ge(sig["gd_Dmin"], 1)
            pe.wait_ge(sig["Y_ready"], 1)
            for h in range(H):
                mm = pe.transpose(G2[0:T, h * T:(h + 1) * T], Y[0:T, h], ident)
            mm.then_inc(sig["gd_X0"], 1)
            pe.wait_ge(sig["gd_vb"], 1)
            turn(G3, kn, H, "k_turned")
            pe.wait_ge(sig["ml_P"], 1)
            turn(M0, mk, 2, "ml_k_turned")

            def inverse(lv):
                pe.wait_ge(sig["AM_ready"], lv)
                pe.wait_ge(sig["X_ready"], lv)
                per_h(G0, T, lambda h: AM[lv % 2][0:T, h], lambda h: X[0:T, h], "inv_p1")
                pe.wait_ge(sig["inv_p1_taken"], lv)
                pe.wait_ge(sig["Y_ready"], lv)
                if lv == 1:
                    pe.wait_ge(sig["gd_att"], 1)
                per_h(G1, T, lambda h: Y[0:T, h], lambda h: p1[0:T, h], "inv_p2")
                if lv < nl - 1:
                    per_h(G2, T, lambda h: p1[0:T, h], lambda h: Y[0:T, h], "inv_p2t")

            def scores(s):
                if s == 0:
                    pe.wait_ge(sig["hg_q"], 2)
                    pe.wait_ge(sig["hg_k"], 2)
                else:
                    pe.wait_ge(sig["lq"], 3 * s)
                if s >= 2:
                    pe.wait_ge(sig["hg_masked"], s - 1)
                a, b = (hk, hq) if s == 0 else (lk[(s - 1) % 2], lq[(s - 1) % 2])
                pairs((H0, H1)[s % 2], a, b, "hg_scores")

            scores(0)
            for lv in range(nl):
                scores(lv + 1)
                if lv > 0:
                    inverse(lv)
            n1 = DKM + 1
            pe.wait_ge(sig["ml_P"], 1)
            pe.wait_ge(sig["ml_qw"], 2)
            pe.wait_ge(sig["ml_v"], 2)
            pe.wait_ge(sig["ml_b"], 2)
            if sample:
                pe.wait_ge(sig["qx_ready"], 1)
            for h in range(H):
                out = M1[0:T, h * n1:(h + 1) * n1]
                for b in range(nseq):
                    lhs = mqx[:, h, b] if sample else mqw[:, h]
                    pe.matmul(out, lhs, st["C_ml"][:, h // 2, b], start=(b == 0), stop=False)
                mm = pe.matmul(out, mW[0:T, h], vext[0:T, h], start=False, stop=True)
            mm.then_inc(sig["ml_num"], 1)
            pe.wait_ge(sig["ml_ks"], 1)
            if not sample:
                for h in range(H):
                    half, j = pair_of(h)
                    mm = pe.matmul(M0[:, h * n1:(h + 1) * n1], mks[0:T, j * P:(j + 1) * P], vext[0:T, h],
                                   start=True, stop=True)
                mm.then_inc(sig["ml_delta"], 1)
            pe.wait_ge(sig["hg_kd"], 1)
            pe.wait_ge(sig["hg_masked"], nl + 1)
            turn(H1, hkd, 2, "hg_k_turned")
            pe.wait_ge(sig["hg_qe"], 2)
            pe.wait_ge(sig["hg_sum"], nl)
            for h in range(H):
                out = H0[0:T, h * DKH:(h + 1) * DKH]
                for b in range(nseq):
                    lhs = hqx[:, h, b] if sample else hqe[:, h]
                    pe.matmul(out, lhs, st["S_hg"][:, h // 2, b], start=(b == 0), stop=False)
                mm = pe.matmul(out, hacc[0:T, h], tk(2, I2 + h * DKH, I2 + (h + 1) * DKH), start=False, stop=True)
            mm.then_inc(sig["hg_o"], 1)
            pe.wait_ge(sig["hg_kT"], 1)
            if not sample:
                for h in range(H):
                    half, j = pair_of(h)
                    mm = pe.matmul(H1[:, h * DKH:(h + 1) * DKH], hkdT[0:T, j * P:(j + 1) * P],
                                   tk(2, I2 + h * DKH, I2 + (h + 1) * DKH), start=True, stop=True)
                mm.then_inc(sig["hg_delta"], 1)
            else:
                pe.wait_ge(sig["values_spread"], 1)
                for i in range(2 * H):
                    h, q = i // 2, i % 2
                    half, j = pair_of(h)
                    if i >= 2:
                        pe.wait_ge(sig["ml_state"], i - 1)
                    b = (M0, H1)[i % 2]
                    pe.matmul(b[:, 0:4 * n1], mks[0:T, j * P:(j + 1) * P],
                              vx[0:T, h, 4 * q:4 * q + 4].rearrange("p b n -> p (b n)"), start=True, stop=True
                              ).then_inc(sig["ml_delta"], 1)
                pe.wait_ge(sig["ml_state"], 2 * H)
                for h in range(H):
                    half, j = pair_of(h)
                    if h >= 2:
                        pe.wait_ge(sig["hg_state"], h - 1)
                    pe.matmul((H1, M0)[h % 2][:, :], hkdT[0:T, j * P:(j + 1) * P],
                              hx[0:T, h].rearrange("p b n -> p (b n)"), start=True, stop=True
                              ).then_inc(sig["hg_delta"], 1)
            pe.wait_ge(sig["gd_kd"], 1)
            if sample:
                pe.wait_ge(sig["gd_x"], 1)
            for h in range(H):
                for b in range(nseq):
                    lhs = kx[:, h, b] if sample else kd[:, h]
                    mm = pe.matmul(G0[0:T, h * DKG:(h + 1) * DKG], lhs, st["S_gd"][:, h, b],
                                   start=(b == 0), stop=(b == nseq - 1))
            mm.then_inc(sig["gd_kS"], 1)
            pe.wait_ge(sig["gd_r"], 2)
            pe.wait_ge(sig["X_ready"], nl)
            per_h(G1, DKG, lambda h: X[0:T, h], lambda h: r[0:T, h], "gd_u")
            pe.wait_ge(sig["gd_qd"], 1)
            pe.wait_ge(sig["u_ready"], 1)
            for h in range(H):
                out = G2[0:T, h * DKG:(h + 1) * DKG]
                for b in range(nseq):
                    lhs = qx[:, h, b] if sample else qd[:, h]
                    pe.matmul(out, lhs, st["S_gd"][:, h, b], start=(b == 0), stop=False)
                mm = pe.matmul(out, EB[0:T, h], u[0:T, h], start=False, stop=True)
            mm.then_inc(sig["gd_o"], 1)
            pe.wait_ge(sig["gd_kdec"], 1)
            if not sample:
                per_h(G3, DKG, lambda h: kdec[0:T, h], lambda h: u[0:T, h], "gd_delta", n=P)
            else:
                for i in range(2 * H):
                    h, q = i // 2, i % 2
                    pe.wait_ge(sig["u_spread"], h + 1)
                    if i >= 2:
                        pe.wait_ge(sig["gd_state"], i - 1)
                    pe.matmul((G3, G0)[i % 2][:, :], kdec[0:T, h],
                              ux[h % 2][0:T, 4 * q:4 * q + 4].rearrange("p b n -> p (b n)"), start=True, stop=True
                              ).then_inc(sig["gd_delta"], 1)
            pe.wait_ge(sig["mix"], 3)
            if sample:
                pe.wait_ge(sig["hg_state"], H)
            else:
                pe.wait_ge(sig["ml_state"], H)
            for g in range(2):
                for k in range(4):
                    kt = 4 * g + k
                    mm = pe.transpose((M0, M1)[g][:, k * T:(k + 1) * T], mix[0:T, kt * P:(kt + 1) * P], ident)
                mm.then_inc(sig["mix_turned"], 1)


def out_phase(nc, m, d, l):
    one = bass.ds(l, 1)
    with phase(nc) as (sig, block):
        @block.sync
        def _(sp):
            with sp.Fori(0, 2) as j:
                for k in range(KT):
                    sp.wait_ge(sig[f"slab{k}_used"], j + 1)
                    sp.dma_start(m.slab[:, k, 0:512], d["w_out"][one, k * P:(k + 1) * P, bass.ds(j * 512, 512)]
                                 .rearrange("o p n -> (o p) n")).then_inc(sig[f"slab{k}_loaded"], 16)

        @block.tensor
        def _(pe):
            for k in range(KT):
                pe.sem_inc(sig[f"slab{k}_used"], 1)
            with pe.Fori(0, 2) as j:
                for k in range(KT):
                    pe.wait_ge(sig[f"slab{k}_loaded"], 16 * j + 16)
                    for i in range(NT):
                        n = tile_rows(i)
                        if k == 0:
                            pe.wait_ge(sig["bank_read"], NT * j + i + 1)
                        mm = pe.matmul(m.bank[i][0:n, :], m.hT[:, k, i * P:i * P + n], m.slab[:, k, 0:512],
                                       start=(k == 0), stop=(k == KT - 1))
                        if k == KT - 1:
                            mm.then_inc(sig["bank_done"], 1)
                        elif i == NT - 1:
                            mm.then_inc(sig[f"slab{k}_used"], 1)
                pe.wait_ge(sig["bank_done"], NT * j + NT)
                pe.sem_inc(sig[f"slab{KT - 1}_used"], 1)

        @block.vector
        def _(dve):
            add_to_x(dve, m, sig)


def add_to_x(dve, m, sig):
    dve.sem_inc(sig["bank_read"], NT)
    with dve.Fori(0, 2) as j:
        for i in range(NT):
            n = tile_rows(i)
            dve.wait_ge(sig["bank_done"], NT * j + i + 1)
            x = m.x[0:n, i, bass.ds(j * 512, 512)]
            dve.tensor_tensor(x, x, m.bank[i][0:n, :], ALU.add).then_inc(sig["bank_read"], 1)


def up_phase(nc, m, d, l):
    one = bass.ds(l, 1)
    m.top = m.arena + 16 * GROUP
    silu = m.take(4, HALF)
    N = FF // 256
    with phase(nc) as (sig, block):
        @block.sync
        def _(sp):
            with sp.Fori(0, N) as j:
                for k in range(KT):
                    if k < KT - 1:
                        sp.wait_ge(sig[f"slab{k}_used"], j + 1)
                    else:
                        sp.wait_ge(sig["up_done"], 4 * j + 4)
                    w = d["w_gate_up"]
                    for half in range(2):
                        sp.dma_start(m.slab[:, k, 256 * half:256 * (half + 1)],
                                     w[one, k * P:(k + 1) * P, bass.ds(j * 256 + half * FF, 256)]
                                     .rearrange("o p n -> (o p) n")).then_inc(sig[f"slab{k}_loaded"], 16)

        @block.tensor
        def _(pe):
            for k in range(KT - 1):
                pe.sem_inc(sig[f"slab{k}_used"], 1)
            pe.sem_inc(sig["up_done"], 4)
            with pe.Fori(0, N) as j:
                for k in range(KT):
                    pe.wait_ge(sig[f"slab{k}_loaded"], 32 * j + 32)
                    for b in range(8):
                        t, half = b // 2, b % 2
                        gate = b < 4
                        if k == 0:
                            pe.wait_ge(sig["gate_read" if gate else "up_read"], 4 * j + b % 4 + 1)
                        mm = pe.matmul(m.bank[b][:, 0:HALF], m.slab[:, k, t * P:(t + 1) * P],
                                       m.hT[:, k, half * HALF:(half + 1) * HALF], start=(k == 0), stop=(k == KT - 1))
                        if k == KT - 1:
                            mm.then_inc(sig["gate_done" if gate else "up_done"], 1)
                        elif b == 7:
                            mm.then_inc(sig[f"slab{k}_used"], 1)

        @block.scalar
        def _(act):
            act.sem_inc(sig["gate_read"], 4)
            with act.Fori(0, N) as j:
                for b in range(4):
                    act.wait_ge(sig["gate_done"], 4 * j + b + 1)
                    act.wait_ge(sig["up_read"], 4 * j + b + 1)
                    act.activation(silu[:, b, :], m.bank[b][:, 0:HALF], ACT.Silu).then_inc(sig["gate_read"], 1)

        @block.vector
        def _(dve):
            dve.sem_inc(sig["up_read"], 4)
            with dve.Fori(0, N) as j:
                for b in range(4):
                    dve.wait_ge(sig["up_done"], 4 * j + b + 5)
                    dve.wait_ge(sig["gate_read"], 4 * j + b + 5)
                    out = m.act[:, bass.ds(2 * j + b // 2, 1), (b % 2) * HALF:(b % 2 + 1) * HALF]
                    dve.tensor_tensor(out.rearrange("p o n -> p (o n)"), silu[:, b, :], m.bank[4 + b][:, 0:HALF],
                                      ALU.mult).then_inc(sig["up_read"], 1)


def down_phase(nc, m, d, l):
    one = bass.ds(l, 1)
    with phase(nc) as (sig, block):
        def turns(k):
            return k % 16, (2 if k % 16 < FT - 16 else 1)

        @block.sync
        def _(sp):
            with sp.Fori(0, 2) as j:
                for k in range(FT):
                    s, per = turns(k)
                    sp.wait_ge(sig[f"slab{s}_used"], per * j + k // 16 + 1)
                    sp.dma_start(m.slab[:, s, 0:512], d["w_down"][one, k * P:(k + 1) * P, bass.ds(j * 512, 512)]
                                 .rearrange("o p n -> (o p) n")).then_inc(sig[f"slab{s}_loaded"], 16)

        @block.tensor
        def _(pe):
            for s in range(16):
                pe.sem_inc(sig[f"slab{s}_used"], 1)
            with pe.Fori(0, 2) as j:
                for k in range(FT):
                    s, per = turns(k)
                    pe.wait_ge(sig[f"slab{s}_loaded"], 16 * per * j + 16 * (k // 16 + 1))
                    for i in range(NT):
                        n = tile_rows(i)
                        if k == 0:
                            pe.wait_ge(sig["bank_read"], NT * j + i + 1)
                        mm = pe.matmul(m.bank[i][0:n, :], m.act[:, k, i * P:i * P + n], m.slab[:, s, 0:512],
                                       start=(k == 0), stop=(k == FT - 1))
                        if k == FT - 1:
                            mm.then_inc(sig["bank_done"], 1)
                        elif i == NT - 1:
                            mm.then_inc(sig[f"slab{s}_used"], 1)
                pe.wait_ge(sig["bank_done"], NT * j + NT)
                pe.sem_inc(sig[f"slab{turns(FT - 1)[0]}_used"], 1)

        @block.vector
        def _(dve):
            add_to_x(dve, m, sig)


def build(nc, d, const_at, n_const):
    with ExitStack() as stack:
        stack.enter_context(nc.allow_non_contiguous_dma(reason="the states n and m are a few thousand words"))
        m = Memory(nc, stack, const_at, n_const)
        setup_phase(nc, m, d)
        with nc.Fori(0, DEPTH) as l:
            norm_phase(nc, m, d, l, 0)
            project_phase(nc, m, d, l)
            prep_phase(nc, m, d, l)
            start_states(nc, m)
            prompt = {"S_gd": m.S_gd, "C_ml": m.C_ml, "S_hg": m.S_hg, "m_ml": m.m_ml}
            with nc.Fori(0, SEQ // P) as c:
                chunk_phase(nc, m, prompt, 1, c)
            store_states(nc, m, d, l, prompt, "p", 1, m.mcol, slice(P - 1, P))
            st = load_sample_states(nc, m, d, l)
            chunk_phase(nc, m, st, NSEQ, None)
            store_states(nc, m, d, l, st, "s", NSEQ, m.mcol, slice(DSEQ - 1, SAMP, DSEQ))
            out_phase(nc, m, d, l)
            norm_phase(nc, m, d, l, 1)
            up_phase(nc, m, d, l)
            down_phase(nc, m, d, l)
        norm_phase(nc, m, d, None, 2)


_INS = ["x_prompt", "x_sample", "state_mlstm_C", "state_mlstm_n", "state_mlstm_m", "state_gdn_S", "state_gdn_conv",
        "state_hgrn_S", "norm1_w", "w_in", "ml_i_bias", "ml_f_bias", "ml_norm_w", "gd_conv_w", "gd_A_log",
        "gd_dt_bias", "gd_norm_w", "hg_lower_bounds", "hg_norm_w", "w_out", "norm2_w", "w_gate_up", "w_down",
        "final_norm_w"]


def _states(who, b):
    return [(who + "_C", (DEPTH, b, H, DKM, DKM)), (who + "_n", (DEPTH, b, H, DKM)), (who + "_m", (DEPTH, b, H)),
            (who + "_S", (DEPTH, b, H, DKG, DKG)), (who + "_conv", (DEPTH, b, CONV - 1, 3 * H * DKG)),
            (who + "_H", (DEPTH, b, H, DKH, DKH))]


_OUTS = [("y_prompt", (1, SEQ, D)), ("y_sample", (NSEQ, DSEQ, D))] + _states("p", 1) + _states("s", NSEQ)


def kernel(**inputs):
    import concourse.bacc as bacc
    from concourse.bass_utils import run_bass_kernel_spmd as run

    nc = bacc.Bacc("TRN2", target_bir_lowering=False, num_devices=1)
    consts, const_at = constants()
    arrays, d = {"in_consts": consts}, {}
    for name in _INS:
        arrays["in_" + name] = np.ascontiguousarray(inputs[name])
    for name, a in arrays.items():
        d[name[3:]] = nc.dram_tensor(name, a.shape, mybir.dt.from_np(a.dtype), kind="ExternalInput").ap()
    for name, shape in _OUTS:
        d[name] = nc.dram_tensor("out_" + name, shape, F32, kind="ExternalOutput").ap()
    build(nc, d, const_at, consts.shape[1])
    r = run(nc, [arrays], core_ids=[0])
    return tuple(r.results[0]["out_" + name] for name, _ in _OUTS)
```

```python
from contextlib import ExitStack, contextmanager

import numpy as np

import concourse.bass as bass
from concourse import mybir

F32 = mybir.dt.float32
F32R = mybir.dt.float32r
ALU = mybir.AluOpType
ACT = mybir.ActivationFunctionType
AX = mybir.AxisListType

P = 128
D, SEQ, DEPTH, NSEQ, DSEQ = 1024, 512, 2, 8, 4
SAMP = NSEQ * DSEQ
TOK = SEQ + SAMP
HALF = TOK // 2
NT = SEQ // P + 1
H = 4
DKM, DKG, DKH = 64, 128, 64
CONV = 4
GT = 3 * H * DKG // P
KT = D // P
FF = 2816
FT = FF // P
MIX = H * (DKM + DKG + DKH)
EPS = 1e-6
LEVELS = 7
TINY = 2.0 ** -63

ML_QK, ML_VO, GD_QKV, GD_G, HG_QF, HG_IG = 0, 512, 1032, 2568, 3088, 3600
GROUP = 520
V0, O0, I0, F0 = 0, 256, 512, 516
OG1, A1, B1 = 0, 512, 516
I2, OG2 = 0, 256
LI, LF, GG, BETA = 0, 4, 8, 12

ARENA = 21240
SLOTS = 11

SEM0 = 110
EXP_LN = "natural_log_exp_and_others"


def constants():
    s, t = np.meshgrid(np.arange(P), np.arange(P), indexing="ij")
    parts, at, n = [], {}, 0

    def put(name, a):
        nonlocal n
        at[name] = (n, a.shape[1])
        parts.append(a.astype(np.float32))
        n += a.shape[1]

    put("ident", s == t)
    put("ones", np.ones((P, P)))
    put("upto", s <= t)
    put("end", np.broadcast_to(t == P - 1, (P, P)))
    for l in range(LEVELS):
        block = (s >> (l + 1)) == (t >> (l + 1))
        put(f"low{l}", block & ((s >> l) & 1 == 1) & ((t >> l) & 1 == 0))
        put(f"up{l}", block & ((t >> l) & 1 == 1) & ((s >> l) & 1 == 0))
    same = (s // DSEQ) == (t // DSEQ)
    k = SAMP
    put("upto_s", (same & (s <= t))[:, :k])
    put("same_s", same[:, :k])
    put("end_s", (same & (t % DSEQ == DSEQ - 1))[:, :k])
    b, tt = np.meshgrid(np.arange(NSEQ), np.arange(k), indexing="ij")
    put("seq_of_column", np.broadcast_to((tt // DSEQ == b).reshape(1, -1), (P, NSEQ * k)))
    put("seq_of_row", (np.arange(P)[:, None] // DSEQ) == np.arange(NSEQ)[None])
    return np.concatenate(parts, axis=1), at


class Signals:

    def __init__(self, nc):
        self.nc, self.named = nc, {}

    def __getitem__(self, name):
        if name not in self.named:
            self.named[name] = self.nc.alloc_semaphore(name, num=SEM0 + len(self.named))
        return self.named[name]


@contextmanager
def phase(nc):
    sig = Signals(nc)
    with nc.Block(no_gpsimd_drain=True) as block:
        yield sig, block
    for s in sig.named.values():
        nc.release_semaphore(s)
    nc.all_engine_barrier(sems_to_clear=range(SEM0, SEM0 + len(sig.named)))


def bc(ap, *shape):
    return ap.broadcast_to(list(shape))


def tile_rows(i):
    return SAMP if i == NT - 1 else P


class Memory:

    def __init__(self, nc, stack, const_at, n_const):
        self.nc, self.stack = nc, stack
        self.words = nc.sbuf_bytes_remaining // 4 // 8 * 8 - 8
        self.arena = self.words - ARENA
        self.all = stack.enter_context(nc.sbuf_tensor("sbuf", [P, self.arena], F32))
        self.area, self.tensors = None, 0
        self.top = 0
        self.bank = [stack.enter_context(nc.psum_tensor(f"bank{i}", [P, 512], F32)) for i in range(8)]
        self.const = self.take(n_const)
        self.const_at = const_at
        self.x = self.take(KT, TOK)
        self.hT_at = self.top
        self.hT = self.take(KT, TOK)
        work = self.top
        self.mlF = self.take(4, TOK)
        self.gdF_at = self.top
        self.gdF = self.take(GT, CONV - 1 + SEQ)
        self.gdS = self.take(GT, NSEQ, CONV - 1 + DSEQ)
        self.gdC_at = self.top
        self.gdC = self.take(GT, SAMP)
        self.hgF = self.take(4, TOK)
        self.tokp_at = self.top
        self.tokp = self.take(NT, 3, GROUP)
        self.act = self.view(work, FT, TOK)
        self.top, tokp_end = work + FT * TOK, self.top
        self.down_slab = self.take(SLOTS, 512)
        self.silu = self.take(4, HALF)
        self.rstd2 = self.take(TOK)
        assert self.top <= tokp_end
        self.top = tokp_end
        self.gates = self.take(NT, 16)
        self.colw = self.take(64)
        self.lb = self.take(DEPTH * 2)
        self.rows = self.take(16 + 64 + 64 + 128)
        self.lbl = self.take(2)
        self.mcol = self.take(4)
        self.S_gd = self.take(H, 1, DKG)
        self.C_ml = self.take(2, 1, DKM + 1)
        self.S_hg = self.take(2, 1, DKH)
        self.m_ml = self.take(H, 1)
        assert self.top <= self.arena

    @contextmanager
    def tensor(self, shape, dtype):
        self.tensors += 1
        with self.nc.sbuf_tensor(f"arena{self.tensors}", [P] + list(shape), dtype) as t:
            yield t

    @contextmanager
    def open_area(self):
        with self.tensor([ARENA], F32) as t:
            self.area = t
            yield
        self.area = None

    def view(self, at, *shape):
        n = int(np.prod(shape))
        ap = self.all[:, at:at + n] if at < self.arena else self.area[:, at - self.arena:at - self.arena + n]
        if len(shape) == 1:
            return ap
        names = "abcd"[:len(shape)]
        sizes = dict(zip(names, shape))
        return ap.rearrange(f"p ({' '.join(names)}) -> p {' '.join(names)}", **sizes)

    def take(self, *shape):
        ap = self.view(self.top, *shape)
        self.top += int(np.prod(shape))
        assert self.top <= self.words
        return ap

    def c(self, name, rows=P):
        at, n = self.const_at[name]
        return self.const[0:rows, at:at + n]


def layer_rows(m):
    r = m.rows
    return {"ibias": r[:, 0:4], "fbias": r[:, 4:8], "negA": r[:, 8:12], "dtb": r[:, 12:16],
            "mlw": r[:, 16:80], "hgw": r[:, 80:144], "gdw": r[:, 144:272]}


def setup_phase(nc, m, d):
    m.top = m.arena
    xt = m.take(NT, D)
    lbr = m.take(P)
    pr = m.take(DEPTH * 2)
    mx, sm = m.take(2), m.take(2)
    with phase(nc) as (sig, block):
        @block.sync
        def _(sp):
            sp.dma_start(m.const, d["consts"]).then_inc(sig["const_loaded"], 16)
            for i in range(NT):
                src = d["x_prompt"][0, i * P:(i + 1) * P, :] if i < NT - 1 else \
                    d["x_sample"].rearrange("b t n -> (b t) n")
                sp.dma_start(xt[0:tile_rows(i), i, :], src).then_inc(sig[f"x{i}_loaded"], 16)
            sp.dma_start(lbr[0:2 * DEPTH, :],
                         d["hg_lower_bounds"].rearrange("l (j p) -> (l j) p", p=P)).then_inc(sig["bounds_loaded"], 16)

        @block.gpsimd
        def _(pool):
            pool.memset(m.tokp[:, NT - 1], 0.0)

        @block.tensor
        def _(pe):
            pe.wait_ge(sig["const_loaded"], 16)
            pe.wait_ge(sig["bounds_loaded"], 16)
            pe.transpose(m.bank[0][:, 0:2 * DEPTH], lbr[0:2 * DEPTH, :], m.c("ident", 2 * DEPTH)[:, 0:2 * DEPTH]
                         ).then_inc(sig["bounds_turned"], 1)
            for i in range(NT):
                n = tile_rows(i)
                pe.wait_ge(sig[f"x{i}_loaded"], 16)
                for g in range(2):
                    u = 2 * i + g
                    if u >= 6:
                        pe.wait_ge(sig["x_taken"], u - 5)
                    for k in range(4):
                        kt = 4 * g + k
                        mm = pe.transpose(m.bank[1 + u % 6][:, k * n:(k + 1) * n], xt[0:n, i, kt * P:(kt + 1) * P],
                                          m.c("ident", n)[:, 0:n])
                    mm.then_inc(sig["x_turned"], 1)

        @block.vector
        def _(dve):
            b = m.bank[0][:, 0:2 * DEPTH]
            dve.wait_ge(sig["bounds_turned"], 1)
            dve.tensor_copy(pr, b).then_inc(sig["bounds"], 1)
            dve.wait_ge(sig["bounds"], 1)
            dve.tensor_tensor(mx, pr[:, 0:2], pr[:, 2:4], ALU.max).then_inc(sig["bounds"], 1)
            dve.wait_ge(sig["bounds"], 2)
            for l in range(DEPTH):
                dve.tensor_tensor(m.lb[:, 2 * l:2 * l + 2], pr[:, 2 * l:2 * l + 2], mx, ALU.subtract
                                  ).then_inc(sig["bounds_shifted"], 1)
            dve.wait_ge(sig["bounds_exp"], 1)
            dve.tensor_tensor(sm, pr[:, 0:2], pr[:, 2:4], ALU.add).then_inc(sig["bounds"], 1)
            dve.wait_ge(sig["bounds"], 3)
            dve.reciprocal(mx, sm).then_inc(sig["bounds"], 1)
            dve.wait_ge(sig["bounds"], 4)
            dve.tensor_tensor(pr[:, 0:2], pr[:, 0:2], mx, ALU.mult).then_inc(sig["bounds"], 1)
            dve.tensor_tensor(pr[:, 2:4], pr[:, 2:4], mx, ALU.mult).then_inc(sig["bounds"], 1)
            dve.wait_ge(sig["bounds"], 6)
            dve.tensor_tensor(m.lb[:, 0:2], pr[:, 0:2], pr[:, 0:2], ALU.subtract)
            dve.tensor_tensor(sm, pr[:, 0:2], pr[:, 2:4], ALU.add).then_inc(sig["bounds"], 1)
            dve.wait_ge(sig["bounds"], 7)
            dve.tensor_tensor(m.lb[:, 2:4], sm, pr[:, 0:2], ALU.subtract)

        @block.scalar
        def _(act):
            nc.scalar.preload_act_table_set(EXP_LN)
            act.wait_ge(sig["bounds_shifted"], DEPTH)
            act.activation(pr, m.lb, ACT.Exp).then_inc(sig["bounds_exp"], 1)
            for i in range(NT):
                n = tile_rows(i)
                for g in range(2):
                    u = 2 * i + g
                    act.wait_ge(sig["x_turned"], u + 1)
                    act.copy(m.x[:, 4 * g:4 * g + 4, i * P:i * P + n],
                             m.bank[1 + u % 6][:, 0:4 * n].rearrange("p (k t) -> p k t", k=4)
                             ).then_inc(sig["x_taken"], 1)




def three_passes(pe, out, wH, wL, hH, hL, first, last):
    pe.matmul(out, wH, hH, start=first, stop=False)
    pe.matmul(out, wH, hL, start=False, stop=False)
    return pe.matmul(out, wL, hH, start=False, stop=last)


def rows_of(w, one, k, cols):
    return w[one, k * P:(k + 1) * P, cols].rearrange("o p n -> (o p) n")


class Slabs:

    def __init__(self, sig, raw, high, low):
        self.sig, self.raw, self.highs, self.lows = sig, raw, high, low
        self.slots = raw.shape[1]

    def all_free(self, pe):
        for s in range(self.slots):
            pe.sem_inc(self.sig[f"slot{s}_used"], 1)

    def all_split(self, dve):
        for s in range(self.slots):
            dve.sem_inc(self.sig[f"slot{s}_split"], 1)

    def load(self, sp, s, n, src, width=512):
        sp.wait_ge(self.sig[f"slot{s}_split"], n + 1)
        dst = self.raw[:, s, 0:width]
        if len(src.shape) == 3:
            dst = dst.rearrange("p (g n) -> p g n", g=src.shape[1])
        sp.dma_start(dst, src).then_inc(self.sig[f"slot{s}_loaded"], 16)

    def high(self, act, s, n, width=512):
        act.wait_ge(self.sig[f"slot{s}_loaded"], 16 * n + 16)
        act.wait_ge(self.sig[f"slot{s}_used"], n + 1)
        act.copy(self.highs[:, s, 0:width], self.raw[:, s, 0:width]).then_inc(self.sig[f"slot{s}_high"], 1)

    def low(self, dve, s, n, width=512):
        dve.wait_ge(self.sig[f"slot{s}_high"], n + 1)
        dve.tensor_tensor(self.lows[:, s, 0:width], self.raw[:, s, 0:width],
                          self.highs[:, s, 0:width].bitcast(F32), ALU.subtract
                          ).then_inc(self.sig[f"slot{s}_split"], 1)

    def wait(self, pe, s, n):
        pe.wait_ge(self.sig[f"slot{s}_split"], n + 2)

    def used(self, s):
        return self.sig[f"slot{s}_used"]


HALF_OF = (slice(0, HALF), slice(HALF, TOK))


def norm_square(act, m, sig, k, sq):
    act.activation(sq, m.x[:, k], ACT.Square).then_inc(sig["squares"], 1)


def norm_sum(dve, m, sig, k, total, sq):
    dve.wait_ge(sig["squares"], k + 1)
    if k > 1:
        dve.wait_ge(sig["square_sum"], k - 1)
    dve.tensor_tensor(total, total, sq, ALU.add).then_inc(sig["square_sum"], 1)


def norm_total(pe, m, sig, total):
    pe.wait_ge(sig["square_sum"], KT - 1)
    for half in range(2):
        pe.matmul(m.bank[half][:, 0:HALF], m.c("ones"), total[:, HALF_OF[half]], start=True, stop=True
                  ).then_inc(sig["total"], 1)


def norm_rstd(act, m, sig, rstd):
    for half in range(2):
        act.wait_ge(sig["total"], half + 1)
        act.activation(rstd[:, HALF_OF[half]], m.bank[half][:, 0:HALF], ACT.Ln, scale=1.0 / D, bias=EPS
                       ).then_inc(sig["rstd_ln"], 1)
    act.wait_ge(sig["rstd_ln"], 2)
    act.activation(rstd, rstd, ACT.Exp, scale=-0.5).then_inc(sig["rstd"], 1)


class Moving:

    def __init__(self, sig, made, high, low):
        self.sig, self.made, self.highs, self.lows = sig, made, high, low

    def high(self, act, k, wait=True):
        if wait:
            act.wait_ge(self.sig["h_made"], k + 1)
        act.copy(self.highs[:, k], self.made[:, k]).then_inc(self.sig["h_high"], 1)

    def low(self, dve, k, base=0):
        dve.wait_ge(self.sig["h_high"], base + k + 1)
        dve.tensor_tensor(self.lows[:, k], self.made[:, k], self.highs[:, k].bitcast(F32), ALU.subtract
                          ).then_inc(self.sig["h_split"], 1)


def norm_apply(dve, m, sig, h, w, rstd, base=0):
    dve.wait_ge(sig["rstd"], 1)
    for k in range(KT + 1):
        if k < KT:
            dve.scalar_tensor_tensor(out=h.made[:, k], in0=m.x[:, k], scalar=w[:, k:k + 1], in1=rstd,
                                     op0=ALU.mult, op1=ALU.mult).then_inc(sig["h_made"], 1)
        if k > 0:
            h.low(dve, k - 1, base)


def feature_group(pe, m, sig, slabs, h, n, g, h_base=None):
    for k in range(KT):
        slabs.wait(pe, k, n)
        if h_base is not None:
            pe.wait_ge(sig["h_split"], h_base + k + 1)
        for b in range(8):
            t, half = b // 2, b % 2
            if k == 0:
                pe.wait_ge(sig["first_banks_read" if b < 4 else "last_banks_read"], 4 * g + b % 4 + 1)
            tile = slice(t * P, (t + 1) * P)
            mm = three_passes(pe, m.bank[b][:, 0:HALF], slabs.highs[:, k, tile], slabs.lows[:, k, tile],
                              h.highs[:, k, HALF_OF[half]], h.lows[:, k, HALF_OF[half]], k == 0, k == KT - 1)
            if k == KT - 1:
                mm.then_inc(sig["bank_done"], 1)
            elif b == 7:
                mm.then_inc(slabs.used(k), 1)
    pe.wait_ge(sig["bank_done"], 8 * g + 8)
    pe.sem_inc(slabs.used(KT - 1), 1)


def input_phase(nc, m, d, l):
    one = bass.ds(l, 1)
    keep, m.top = m.top, m.hT_at
    wrows = m.take(P)
    acc = [m.take(SEQ) for _ in range(2)]
    last = m.last = m.take(GT, 27)
    bufs = m.take(GT * P)
    sacc, stmp = m.take(GT, NSEQ, DSEQ), m.take(GT, NSEQ, DSEQ)
    rstd = m.take(TOK)
    assert m.top <= m.hT_at + KT * TOK
    m.top = keep
    sq = [m.mlF[:, k] for k in range(4)] + [m.hgF[:, k] for k in range(4)]
    made = m.view(m.tokp_at, KT, TOK)
    rows = layer_rows(m)
    taps = m.colw[:, 0:48].rearrange("p (j t) -> p j t", j=CONV)
    OLD = NSEQ * (CONV - 1)
    NF = 5
    FLAT = ((1, GD_G, 520), (0, ML_VO, 520), (2, HG_IG, 512))
    widths = [512] * NF + [w for _, _, w in FLAT]
    PER = GT // 2
    parts = ExitStack()
    with parts, phase(nc) as (sig, block):
        def tensor(shape, dtype):
            return parts.enter_context(m.tensor(shape, dtype))

        slabs = Slabs(sig, tensor([KT, GROUP], F32), tensor([KT, GROUP], F32R), tensor([KT, GROUP], F32R))
        h = Moving(sig, made, tensor([KT, TOK], F32R), tensor([KT, TOK], F32R))

        @block.sync
        def _(sp):
            sp.dma_start(wrows[0:48, :], d["gd_conv_w"][one].rearrange("o j (t p) -> (o j t) p", p=P)
                         ).then_inc(sig["rows_loaded"], 16)
            for at, name in ((48, "norm1_w"), (56, "norm2_w")):
                sp.dma_start(wrows[at:at + KT, :], d[name][one].rearrange("o (k p) -> (o k) p", p=P)
                             ).then_inc(sig["rows_loaded"], 16)
            sp.dma_start(bufs[0:OLD, :], d["state_gdn_conv"][one].rearrange("o b j n -> (o b j) n")
                         ).then_inc(sig["stored_rows_loaded"], 16)
            w = d["w_in"]
            with sp.Fori(0, 3) as j:
                for k in range(KT):
                    slabs.load(sp, k, j, rows_of(w, one, k, bass.ds(j * 512 + GD_QKV, 512)))
            for key, name, n in (("ibias", "ml_i_bias", 4), ("fbias", "ml_f_bias", 4), ("negA", "gd_A_log", 4),
                                 ("dtb", "gd_dt_bias", 4), ("mlw", "ml_norm_w", 64), ("hgw", "hg_norm_w", 64),
                                 ("gdw", "gd_norm_w", 128)):
                sp.dma_start(rows[key], bc(d[name][one, :], P, n)).then_inc(sig["small_loaded"], 16)
            for n, c0 in enumerate((ML_QK, HG_QF) + tuple(c0 for _, c0, _ in FLAT)):
                for k in range(KT):
                    width = widths[3 + n]
                    slabs.load(sp, k, 3 + n, rows_of(w, one, k, slice(c0, c0 + width)), width)
            sp.wait_ge(sig["small_loaded"], 7 * 16)

        @block.tensor
        def _(pe):
            slabs.all_free(pe)
            pe.wait_ge(sig["rows_loaded"], 48)
            pe.transpose(m.bank[7][:, 0:64], wrows[0:64, :], m.c("ident", 64)[:, 0:64]).then_inc(sig["rows_turned"], 1)
            pe.wait_ge(sig["stored_rows_loaded"], 16)
            for t in range(GT):
                mm = pe.transpose(m.bank[6][:, t * OLD:(t + 1) * OLD], bufs[0:OLD, t * P:(t + 1) * P],
                                  m.c("ident", OLD)[:, 0:OLD])
            mm.then_inc(sig["stored_rows_turned"], 1)
            norm_total(pe, m, sig, sq[0])
            pe.wait_ge(sig["rstd_ln"], 2)
            feature_group(pe, m, sig, slabs, h, 0, 0, h_base=0)
            with pe.Fori(1, 3) as j:
                feature_group(pe, m, sig, slabs, h, j, j)
            for g in range(3, NF):
                feature_group(pe, m, sig, slabs, h, g, g)
            u = 4 * NF
            for n, (place, c0, width) in enumerate(FLAT):
                w2 = width // 2
                for i in range(NT):
                    n_tok, tokens = tile_rows(i), slice(i * P, i * P + tile_rows(i))
                    pe.wait_ge(sig["first_banks_read" if u % 4 < 2 else "last_banks_read"],
                               2 * (u // 4 * 2 + u % 2) + 2)
                    for k in range(KT):
                        if i == 0:
                            slabs.wait(pe, k, NF + n)
                        for half in range(2):
                            cols = slice(half * w2, (half + 1) * w2)
                            mm = three_passes(pe, m.bank[2 * (u % 4) + half][0:n_tok, 0:w2],
                                              h.highs[:, k, tokens], h.lows[:, k, tokens],
                                              slabs.highs[:, k, cols], slabs.lows[:, k, cols],
                                              k == 0, k == KT - 1)
                            if k == KT - 1:
                                mm.then_inc(sig["bank_done"], 1)
                            elif i == NT - 1 and half == 1:
                                mm.then_inc(slabs.used(k), 1)
                    u += 1
                pe.wait_ge(sig["bank_done"], 2 * u)
                pe.sem_inc(slabs.used(KT - 1), 1)

        def evacuate(eng, copy, mine):
            read = sig[("first_banks_read", "last_banks_read")[mine]]

            def features(g, prompt, sample):
                for t in (2 * mine, 2 * mine + 1):
                    eng.wait_ge(sig["bank_done"], 8 * g + 2 * t + 1)
                    copy(prompt(t)[:, 0:HALF], m.bank[2 * t][:, 0:HALF]).then_inc(read, 1)
                    eng.wait_ge(sig["bank_done"], 8 * g + 2 * t + 2)
                    copy(prompt(t)[:, HALF:SEQ], m.bank[2 * t + 1][:, 0:SEQ - HALF])
                    copy(sample(t), m.bank[2 * t + 1][:, SEQ - HALF:HALF]).then_inc(read, 1)

            def conv(g):
                features(g, lambda t: m.gdF[:, bass.ds(4 * g + t, 1), CONV - 1:].rearrange("p a n -> p (a n)"),
                         lambda t: m.gdS[:, bass.ds(4 * g + t, 1), :, CONV - 1:].rearrange("p a b n -> p (a b) n"))

            def plain(g, to):
                features(g, lambda t: to[:, t, 0:SEQ], lambda t: to[:, t, SEQ:])

            def unit(u, i, place, w2):
                if (u % 4) // 2 != mine:
                    return
                n = tile_rows(i)
                for half in range(2):
                    eng.wait_ge(sig["bank_done"], 2 * u + half + 1)
                    copy(m.tokp[0:n, i, place, half * w2:(half + 1) * w2], m.bank[2 * (u % 4) + half][0:n, 0:w2]
                         ).then_inc(read, 1)

            return conv, plain, unit

        def stream(eng, split, copy, mine, convolve):
            conv, plain, unit = evacuate(eng, copy, mine)

            def step(g, evac):
                for k in range(6):
                    split(k, g + 1, widths[g + 1] if isinstance(g, int) else 512)
                    if isinstance(g, int) and g >= 3:
                        convolve((g - 3) * PER + k)
                evac(g)
                for k in (6, 7):
                    split(k, g + 1, widths[g + 1] if isinstance(g, int) else 512)

            def deltanet():
                with eng.Fori(0, 2) as g:
                    step(g, conv)
                step(2, conv)

            def others():
                step(3, lambda g: plain(g, m.mlF))
                step(4, lambda g: plain(g, m.hgF))
                u = 4 * NF
                for n, (place, c0, width) in enumerate(FLAT):
                    for i in range(NT):
                        if i == NT - 1 and n + 1 < len(FLAT):
                            for k in range(7):
                                split(k, NF + n + 1, widths[NF + n + 1])
                        unit(u, i, place, width // 2)
                        u += 1
                    if n + 1 < len(FLAT):
                        split(7, NF + n + 1, widths[NF + n + 1])

            return deltanet, others

        @block.scalar
        def _(act):
            def convolve(t):
                b = t % 2
                act.wait_ge(sig[f"conv{b}"], t // 2 * 4 + 4)
                act.activation(m.gdF[:, t, CONV - 1:], acc[b], ACT.Silu).then_inc(sig[f"conv{b}_stored"], 1)

            act.sem_inc(sig["first_banks_read"], 4)
            for k in range(KT):
                norm_square(act, m, sig, k, sq[k])
            for k in range(KT):
                slabs.high(act, k, 0)
            norm_rstd(act, m, sig, rstd)
            for k in range(KT):
                h.high(act, k)
            deltanet, others = stream(act, lambda k, n, width: slabs.high(act, k, n, width), act.copy, 0, convolve)
            deltanet()
            act.wait_ge(sig["last_taken"], 2)
            others()
            act.wait_ge(sig["tap_added"], CONV - 1)
            act.activation(m.gdC.rearrange("p t n -> p (t n)"), sacc.rearrange("p t b n -> p (t b n)"), ACT.Silu)

        @block.vector
        def _(dve):
            def copy(o, i):
                if len(o.shape) == 3:
                    i = i.rearrange("p (b n) -> p b n", b=NSEQ)
                return dve.tensor_copy(o, i)

            def convolve(t):
                b = t % 2
                if t >= 2:
                    dve.wait_ge(sig[f"conv{b}_stored"], t // 2)
                for tap in range(CONV):
                    src, w = m.gdF[:, t, tap:tap + SEQ], taps[:, tap, t:t + 1]
                    if tap == 0:
                        dve.tensor_scalar(acc[b], src, w, None, ALU.mult).then_inc(sig[f"conv{b}"], 1)
                    else:
                        dve.wait_ge(sig[f"conv{b}"], t // 2 * 4 + tap)
                        dve.scalar_tensor_tensor(out=acc[b], in0=src, scalar=w, in1=acc[b],
                                                 op0=ALU.mult, op1=ALU.add).then_inc(sig[f"conv{b}"], 1)

            slabs.all_split(dve)
            dve.wait_ge(sig["rows_turned"], 1)
            dve.tensor_copy(m.colw, m.bank[7][:, 0:64]).then_inc(sig["colw_ready"], 1)
            dve.wait_ge(sig["stored_rows_turned"], 1)
            dve.tensor_copy(m.gdS[:, :, :, 0:CONV - 1],
                            m.bank[6][:, 0:GT * OLD].rearrange("p (t b j) -> p t b j", t=GT, b=NSEQ)
                            ).then_inc(sig["rows_placed"], 1)
            dve.wait_ge(sig["rows_placed"], 1)
            dve.sem_inc(sig["last_banks_read"], 4)
            for k in range(1, KT):
                norm_sum(dve, m, sig, k, sq[0], sq[k])
            for k in range(KT):
                slabs.low(dve, k, 0)
            dve.wait_ge(sig["colw_ready"], 1)
            norm_apply(dve, m, sig, h, m.colw[:, 48:56], rstd)
            deltanet, others = stream(dve, lambda k, n, width: slabs.low(dve, k, n, width), copy, 1, convolve)
            deltanet()
            dve.wait_ge(sig["first_banks_read"], 16)
            dve.wait_ge(sig["last_banks_read"], 16)
            dve.wait_ge(sig["window_empty"], 1)
            others()

        @block.gpsimd
        def _(pool):
            pool.memset(m.gdF[:, :, 0:CONV - 1], 0.0).then_inc(sig["window_empty"], 1)
            pool.wait_ge(sig["first_banks_read"], 16)
            pool.wait_ge(sig["last_banks_read"], 16)
            pool.tensor_copy(last[:, :, 0:3], m.gdF[:, :, SEQ:SEQ + 3]).then_inc(sig["last_taken"], 1)
            for t in range(GT):
                cp = pool.tensor_copy(last[:, t, 3:27].rearrange("p (b j) -> p b j", b=NSEQ), m.gdS[:, t, :, DSEQ:])
            cp.then_inc(sig["last_taken"], 1)
            pool.wait_ge(sig["rows_placed"], 1)
            for j in range(CONV):
                wj = bc(taps[:, j, :].unsqueeze(2).unsqueeze(3), P, GT, NSEQ, DSEQ)
                dst = sacc if j == 0 else stmp
                if j > 1:
                    pool.wait_ge(sig["tap_added"], j - 1)
                pool.tensor_tensor(dst, m.gdS[:, :, :, j:j + DSEQ], wj, ALU.mult).then_inc(sig["tap_scaled"], 1)
                if j > 0:
                    pool.wait_ge(sig["tap_scaled"], j + 1)
                    if j > 1:
                        pool.wait_ge(sig["tap_added"], j - 1)
                    pool.tensor_tensor(sacc, sacc, stmp, ALU.add).then_inc(sig["tap_added"], 1)


def prep_phase(nc, m, d, l):
    one = bass.ds(l, 1)
    last = m.last
    m.top = m.arena + 6 * H * P
    fy, ab = m.take(NT, 8), m.take(NT, 8)
    pos = m.take(NT, 4)
    lastT = m.take(GT * P)
    rows = layer_rows(m)
    with phase(nc) as (sig, block):
        @block.sync
        def _(sp):
            sp.wait_ge(sig["last_ready"], 3)
            sp.dma_start(d["p_conv"][one].rearrange("o b j n -> (o b j) n"), lastT[0:3, :]
                         ).then_inc(sig["last_stored"], 16)
            sp.dma_start(d["s_conv"][one].rearrange("o b j n -> (o b j) n"), lastT[3:27, :]
                         ).then_inc(sig["last_stored"], 16)
            sp.wait_ge(sig["last_stored"], 32)

        @block.tensor
        def _(pe):
            for t in range(GT):
                mm = pe.transpose(m.bank[1 + t // 4][0:27, (t % 4) * P:(t % 4 + 1) * P], last[:, t, :], m.c("ident"))
                if t % 4 == 3:
                    mm.then_inc(sig["last_turned"], 1)

        @block.gpsimd
        def _(pool):
            pool.tensor_copy(m.lbl, m.lb[:, bass.ds(l * 2, 2)])
            for s in (m.S_gd, m.C_ml, m.S_hg, m.m_ml):
                pool.memset(s, 0.0)
            pool.memset(m.view(m.arena, 6 * H * P), 0.0)
            pool.wait_ge(sig["gates_silu"], 2)
            for i in range(NT):
                g = m.tokp[:, i, 2, OG2:OG2 + H * DKH].rearrange("p (h n) -> p h n", h=H)
                pool.tensor_tensor(g, g, bc(rows["hgw"].unsqueeze(1), P, H, DKH), ALU.mult)

        @block.vector
        def _(dve):
            t0 = m.tokp
            dve.tensor_tensor(m.gates[:, :, LI:LI + 4], t0[:, :, 0, I0:I0 + 4],
                              bc(rows["ibias"].unsqueeze(1), P, NT, 4), ALU.add)
            dve.tensor_tensor(fy[:, :, 0:4], t0[:, :, 0, F0:F0 + 4], bc(rows["fbias"].unsqueeze(1), P, NT, 4),
                              ALU.add).then_inc(sig["fy_ready"], 1)
            dve.tensor_tensor(fy[:, :, 4:8], t0[:, :, 1, A1:A1 + 4], bc(rows["dtb"].unsqueeze(1), P, NT, 4),
                              ALU.add).then_inc(sig["fy_ready"], 1)
            dve.wait_ge(sig["fy_ready"], 2)
            dve.scalar_tensor_tensor(out=ab, in0=fy, scalar=-1.0, in1=fy, op0=ALU.mult, op1=ALU.max
                                     ).then_inc(sig["fy_abs"], 1)
            dve.tensor_scalar(m.gates[:, :, LF:LF + 4], fy[:, :, 0:4], 0.0, None, ALU.min).then_inc(sig["fy_clipped"], 1)
            dve.tensor_scalar(pos, fy[:, :, 4:8], 0.0, None, ALU.max).then_inc(sig["fy_clipped"], 1)
            for g in range(3):
                dve.wait_ge(sig["last_turned"], g + 1)
                dve.tensor_copy(lastT[0:27, g * 512:(g + 1) * 512], m.bank[1 + g][0:27, :]
                                ).then_inc(sig["last_ready"], 1)
            for i in range(NT):
                dve.wait_ge(sig["gates_silu"], 1)
                g = m.tokp[:, i, 1, 0:H * DKG].rearrange("p (h n) -> p h n", h=H)
                dve.tensor_tensor(g, g, bc(rows["gdw"].unsqueeze(1), P, H, DKG), ALU.mult)
            dve.wait_ge(sig["decay_rates"], 1)
            dve.tensor_scalar(rows["negA"], rows["negA"], -1.0, None, ALU.mult).then_inc(sig["rates_negated"], 1)
            dve.wait_ge(sig["fy_ln"], 2)
            dve.wait_ge(sig["fy_clipped"], 2)
            dve.tensor_tensor(m.gates[:, :, LF:LF + 4], m.gates[:, :, LF:LF + 4], ab[:, :, 0:4], ALU.subtract)
            dve.tensor_tensor(pos, pos, ab[:, :, 4:8], ALU.add).then_inc(sig["softplus"], 1)
            dve.wait_ge(sig["softplus"], 1)
            dve.wait_ge(sig["rates_negated"], 1)
            dve.tensor_tensor(m.gates[:, :, GG:GG + 4], pos, bc(rows["negA"].unsqueeze(1), P, NT, 4), ALU.mult)

        @block.scalar
        def _(act):
            g1 = m.tokp[:, :, 1, 0:H * DKG]
            g2 = m.tokp[:, :, 2, OG2:OG2 + H * DKH]
            act.activation(g1, g1, ACT.Silu).then_inc(sig["gates_silu"], 1)
            act.activation(g2, g2, ACT.Silu).then_inc(sig["gates_silu"], 1)
            q = m.hgF[:, 0:2, :]
            act.activation(q, q, ACT.Silu)
            z = m.hgF[:, 2:4, :]
            act.activation(z, z, ACT.Sigmoid)
            o = m.tokp[:, :, 0, O0:O0 + H * DKM]
            act.activation(o, o, ACT.Sigmoid)
            act.activation(m.gates[:, :, BETA:BETA + 4], m.tokp[:, :, 1, B1:B1 + 4], ACT.Sigmoid)
            nc.scalar.preload_act_table_set(EXP_LN)
            act.activation(rows["negA"], rows["negA"], ACT.Exp).then_inc(sig["decay_rates"], 1)
            act.wait_ge(sig["fy_abs"], 1)
            act.activation(ab, ab, ACT.Exp, scale=-1.0).then_inc(sig["fy_ln"], 1)
            act.wait_ge(sig["fy_ln"], 1)
            act.activation(ab, ab, ACT.Ln, bias=1.0).then_inc(sig["fy_ln"], 1)


def states_phase(nc, m, d, l):
    one = bass.ds(l, 1)
    m.top = m.gdF_at
    st = {"S_gd": m.take(H, NSEQ, DKG), "C_ml": m.take(2, NSEQ, DKM + 1), "S_hg": m.take(2, NSEQ, DKH),
          "m_ml": m.take(H, NSEQ)}
    assert m.top <= m.gdC_at
    prompt = {"S_gd": m.S_gd, "C_ml": m.C_ml, "S_hg": m.S_hg}
    with phase(nc) as (sig, block):
        @block.gpsimd
        def _(pool):
            pool.memset(m.view(m.arena, 6 * H * SAMP), 0.0)

        @block.scalar
        def _(act):
            for h in range(H):
                half, pair = slice(64 * (h % 2), 64 * (h % 2) + 64), h // 2
                act.dma_start(st["S_gd"][:, h], d["state_gdn_S"][one, :, h].rearrange("o b k v -> k (o b) v")
                              ).then_inc(sig["state_loaded"], 16)
                act.dma_start(st["C_ml"][half, pair, :, 0:DKM],
                              d["state_mlstm_C"][one, :, h].rearrange("o b k v -> k (o b) v")
                              ).then_inc(sig["state_loaded"], 16)
            act.wait_ge(sig["state_loaded"], 16 * 2 * H)

        @block.sync
        def _(sp):
            for h in range(H):
                half, pair = slice(64 * (h % 2), 64 * (h % 2) + 64), h // 2
                sp.dma_start(st["C_ml"][half, pair, :, DKM:],
                             d["state_mlstm_n"][one, :, h].rearrange("o b (k x) -> k (o b) x", x=1)
                             ).then_inc(sig["rest_loaded"], 16)
                sp.dma_start(st["S_hg"][half, pair], d["state_hgrn_S"][one, :, h].rearrange("o b k v -> k (o b) v")
                             ).then_inc(sig["rest_loaded"], 16)
                sp.dma_start(st["m_ml"][:, h, :], bc(d["state_mlstm_m"][one, :, h], P, NSEQ)
                             ).then_inc(sig["rest_loaded"], 16)
            store_states(sp, m, d, l, prompt, "p", slice(P - 1, P), sig)
            sp.wait_ge(sig["rest_loaded"], 16 * 3 * H)
            sp.wait_ge(sig["state_stored"], STORES)
    return st


STORES = 16 * (4 * H + 1)


def store_states(sp, m, d, l, st, who, rows, sig):
    one = bass.ds(l, 1)
    for h in range(H):
        half, pair = slice(64 * (h % 2), 64 * (h % 2) + 64), h // 2
        sp.dma_start(d[who + "_S"][one, :, h].rearrange("o b k v -> k (o b) v"), st["S_gd"][:, h]
                     ).then_inc(sig["state_stored"], 16)
        sp.dma_start(d[who + "_C"][one, :, h].rearrange("o b k v -> k (o b) v"),
                     st["C_ml"][half, pair, :, 0:DKM]).then_inc(sig["state_stored"], 16)
        sp.dma_start(d[who + "_n"][one, :, h].rearrange("o b (k x) -> k (o b) x", x=1),
                     st["C_ml"][half, pair, :, DKM:]).then_inc(sig["state_stored"], 16)
        sp.dma_start(d[who + "_H"][one, :, h].rearrange("o b k v -> k (o b) v"), st["S_hg"][half, pair]
                     ).then_inc(sig["state_stored"], 16)
    sp.dma_start(d[who + "_m"][one].rearrange("o b h -> (o b) h"), m.mcol[rows, :]
                 ).then_inc(sig["state_stored"], 16)


HALVES = tuple((odd, slice(64 * odd, 64 * odd + 64)) for odd in range(2))


def chunk_phase(nc, m, st, nseq, c):
    sample = c is None
    L = DSEQ if sample else P
    T = nseq * L
    nl = 2 if sample else LEVELS
    W = H * T
    tile = NT - 1 if sample else None
    upto = m.c("upto_s" if sample else "upto", T)[:, 0:T]
    same = m.c("same_s" if sample else "ones", T)[:, 0:T]
    endsel = m.c("end_s" if sample else "end", T)[:, 0:T]
    ident = m.c("ident", T)[:, 0:T]
    ones = m.c("ones")
    rows = layer_rows(m)

    def low(lv):
        return m.c(f"low{lv}", T)[:, 0:T]

    def up(lv):
        return m.c(f"up{lv}", T)[:, 0:T]

    def heads(ap, n=None):
        return ap.rearrange("p (h n) -> p h n", h=H)

    def over_heads(mask):
        return bc(mask.unsqueeze(1), mask.shape[0], H, mask.shape[1])

    def per_head(col, n):
        return bc(col.unsqueeze(2), col.shape[0], H, n)

    m.top = m.arena
    padded = m.take(6, H, T)
    mq, mqw, hq, hqe = (padded[:, i] for i in range(4))
    lq = [padded[:, 4], padded[:, 5]]
    t4 = lambda: m.take(H, T)
    tv = lambda: m.take(H, DKG)
    kn, qn, EA, EB, X, Y, kd, qd, edb = (t4() for _ in range(9))
    A = EA
    at = m.top
    AM = [t4(), t4()]
    first = m.top
    m.take(5, H * DKG)
    spot = lambda i, n: m.view(first + i * H * DKG, H, n)
    sqk, r = spot(0, T), spot(0, DKG)
    sqq, u = spot(1, T), spot(1, DKG)
    p1 = spot(2, T)
    ug, og = spot(3, T), m.view(first + 3 * H * DKG, H * DKG)
    Dg, kdec = spot(4, T), spot(4, DKG)
    vS = t4()
    gates = m.take(16)
    dcol, ddc, kfac, msg, nbeta = m.take(12), m.take(4), m.take(4), m.take(4), m.take(4)
    hk, bH, hlf, hkd, mk = (m.take(2, T) for _ in range(5))
    hkdT, mks = (m.take(2 * P), m.take(2 * P)) if sample else \
        (a.rearrange("p x t -> p (x t)") for a in (hkd, mk))
    lev = m.take(nl, 2, T)
    lk = [m.take(2, T) for _ in range(2)]
    hacc, htmp = t4(), [t4(), t4()]
    hms, hog = m.take(4), m.take(H * DKH)
    vext = m.take(H, DKM + 1)
    ua, ma, M, mW = t4(), t4(), t4(), t4()
    wexp = t4()
    bcol, acol, gend, emt, den, mms, kw = (m.take(12 if i == 0 else 4) for i in range(7))
    mog = m.take(H * DKM)
    m_sq = m.take(H * DKM) if sample else hlf.rearrange("p x t -> p (x t)")
    lbm, lbn = m.take(2), m.take(2)
    mix = m.take(MIX) if sample else m.view(at, MIX)
    if sample:
        kx, qx = m.take(H, nseq, T), m.take(H, nseq, T)
        hqx, mqx = m.take(H, nseq, T), m.take(H, nseq, T)
        ux = [m.view(m.tokp_at + i * nseq * DKG, nseq, DKG) for i in range(2)]
        hx = m.view(m.tokp_at + 2 * nseq * DKG, H, nseq, DKH)
        vx = m.view(m.tokp_at + 2 * nseq * DKG + H * nseq * DKH, H, nseq, DKM + 1)
        seqcol = m.c("seq_of_column").rearrange("p (b t) -> p b t", b=nseq)
        seqrow = m.c("seq_of_row", T)
    else:
        kx, qx, hqx, mqx = kd, qd, hqe, mqw
    M0, M1, H0, H1, G0, G1, G2, G3 = m.bank

    if sample:
        gt = lambda a, z: m.gdC[:, a:z, :]
        mlF, hgF = (lambda a, z: m.mlF[:, a:z, SEQ:]), (lambda a, z: m.hgF[:, a:z, SEQ:])
        tk = lambda g, a, z: m.tokp[0:T, tile, g, a:z]
        gates_src = m.gates[0:T, tile, :]
        hTc = m.hT[:, :, SEQ:]
    else:
        gt = lambda a, z: m.gdF[:, a:z, bass.ds(c * P + (CONV - 1), P)]
        mlF = lambda a, z: m.mlF[:, a:z, bass.ds(c * P, P)]
        hgF = lambda a, z: m.hgF[:, a:z, bass.ds(c * P, P)]
        tk = lambda g, a, z: m.tokp[:, bass.ds(c, 1), g, a:z].rearrange("p o n -> p (o n)")
        gates_src = m.gates[:, bass.ds(c, 1), :].rearrange("p o n -> p (o n)")
        hTc = m.hT[:, :, bass.ds(c * P, P)]
    li, lf, gg, beta = (gates[0:T, a:a + 4] for a in (LI, LF, GG, BETA))
    pair_of = lambda h: (slice(64 * (h % 2), 64 * (h % 2) + 64), h // 2)

    def flat(ap):
        return ap.rearrange("p h t -> p (h t)")

    def seqs(ap):
        return ap.rearrange("p x (b j) -> p x b j", b=nseq)

    with phase(nc) as (sig, block):
        @block.scalar
        def _(act):
            def rstd(ms, n, ready, name):
                act.wait_ge(sig[ready], H)
                act.activation(ms, ms, ACT.Ln, scale=1.0 / n, bias=EPS).then_inc(sig[name], 1)
                act.wait_ge(sig[name], 1)
                act.activation(ms, ms, ACT.Exp, scale=-0.5).then_inc(sig[name], 1)

            def head_squares(sq, src, ms, name):
                for h in range(H):
                    act.activation(sq[:, h], src[:, h], ACT.Square, accum_out=ms[:, h:h + 1]
                                   ).then_inc(sig[name + "_ms"], 1)

            def norm(i):
                b, sq = ((G0, sqk), (G1, sqq))[i]
                act.wait_ge(sig["norm_sums"], i + 1)
                act.activation(flat(sq), b[:, 0:W], ACT.Ln, bias=EPS).then_inc(sig["norm_ln"], 1)
                act.wait_ge(sig["norm_ln"], i + 1)
                act.activation(flat(sq), flat(sq), ACT.Exp, scale=-0.5).then_inc(sig["norm_ready"], 1)

            act.copy(gates[0:T, :], gates_src).then_inc(sig["gates_taken"], 1)
            act.activation(sqk, gt(4, 8), ACT.Square).then_inc(sig["squares"], 1)
            act.activation(sqq, gt(0, 4), ACT.Square).then_inc(sig["squares"], 1)
            act.wait_ge(sig["f_ready"], 1)
            act.activation(hlf, hlf, ACT.Ln).then_inc(sig["logf"], 1)
            norm(0)
            norm(1)
            act.wait_ge(sig["gd_Dmax"], 1)
            act.activation(EA[0:T], EA[0:T], ACT.Exp, scale=-1.0).then_inc(sig["gd_EA"], 1)
            act.wait_ge(sig["gd_Dmin"], 1)
            act.activation(EB[0:T], EB[0:T], ACT.Exp).then_inc(sig["gd_EB"], 1)
            act.activation(flat(edb), G2[:, 0:W], ACT.Exp).then_inc(sig["gd_edb"], 1)
            act.wait_ge(sig["gd_dd"], 1)
            act.activation(kfac[0:T], ddc[0:T], ACT.Exp).then_inc(sig["gd_kfac"], 1)
            for odd, half in HALVES:
                act.copy(hq[half, odd::2, :], hgF(0, 2)[half]).then_inc(sig["hg_q"], 1)
            act.wait_ge(sig["ml_arows"], 1)
            act.copy(flat(ma), M0[:, 0:W]).then_inc(sig["ml_a_taken"], 1)
            act.wait_ge(sig["gd_X0"], 1)
            act.copy(flat(X[0:T]), G2[0:T, 0:W]).then_inc(sig["X_ready"], 1)
            act.mul(mk, mlF(2, 4), DKM ** -0.5).then_inc(sig["ml_k"], 1)
            for odd, half in HALVES:
                act.copy(mq[half, odd::2, :], mlF(0, 2)[half]).then_inc(sig["ml_q"], 1)
            act.wait_ge(sig["lev"], 2 * nl)
            act.activation(lev, lev, ACT.Exp).then_inc(sig["lev_ready"], 1)

            def inverse(lv):
                if lv > 1:
                    act.wait_ge(sig["X_turned"], lv - 1)
                    act.copy(flat(Y[0:T]), G2[0:T, 0:W]).then_inc(sig["Y_taken"], 1)
                act.wait_ge(sig["inv_p1"], lv)
                act.copy(flat(p1[0:T]), G0[0:T, 0:W]).then_inc(sig["inv_p1_taken"], 1)

            def hg_decays():
                act.wait_ge(sig["hg_dl"], 1)
                act.activation(bH, bH, ACT.Exp).then_inc(sig["hg_eb"], 1)
                act.activation(hkd, hkd, ACT.Exp, scale=-1.0).then_inc(sig["hg_ekd"], 1)
                act.mul(vS, gt(8, 12), -1.0).then_inc(sig["v_taken"], 1)

            def decayed_keys():
                act.wait_ge(sig["k_turned"], 1)
                act.wait_ge(sig["gd_kfac"], 1)
                for h in range(H):
                    act.activation(kdec[0:T, h], G3[0:T, h * DKG:(h + 1) * DKG], ACT.Copy, scale=kfac[0:T, h:h + 1]
                                   ).then_inc(sig["gd_kdec"], 1)

            def ml_weights():
                act.wait_ge(sig["ml_D"], 2)
                act.activation(mW[0:T], mW[0:T], ACT.Exp, scale=-1.0).then_inc(sig["ml_E"], 1)
                act.wait_ge(sig["ml_wD"], 1)
                act.activation(wexp, wexp, ACT.Exp, scale=-1.0).then_inc(sig["ml_wexp"], 1)

            def ml_columns():
                act.wait_ge(sig["ml_kwD"], 1)
                act.activation(kw[0:T], kw[0:T], ACT.Exp).then_inc(sig["ml_kw"], 1)
                act.wait_ge(sig["ml_mt"], 1)
                act.activation(emt[0:T], m.mcol[0:T, :], ACT.Exp, scale=-1.0).then_inc(sig["ml_emt"], 1)
                act.wait_ge(sig["hg_k_turned"], 1)
                act.copy(hkdT[0:T, :], H1[0:T, 0:2 * P]).then_inc(sig["hg_kT"], 1)

            extras = {0: hg_decays, 1: decayed_keys, 2: ml_weights}
            if sample:
                decayed_keys()
                hg_decays()
                inverse(1)
                ml_weights()
            else:
                for lv in range(1, nl):
                    inverse(lv)
                    if lv - 1 in extras:
                        extras[lv - 1]()
            ml_columns()
            act.wait_ge(sig["gd_u"], 1)
            act.copy(flat(u[0:T]), G1[0:T, :]).then_inc(sig["u_ready"], 1)
            act.wait_ge(sig["ml_h"], H)
            head_squares(heads(m_sq[0:T, :]), heads(mog[0:T, :]), mms[0:T], "ml")
            rstd(mms[0:T], DKM, "ml_ms", "ml_rstd")
            act.wait_ge(sig["hg_o"], 1)
            head_squares(heads(hog[0:T, :]), heads(H0[0:T, 0:H * DKH]), hms[0:T], "hg")
            rstd(hms[0:T], DKH, "hg_ms", "hg_rstd")
            act.wait_ge(sig["gd_o"], 1)
            head_squares(heads(og[0:T, :]), heads(G2[0:T, :]), msg[0:T], "gd")
            rstd(msg[0:T], DKG, "gd_ms", "gd_rstd")
            act.wait_ge(sig["mix_turned"], 2)
            act.copy(hTc[:, 2:6, :], M1[:, 0:W].rearrange("p (k t) -> p k t", k=4))

        @block.gpsimd
        def _(pool):
            def mul(out, a, b):
                return pool.tensor_tensor(out, a, b, ALU.mult)

            def blocks(lv):
                pool.wait_ge(sig["gd_A"], 1)
                if lv > 2:
                    pool.wait_ge(sig["inv_p1"], lv - 2)
                mul(AM[lv % 2][0:T], A[0:T], over_heads(low(lv))).then_inc(sig["AM_ready"], 1)

            pool.wait_ge(sig["gates_taken"], 1)
            mul(ug[0:T], over_heads(upto), per_head(gg, T)).then_inc(sig["gd_ug"], 1)
            pool.wait_ge(sig["ml_acol"], 1)
            mul(ua[0:T], over_heads(ident), per_head(acol[0:T], T)).then_inc(sig["ml_ua_ready"], 1)
            pool.wait_ge(sig["gd_EA"], 1)
            mul(EA[0:T], EA[0:T], per_head(beta, T)).then_inc(sig["gd_EAb"], 1)
            pool.wait_ge(sig["gd_EB"], 1)
            mul(EB[0:T], EB[0:T], over_heads(upto)).then_inc(sig["gd_EBm"], 1)
            blocks(1)
            if nl > 2:
                blocks(2)
            pool.tensor_copy(vext[0:T, :, 0:DKM], heads(tk(0, V0, V0 + H * DKM))).then_inc(sig["ml_v"], 1)
            pool.memset(vext[0:T, :, DKM:], 1.0).then_inc(sig["ml_v"], 1)
            if sample:
                pool.wait_ge(sig["ml_v"], 2)
            pool.wait_ge(sig["gd_edb"], 1)
            pool.wait_ge(sig["gd_kn"], 1)
            mul(kd, kn, edb).then_inc(sig["gd_kd"], 1)
            pool.wait_ge(sig["gd_qn"], 1)
            mul(qd, qn, edb).then_inc(sig["gd_qd"], 1)
            if sample:
                pool.wait_ge(sig["gd_kd"], 1)
                pool.wait_ge(sig["gd_qd"], 1)
                for h in range(H):
                    mul(kx[:, h], bc(kd[:, h].unsqueeze(1), P, nseq, T), seqcol)
                    x = mul(qx[:, h], bc(qd[:, h].unsqueeze(1), P, nseq, T), seqcol)
                x.then_inc(sig["gd_x"], 1)
                pool.wait_ge(sig["gd_x"], 1)

            def ml_mask():
                pool.wait_ge(sig["ml_E"], 1)
                mul(mW[0:T], mW[0:T], over_heads(upto)).then_inc(sig["ml_W"], 1)

            for s in range(1, nl + 1):
                if 2 < s + 2 < nl:
                    blocks(s + 2)
                pool.wait_ge(sig["hg_masked"], s + 1)
                if s > 1:
                    pool.wait_ge(sig["hg_sum"], s - 1)
                pool.tensor_tensor(hacc[0:T], hacc[0:T], htmp[s % 2][0:T], ALU.add).then_inc(sig["hg_sum"], 1)
                if s == min(4, nl):
                    ml_mask()
            if sample:
                pool.wait_ge(sig["ml_W"], 1)
                pool.wait_ge(sig["hg_qe"], 2)
                pool.wait_ge(sig["ml_qw"], 2)
                for j in range(H):
                    mul(hqx[:, j], bc(hqe[:, j].unsqueeze(1), P, nseq, T), seqcol)
                    x = mul(mqx[:, j], bc(mqw[:, j].unsqueeze(1), P, nseq, T), seqcol)
                x.then_inc(sig["qx_ready"], 1)
                pool.wait_ge(sig["qx_ready"], 1)
                for h in range(H):
                    mul(hx[0:T, h], bc(tk(2, I2 + h * DKH, I2 + (h + 1) * DKH).unsqueeze(1), T, nseq, DKH),
                        bc(seqrow.unsqueeze(2), T, nseq, DKH))
                    x = mul(vx[0:T, h], bc(vext[0:T, h].unsqueeze(1), T, nseq, DKM + 1),
                            bc(seqrow.unsqueeze(2), T, nseq, DKM + 1))
                x.then_inc(sig["values_spread"], 1)

                def spread(h):
                    if h > 1:
                        pool.wait_ge(sig["gd_delta"], 2 * h - 2)
                    mul(ux[h % 2][0:T], bc(u[0:T, h].unsqueeze(1), T, nseq, DKG),
                        bc(seqrow.unsqueeze(2), T, nseq, DKG)).then_inc(sig["u_spread"], 1)

                pool.wait_ge(sig["u_ready"], 1)
                spread(0)
                spread(1)
                pool.wait_ge(sig["u_spread"], 2)
                pool.wait_ge(sig["gd_o"], 1)
                for h in range(H):
                    e = seqs(edb)[:, h, :, L - 1]
                    mul(st["S_gd"][:, h], st["S_gd"][:, h], bc(e.unsqueeze(2), P, nseq, DKG)
                        ).then_inc(sig["gd_decayed"], 1)
                pool.wait_ge(sig["gd_decayed"], H)
                spread(2)
                spread(3)

        @block.vector
        def _(dve):
            def tt(out, a, b, op):
                return dve.tensor_tensor(out, a, b, op)

            def mul(out, a, b):
                return dve.tensor_tensor(out, a, b, ALU.mult)

            dve.tensor_scalar(lbm, m.lbl, -1.0, 1.0, ALU.mult, ALU.add).then_inc(sig["lb_rest"], 1)
            dve.tensor_scalar(lbn, m.lbl, 1.0, None, ALU.subtract).then_inc(sig["lb_rest"], 1)
            dve.wait_ge(sig["lb_rest"], 2)
            for j in range(2):
                z = hgF(2 + j, 3 + j).rearrange("p a t -> p (a t)")
                dve.tensor_scalar(hlf[:, j], z, lbm[:, j:j + 1], m.lbl[:, j:j + 1], ALU.mult, ALU.add
                                  ).then_inc(sig["f_raw"], 1)
            dve.wait_ge(sig["f_raw"], 2)
            dve.tensor_scalar(hlf, hlf, TINY, None, ALU.max).then_inc(sig["f_ready"], 1)
            dve.wait_ge(sig["ml_bcols"], 1)
            dve.tensor_copy(bcol[0:T, 0:4], M1[0:T, 0:4]).then_inc(sig["ml_b"], 1)
            dve.tensor_copy(bcol[:, 8:12], M1[:, 8:12]).then_inc(sig["ml_b"], 1)
            dve.wait_ge(sig["ml_b"], 2)
            tt(acol[0:T], li, bcol[0:T, 0:4], ALU.subtract).then_inc(sig["ml_acol"], 1)
            dve.tensor_scalar(nbeta[0:T], beta, -1.0, None, ALU.mult).then_inc(sig["nbeta"], 1)
            dve.wait_ge(sig["gd_dcols"], 1)
            dve.tensor_copy(dcol[0:T, 0:8], G3[0:T, 0:8]).then_inc(sig["dcol_taken"], 1)
            for j in range(2):
                z = hgF(2 + j, 3 + j).rearrange("p a t -> p (a t)")
                dve.tensor_scalar(hk[:, j], z, lbn[:, j:j + 1], lbm[:, j:j + 1], ALU.mult, ALU.add
                                  ).then_inc(sig["hg_k"], 1)
            dve.wait_ge(sig["dcol_taken"], 1)
            tt(ddc[0:T], dcol[0:T, 4:8], dcol[0:T, 0:4], ALU.subtract).then_inc(sig["gd_dd"], 1)
            dve.wait_ge(sig["gd_drows"], 1)
            tt(Dg[0:T], G2[0:T, 0:W].rearrange("p (h t) -> p h t", h=H), per_head(dcol[0:T, 0:4], T), ALU.subtract
               ).then_inc(sig["gd_D"], 1)
            dve.wait_ge(sig["norm_ready"], 1)
            mul(kn, gt(4, 8), sqk).then_inc(sig["gd_kn"], 1)
            dve.wait_ge(sig["gd_D"], 1)
            dve.tensor_scalar(EA[0:T], Dg[0:T], 0.0, None, ALU.max).then_inc(sig["gd_Dmax"], 1)
            dve.tensor_scalar(EB[0:T], Dg[0:T], 0.0, None, ALU.min).then_inc(sig["gd_Dmin"], 1)
            dve.wait_ge(sig["logf"], 1)
            if sample:
                dve.tensor_copy(seqs(bH)[:, :, :, 0], seqs(hlf)[:, :, :, 0]).then_inc(sig["hg_b"], 1)
                for t in range(1, L):
                    dve.wait_ge(sig["hg_b"], t)
                    tt(seqs(bH)[:, :, :, t], seqs(bH)[:, :, :, t - 1], seqs(hlf)[:, :, :, t], ALU.add
                       ).then_inc(sig["hg_b"], 1)
            else:
                for j in range(2):
                    dve.tensor_tensor_scan(bH[:, j], ones[:, 0:T], hlf[:, j], 0.0, ALU.mult, ALU.add
                                           ).then_inc(sig["hg_b"], 1)
            dve.wait_ge(sig["norm_ready"], 2)
            dve.scalar_tensor_tensor(out=qn, in0=gt(0, 4), scalar=DKG ** -0.5, in1=sqq, op0=ALU.mult, op1=ALU.mult
                                     ).then_inc(sig["gd_qn"], 1)
            dve.wait_ge(sig["gd_kk"], 1)
            dve.wait_ge(sig["gd_EAb"], 1)
            mul(A[0:T], heads(G0[0:T, 0:W]), EA[0:T]).then_inc(sig["gd_A"], 1)
            dve.wait_ge(sig["gd_A"], 1)
            mul(Dg[0:T], A[0:T], over_heads(low(0))).then_inc(sig["gd_A0"], 1)
            dve.wait_ge(sig["gd_A0"], 1)
            tt(Y[0:T], over_heads(ident), Dg[0:T], ALU.subtract).then_inc(sig["Y_ready"], 1)
            dve.wait_ge(sig["hg_b"], L if sample else 2)
            for lv in range(nl):
                n = 1 << (lv + 1)
                v = bH.rearrange("p x (k n) -> p x k n", n=n)
                o = lev[:, lv].rearrange("p x (k n) -> p x k n", n=n)
                mid = bc(v[:, :, :, n // 2 - 1:n // 2], P, 2, T // n, n // 2)
                tt(o[:, :, :, 0:n // 2], mid, v[:, :, :, 0:n // 2], ALU.subtract).then_inc(sig["lev"], 1)
                tt(o[:, :, :, n // 2:], v[:, :, :, n // 2:], mid, ALU.subtract).then_inc(sig["lev"], 1)
            tt(seqs(hkd), seqs(bH), bc(seqs(bH)[:, :, :, L - 1:L], P, 2, nseq, L), ALU.subtract
               ).then_inc(sig["hg_dl"], 1)
            dve.wait_ge(sig["gd_kq"], 1)
            dve.wait_ge(sig["gd_EBm"], 1)
            mul(EB[0:T], heads(G1[0:T, 0:W]), EB[0:T]).then_inc(sig["gd_att"], 1)
            mp = st["m_ml"]

            def ml_maxima():
                dve.wait_ge(sig["ml_a_taken"], 1)
                if sample:
                    tt(seqs(M)[:, :, :, 0], seqs(ma)[:, :, :, 0], mp, ALU.max).then_inc(sig["ml_M"], 1)
                    for t in range(1, L):
                        dve.wait_ge(sig["ml_M"], t)
                        tt(seqs(M)[:, :, :, t], seqs(M)[:, :, :, t - 1], seqs(ma)[:, :, :, t], ALU.max
                           ).then_inc(sig["ml_M"], 1)
                else:
                    for h in range(H):
                        dve.tensor_tensor_scan(M[:, h], ma[:, h], ma[:, h], mp[:, h], ALU.max, ALU.max
                                               ).then_inc(sig["ml_M"], 1)
                dve.wait_ge(sig["ml_M"], 4)
                tt(mW[0:T], M[0:T], per_head(acol[0:T], T), ALU.subtract).then_inc(sig["ml_D"], 1)
                dve.wait_ge(sig["ml_D"], 1)
                dve.tensor_scalar(mW[0:T], mW[0:T], 0.0, None, ALU.max).then_inc(sig["ml_D"], 1)

            def ml_columns():
                tt(seqs(wexp), seqs(M), bc(mp.unsqueeze(3), P, H, nseq, L), ALU.subtract).then_inc(sig["ml_wD"], 1)
                last_M = M[:, :, T - 1]
                if sample:
                    mul(ma[0:T], M[0:T], over_heads(endsel)).then_inc(sig["ml_pick"], 1)
                    dve.wait_ge(sig["ml_pick"], 1)
                    dve.tensor_reduce(gend[0:T], ma[0:T], AX.X, ALU.add).then_inc(sig["ml_pick"], 1)
                    dve.wait_ge(sig["ml_pick"], 2)
                    last_M = gend[0:T]
                tt(kw[0:T], acol[0:T], last_M, ALU.subtract).then_inc(sig["ml_kwD"], 1)
                dve.wait_ge(sig["ml_Mcols"], 1)
                tt(m.mcol[0:T, :], M1[0:T, 16:20], bcol[0:T, 0:4], ALU.add).then_inc(sig["ml_mt"], 1)
                if not sample:
                    dve.wait_ge(sig["ml_wD"], 1)
                    tt(mp.rearrange("p h b -> p (h b)"), bcol[:, 8:12], last_M, ALU.add).then_inc(sig["m_next"], 1)

            def hg_decayed():
                dve.wait_ge(sig["hg_eb"], 1)
                for odd, half in HALVES:
                    mul(hqe[half, odd::2, :], hq[half, odd::2, :], bH[half]).then_inc(sig["hg_qe"], 1)
                dve.wait_ge(sig["hg_ekd"], 1)
                mul(hkd, hk, hkd).then_inc(sig["hg_kd"], 1)

            def ml_decayed():
                dve.wait_ge(sig["ml_wexp"], 1)
                for odd, half in HALVES:
                    mul(mqw[half, odd::2, :], mq[half, odd::2, :], wexp[half, odd::2, :]).then_inc(sig["ml_qw"], 1)

            def ml_scores():
                dve.wait_ge(sig["ml_scores"], 1)
                dve.wait_ge(sig["ml_W"], 1)
                mul(mW[0:T], heads(M0[0:T, 0:W]), mW[0:T]).then_inc(sig["ml_P"], 1)

            def delta_targets():
                dve.wait_ge(sig["gd_kS"], 1)
                mul(r[0:T], heads(G3[0:T, :]), per_head(nbeta[0:T], DKG)).then_inc(sig["gd_r"], 1)

            def ml_keys():
                dve.wait_ge(sig["ml_k_turned"], 1)
                dve.wait_ge(sig["ml_kw"], 1)
                mul(heads(mks[0:T, :]), heads(M0[0:T, 0:2 * P]), per_head(kw[0:T], DKM)).then_inc(sig["ml_ks"], 1)

            def inverse(lv):
                dve.wait_ge(sig["inv_p2"], lv)
                tt(X[0:T], X[0:T], heads(G1[0:T, 0:W]), ALU.subtract).then_inc(sig["X_ready"], 1)

            def masked(s):
                dve.wait_ge(sig["hg_scores"], s + 1)
                dst = hacc if s == 0 else htmp[s % 2]
                if s > 2:
                    dve.wait_ge(sig["hg_sum"], s - 2)
                mul(dst[0:T], heads((H0, H1)[s % 2][0:T, 0:W]), over_heads(ident if s == 0 else up(s - 1))
                    ).then_inc(sig["hg_masked"], 1)

            def level_operands(lv):
                dve.wait_ge(sig["lev_ready"], 1)
                if lv >= 2:
                    dve.wait_ge(sig["hg_scores"], lv)
                for odd, half in HALVES:
                    mul(lq[lv % 2][half, odd::2, :], hq[half, odd::2, :], lev[half, lv]).then_inc(sig["lq"], 1)
                mul(lk[lv % 2], hk, lev[:, lv]).then_inc(sig["lq"], 1)

            masked(0)
            level_operands(0)
            extras = {1: (ml_maxima,), 2: (ml_columns, hg_decayed), 3: (delta_targets,), 4: (ml_decayed,),
                      5: (ml_scores,)}
            if sample:
                extras = {1: (ml_maxima, ml_columns, hg_decayed, ml_decayed)}
            for lv in range(1, nl):
                inverse(lv)
                masked(lv)
                level_operands(lv)
                for step in extras.get(lv, ()):
                    step()
            masked(nl)
            if sample:
                ml_scores()
                delta_targets()
            ml_keys()
            dve.wait_ge(sig["ml_num"], 1)
            num = M1[0:T, 0:H * (DKM + 1)].rearrange("p (h n) -> p h n", h=H)
            dve.tensor_copy(den[0:T], num[:, :, DKM]).then_inc(sig["ml_den"], 1)
            dve.wait_ge(sig["ml_den"], 1)
            dve.scalar_tensor_tensor(out=den[0:T], in0=den[0:T], scalar=-1.0, in1=den[0:T], op0=ALU.mult, op1=ALU.max
                                     ).then_inc(sig["ml_den"], 1)
            dve.wait_ge(sig["ml_den"], 2)
            dve.wait_ge(sig["ml_emt"], 1)
            tt(den[0:T], den[0:T], emt[0:T], ALU.max).then_inc(sig["ml_den"], 1)
            dve.wait_ge(sig["ml_den"], 3)
            dve.reciprocal(den[0:T], den[0:T]).then_inc(sig["ml_den"], 1)
            dve.wait_ge(sig["ml_den"], 4)
            og4 = heads(tk(0, O0, O0 + H * DKM))
            for h in range(H):
                dve.scalar_tensor_tensor(out=heads(mog[0:T, :])[:, h], in0=num[:, h, 0:DKM], scalar=den[0:T, h:h + 1],
                                         in1=og4[:, h], op0=ALU.mult, op1=ALU.mult).then_inc(sig["ml_h"], 1)
            C = st["C_ml"]
            if not sample:
                dve.wait_ge(sig["ml_delta"], 1)
                for h in range(H):
                    half, j = pair_of(h)
                    dve.scalar_tensor_tensor(out=C[half, j, 0], in0=C[half, j, 0], scalar=wexp[half, h, T - 1:T],
                                             in1=M0[half, h * (DKM + 1):(h + 1) * (DKM + 1)],
                                             op0=ALU.mult, op1=ALU.add).then_inc(sig["ml_state"], 1)
            else:
                dve.wait_ge(sig["hg_o"], 1)
                for h in range(H):
                    half, j = pair_of(h)
                    e = seqs(wexp)[half, h, :, L - 1]
                    mul(C[half, j], C[half, j], bc(e.unsqueeze(2), 64, nseq, DKM + 1)
                        ).then_inc(sig["ml_decayed"], 1)
                    e = seqs(bH)[half, j, :, L - 1]
                    mul(st["S_hg"][half, j], st["S_hg"][half, j], bc(e.unsqueeze(2), 64, nseq, DKH)
                        ).then_inc(sig["hg_decayed"], 1)
                for h in range(H):
                    half, j = pair_of(h)
                    dve.wait_ge(sig["ml_decayed"], h + 1)
                    for q in range(2):
                        i = 2 * h + q
                        dve.wait_ge(sig["ml_delta"], i + 1)
                        b = (M0, H1)[i % 2]
                        tt(C[half, j, 4 * q:4 * q + 4], C[half, j, 4 * q:4 * q + 4],
                           b[half, 0:4 * (DKM + 1)].rearrange("p (b n) -> p b n", b=4), ALU.add
                           ).then_inc(sig["ml_state"], 1)
            Sh = st["S_hg"]
            for h in range(H):
                half, j = pair_of(h)
                if not sample:
                    dve.wait_ge(sig["hg_delta"], 1)
                    dve.scalar_tensor_tensor(out=Sh[half, j, 0], in0=Sh[half, j, 0], scalar=bH[half, j, T - 1:T],
                                             in1=H1[half, h * DKH:(h + 1) * DKH], op0=ALU.mult, op1=ALU.add
                                             ).then_inc(sig["hg_state"], 1)
                else:
                    dve.wait_ge(sig["hg_decayed"], h + 1)
                    dve.wait_ge(sig["hg_delta"], h + 1)
                    tt(Sh[half, j], Sh[half, j], (H1, M0)[h % 2][half, :].rearrange("p (b n) -> p b n", b=nseq),
                       ALU.add).then_inc(sig["hg_state"], 1)

            def normed(out, src, ms, weight, name):
                dve.wait_ge(sig[name + "_rstd"], 2)
                for h in range(H):
                    dve.scalar_tensor_tensor(out=out[:, h], in0=src[:, h], scalar=ms[0:T, h:h + 1], in1=weight(h),
                                             op0=ALU.mult, op1=ALU.mult).then_inc(sig["mix"], 1)

            normed(heads(mix[0:T, 0:H * DKM]), heads(mog[0:T, :]), mms, lambda h: rows["mlw"][0:T], "ml")
            gate = heads(tk(2, OG2, OG2 + H * DKH))
            normed(heads(mix[0:T, H * (DKM + DKG):]), heads(H0[0:T, 0:H * DKH]), hms, lambda h: gate[:, h], "hg")
            S = st["S_gd"]
            gate1 = heads(tk(1, OG1, OG1 + H * DKG))
            normed(heads(mix[0:T, H * DKM:H * (DKM + DKG)]), heads(G2[0:T, :]), msg, lambda h: gate1[:, h], "gd")
            if not sample:
                dve.wait_ge(sig["gd_delta"], 1)
                for h in range(H):
                    dve.scalar_tensor_tensor(out=S[:, h, 0], in0=S[:, h, 0], scalar=edb[:, h, T - 1:T],
                                             in1=G3[:, h * DKG:(h + 1) * DKG], op0=ALU.mult, op1=ALU.add)
            else:
                for h in range(H):
                    dve.wait_ge(sig["gd_decayed"], h + 1)
                    for q in range(2):
                        i = 2 * h + q
                        dve.wait_ge(sig["gd_delta"], i + 1)
                        tt(S[:, h, 4 * q:4 * q + 4], S[:, h, 4 * q:4 * q + 4],
                           (G3, G0)[i % 2][:, :].rearrange("p (b n) -> p b n", b=4), ALU.add
                           ).then_inc(sig["gd_state"], 1)
            dve.wait_ge(sig["mix_turned"], 1)
            src = M0[:, 0:W].rearrange("p (k t) -> p k t", k=4)
            dve.tensor_copy(hTc[:, 0:2, :], src[:, 0:2])
            dve.tensor_copy(hTc[:, 6:8, :], src[:, 2:4])

        @block.tensor
        def _(pe):
            def per_h(bank, width, lhs, rhs, done, n=T):
                for h in range(H):
                    mm = pe.matmul(bank[0:n, h * width:(h + 1) * width], lhs(h), rhs(h), start=True, stop=True)
                return mm.then_inc(sig[done], 1)

            def turn(bank, src, n, done):
                for k in range(n):
                    mm = pe.transpose(bank[0:T, k * P:(k + 1) * P], src[:, k, :], m.c("ident"))
                mm.then_inc(sig[done], 1)

            def turn_square(src, done):
                for h in range(H):
                    mm = pe.transpose(G2[0:T, h * T:(h + 1) * T], src[0:T, h], ident)
                mm.then_inc(sig[done], 1)

            def pairs(bank, a, b, done):
                for h in range(H):
                    mm = pe.matmul(bank[0:T, h * T:(h + 1) * T], a[:, h // 2], b[:, h], start=True, stop=True)
                mm.then_inc(sig[done], 1)

            n1 = DKM + 1
            pe.wait_ge(sig["gates_taken"], 1)
            pe.matmul(M1[:, 8:12], ones[0:T, :], lf, start=True, stop=True)
            pe.matmul(M1[0:T, 0:4], upto, lf, start=True, stop=True).then_inc(sig["ml_bcols"], 1)
            pe.matmul(G3[0:T, 0:4], upto, gg, start=True, stop=True)
            pe.matmul(G3[0:T, 4:8], same, gg, start=True, stop=True).then_inc(sig["gd_dcols"], 1)
            pe.wait_ge(sig["squares"], 1)
            pe.matmul(G0[:, 0:W], ones, flat(sqk), start=True, stop=True).then_inc(sig["norm_sums"], 1)
            pe.wait_ge(sig["gd_ug"], 1)
            pe.matmul(G2[:, 0:W], ones[0:T, :], flat(ug[0:T]), start=True, stop=True).then_inc(sig["gd_drows"], 1)
            pe.wait_ge(sig["squares"], 2)
            pe.matmul(G1[:, 0:W], ones, flat(sqq), start=True, stop=True).then_inc(sig["norm_sums"], 1)
            pe.wait_ge(sig["ml_ua_ready"], 1)
            pe.matmul(M0[:, 0:W], ones[0:T, :], flat(ua[0:T]), start=True, stop=True).then_inc(sig["ml_arows"], 1)
            pe.wait_ge(sig["gd_kn"], 1)
            per_h(G0, T, lambda h: kn[:, h], lambda h: kn[:, h], "gd_kk")
            pe.wait_ge(sig["gd_qn"], 1)
            per_h(G1, T, lambda h: kn[:, h], lambda h: qn[:, h], "gd_kq")
            pe.wait_ge(sig["dcol_taken"], 1)
            turn(G3, kn, H, "k_turned")
            pe.wait_ge(sig["gd_edb"], 1)
            pe.wait_ge(sig["Y_ready"], 1)
            turn_square(Y, "gd_X0")

            def scores(s):
                if s == 0:
                    pe.wait_ge(sig["hg_q"], 2)
                    pe.wait_ge(sig["hg_k"], 2)
                else:
                    pe.wait_ge(sig["lq"], 3 * s)
                if s >= 2:
                    pe.wait_ge(sig["hg_masked"], s - 1)
                a, b = (hk, hq) if s == 0 else (lk[(s - 1) % 2], lq[(s - 1) % 2])
                pairs((H0, H1)[s % 2], a, b, "hg_scores")

            def ml_products():
                pe.wait_ge(sig["ml_a_taken"], 1)
                pe.wait_ge(sig["ml_q"], 2)
                pe.wait_ge(sig["ml_k"], 1)
                pairs(M0, mk, mq, "ml_scores")

            def ml_max_columns():
                pe.wait_ge(sig["ml_M"], 4)
                for h in range(H):
                    mm = pe.matmul(M1[0:T, 16 + h:17 + h], M[:, h], m.c("ident")[:, 0:1], start=True, stop=True)
                mm.then_inc(sig["ml_Mcols"], 1)

            def ml_key_turn():
                pe.wait_ge(sig["ml_P"], 1)
                turn(M0, mk, 2, "ml_k_turned")

            def ml_output():
                pe.wait_ge(sig["ml_P"], 1)
                pe.wait_ge(sig["ml_qw"], 2)
                pe.wait_ge(sig["ml_v"], 2)
                pe.wait_ge(sig["ml_mt"], 1)
                if sample:
                    pe.wait_ge(sig["qx_ready"], 1)
                for h in range(H):
                    out = M1[0:T, h * n1:(h + 1) * n1]
                    for b in range(nseq):
                        lhs = mqx[:, h, b] if sample else mqw[:, h]
                        pe.matmul(out, lhs, st["C_ml"][:, h // 2, b], start=(b == 0), stop=False)
                    mm = pe.matmul(out, mW[0:T, h], vext[0:T, h], start=False, stop=True)
                mm.then_inc(sig["ml_num"], 1)

            def delta_products():
                pe.wait_ge(sig["gd_kdec"], H)
                pe.wait_ge(sig["gd_kd"], 1)
                pe.wait_ge(sig["v_taken"], 1)
                if sample:
                    pe.wait_ge(sig["gd_x"], 1)
                for h in range(H):
                    out = G3[0:T, h * DKG:(h + 1) * DKG]
                    pe.matmul(out, vS[:, h], m.c("ident"), start=True, stop=False)
                    for b in range(nseq):
                        lhs = kx[:, h, b] if sample else kd[:, h]
                        mm = pe.matmul(out, lhs, st["S_gd"][:, h, b], start=False, stop=(b == nseq - 1))
                mm.then_inc(sig["gd_kS"], 1)

            def inverse(lv):
                if lv > 1:
                    pe.wait_ge(sig["X_ready"], lv)
                    turn_square(X, "X_turned")
                pe.wait_ge(sig["AM_ready"], lv)
                pe.wait_ge(sig["X_ready"], lv)
                if lv == 1:
                    pe.wait_ge(sig["gd_A"], 1)
                per_h(G0, T, lambda h: AM[lv % 2][0:T, h], lambda h: X[0:T, h], "inv_p1")
                scores(lv)
                pe.wait_ge(sig["inv_p1_taken"], lv)
                if lv == 1:
                    pe.wait_ge(sig["gd_att"], 1)
                else:
                    pe.wait_ge(sig["Y_taken"], lv - 1)
                per_h(G1, T, lambda h: Y[0:T, h], lambda h: p1[0:T, h], "inv_p2")

            def hg_key_turn():
                pe.wait_ge(sig["hg_kd"], 1)
                pe.wait_ge(sig["hg_masked"], nl + 1)
                turn(H1, hkd, 2, "hg_k_turned")

            def hg_output():
                pe.wait_ge(sig["hg_qe"], 2)
                pe.wait_ge(sig["hg_sum"], nl)
                if sample:
                    pe.wait_ge(sig["qx_ready"], 1)
                for h in range(H):
                    out = H0[0:T, h * DKH:(h + 1) * DKH]
                    for b in range(nseq):
                        lhs = hqx[:, h, b] if sample else hqe[:, h]
                        pe.matmul(out, lhs, st["S_hg"][:, h // 2, b], start=(b == 0), stop=False)
                    mm = pe.matmul(out, hacc[0:T, h], tk(2, I2 + h * DKH, I2 + (h + 1) * DKH), start=False, stop=True)
                mm.then_inc(sig["hg_o"], 1)

            extras = {1: (ml_products,), 2: (ml_max_columns,), 3: (delta_products,)}
            if sample:
                extras = {1: (ml_products, ml_max_columns, delta_products)}
            scores(0)
            for lv in range(1, nl):
                inverse(lv)
                for step in extras.get(lv, ()):
                    step()
            scores(nl)
            ml_key_turn()
            ml_output()
            pe.wait_ge(sig["gd_r"], 1)
            pe.wait_ge(sig["X_ready"], nl)
            per_h(G1, DKG, lambda h: X[0:T, h], lambda h: r[0:T, h], "gd_u")
            hg_key_turn()
            pe.wait_ge(sig["ml_ks"], 1)
            if not sample:
                for h in range(H):
                    half, j = pair_of(h)
                    mm = pe.matmul(M0[:, h * n1:(h + 1) * n1], mks[0:T, j * P:(j + 1) * P], vext[0:T, h],
                                   start=True, stop=True)
                mm.then_inc(sig["ml_delta"], 1)
            pe.wait_ge(sig["gd_qd"], 1)
            pe.wait_ge(sig["u_ready"], 1)
            if nl > 2:
                pe.wait_ge(sig["Y_taken"], nl - 2)
            for h in range(H):
                out = G2[0:T, h * DKG:(h + 1) * DKG]
                for b in range(nseq):
                    lhs = qx[:, h, b] if sample else qd[:, h]
                    pe.matmul(out, lhs, st["S_gd"][:, h, b], start=(b == 0), stop=False)
                mm = pe.matmul(out, EB[0:T, h], u[0:T, h], start=False, stop=True)
            mm.then_inc(sig["gd_o"], 1)
            hg_output()
            pe.wait_ge(sig["hg_kT"], 1)
            if not sample:
                for h in range(H):
                    half, j = pair_of(h)
                    mm = pe.matmul(H1[:, h * DKH:(h + 1) * DKH], hkdT[0:T, j * P:(j + 1) * P],
                                   tk(2, I2 + h * DKH, I2 + (h + 1) * DKH), start=True, stop=True)
                mm.then_inc(sig["hg_delta"], 1)
            else:
                pe.wait_ge(sig["values_spread"], 1)
                for i in range(2 * H):
                    h, q = i // 2, i % 2
                    half, j = pair_of(h)
                    if i >= 2:
                        pe.wait_ge(sig["ml_state"], i - 1)
                    b = (M0, H1)[i % 2]
                    pe.matmul(b[:, 0:4 * n1], mks[0:T, j * P:(j + 1) * P],
                              vx[0:T, h, 4 * q:4 * q + 4].rearrange("p b n -> p (b n)"), start=True, stop=True
                              ).then_inc(sig["ml_delta"], 1)
                pe.wait_ge(sig["ml_state"], 2 * H)
                for h in range(H):
                    half, j = pair_of(h)
                    if h >= 2:
                        pe.wait_ge(sig["hg_state"], h - 1)
                    pe.matmul((H1, M0)[h % 2][:, :], hkdT[0:T, j * P:(j + 1) * P],
                              hx[0:T, h].rearrange("p b n -> p (b n)"), start=True, stop=True
                              ).then_inc(sig["hg_delta"], 1)
            if not sample:
                per_h(G3, DKG, lambda h: kdec[0:T, h], lambda h: u[0:T, h], "gd_delta", n=P)
            else:
                for i in range(2 * H):
                    h, q = i // 2, i % 2
                    pe.wait_ge(sig["u_spread"], h + 1)
                    if i >= 2:
                        pe.wait_ge(sig["gd_state"], i - 1)
                    pe.matmul((G3, G0)[i % 2][:, :], kdec[0:T, h],
                              ux[h % 2][0:T, 4 * q:4 * q + 4].rearrange("p b n -> p (b n)"), start=True, stop=True
                              ).then_inc(sig["gd_delta"], 1)
            pe.wait_ge(sig["mix"], 2 * H)
            if sample:
                pe.wait_ge(sig["hg_state"], H)
            else:
                pe.wait_ge(sig["ml_state"], H)
            for k, kt in enumerate((0, 1, 6, 7)):
                mm = pe.transpose(M0[:, k * T:(k + 1) * T], mix[0:T, kt * P:(kt + 1) * P], ident)
            mm.then_inc(sig["mix_turned"], 1)
            pe.wait_ge(sig["mix"], 3 * H)
            for k, kt in enumerate((2, 3, 4, 5)):
                mm = pe.transpose(M1[:, k * T:(k + 1) * T], mix[0:T, kt * P:(kt + 1) * P], ident)
            mm.then_inc(sig["mix_turned"], 1)


def output_phase(nc, m, d, l, st):
    one = bass.ds(l, 1)
    OUT, UP = D // 512, FF // 256
    DOWN0 = OUT + UP
    silu, rstd = m.silu, m.rstd2
    spare = silu.rearrange("p (k x) n -> p k (x n)", k=2)
    sq = [m.act[:, FT - 6 + k] for k in range(6)] + [spare[:, 0], spare[:, 1]]

    def slot_fill(e):
        return e % SLOTS, (DOWN0 if e % SLOTS < KT else 0) + e // SLOTS

    parts = ExitStack()
    with parts, phase(nc) as (sig, block):
        def tensor(shape, dtype):
            return parts.enter_context(m.tensor(shape, dtype))

        slabs = Slabs(sig, m.down_slab, tensor([SLOTS, 512], F32R), tensor([SLOTS, 512], F32R))
        h = Moving(sig, m.hT, tensor([KT, TOK], F32R), tensor([KT, TOK], F32R))
        first = (tensor([TOK], F32R), tensor([TOK], F32R))

        def act_parts(k):
            return (first[0][:, :], first[1][:, :]) if k == 0 else (h.highs[:, k % KT], h.lows[:, k % KT])

        @block.sync
        def _(sp):
            with sp.Fori(0, OUT) as j:
                for k in range(KT):
                    slabs.load(sp, k, j, rows_of(d["w_out"], one, k, bass.ds(j * 512, 512)))
            store_states(sp, m, d, l, st, "s", slice(DSEQ - 1, SAMP, DSEQ), sig)
            w = d["w_gate_up"].rearrange("l p (g n) -> l p g n", g=2)
            with sp.Fori(0, UP) as j:
                for k in range(KT):
                    slabs.load(sp, k, OUT + j, w[one, k * P:(k + 1) * P, :, bass.ds(j * 256, 256)]
                               .rearrange("o p g n -> (o p) g n"))
            with sp.Fori(0, 2) as j:
                for k in range(FT):
                    s, n = slot_fill(k)
                    slabs.load(sp, s, n + 2 * j, rows_of(d["w_down"], one, k, bass.ds(j * 512, 512)))
            sp.wait_ge(sig["state_stored"], STORES)

        @block.tensor
        def _(pe):
            slabs.all_free(pe)
            feature_group(pe, m, sig, slabs, h, 0, 0, h_base=0)
            feature_group(pe, m, sig, slabs, h, 1, 1)
            pe.wait_ge(sig["first_banks_read"], 4 + 4 * OUT)
            norm_total(pe, m, sig, sq[0])
            pe.wait_ge(sig["rstd_ln"], 2)
            feature_group(pe, m, sig, slabs, h, OUT, OUT, h_base=KT)
            with pe.Fori(OUT + 1, DOWN0) as g:
                feature_group(pe, m, sig, slabs, h, g, g)
            with pe.Fori(0, 2) as j:
                for k in range(FT):
                    s, n = slot_fill(k)
                    slabs.wait(pe, s, n + 2 * j)
                    pe.wait_ge(sig["act_split"], FT * j + k + 1)
                    for b in range(8):
                        t, half = b // 2, b % 2
                        if k == 0:
                            pe.wait_ge(sig["first_banks_read" if b < 4 else "last_banks_read"],
                                       4 * j + 4 * DOWN0 + b % 4 + 1)
                        tile = slice(t * P, (t + 1) * P)
                        high, low = (x[:, HALF_OF[half]] for x in act_parts(k))
                        mm = three_passes(pe, m.bank[b][:, 0:HALF], slabs.highs[:, s, tile], slabs.lows[:, s, tile],
                                          high, low, k == 0, k == FT - 1)
                        if k == FT - 1:
                            mm.then_inc(sig["bank_done"], 1)
                        elif b == 7:
                            mm.then_inc(slabs.used(s), 1)
                pe.wait_ge(sig["bank_done"], 8 * j + 8 * DOWN0 + 8)
                pe.sem_inc(slabs.used(slot_fill(FT - 1)[0]), 1)

        def down(split, tile, evac):
            for e in range(2 * FT):
                if e + 6 < 2 * FT:
                    split(*slot_fill(e + 6))
                if e % FT == FT - 1:
                    evac(DOWN0 + e // FT)
                if e + 2 < 2 * FT:
                    tile(e + 2)

        @block.scalar
        def _(act):
            def high(s, n):
                slabs.high(act, s, n)

            def tile(e):
                if e == 0:
                    act.wait_ge(sig["last_banks_read"], 4 + 4 * (OUT + 1))
                elif e <= FT:
                    act.wait_ge(sig["last_banks_read"], 4 + 4 * DOWN0)
                if e >= KT:
                    s, n = slot_fill(e - 2)
                    act.wait_ge(slabs.used(s), n + 2)
                act.copy(act_parts(e % FT)[0], m.act[:, e % FT]).then_inc(sig["act_high"], 1)

            def gates(g):
                for b in range(4):
                    act.wait_ge(sig["bank_done"], 8 * g + b + 1)
                    act.wait_ge(sig["last_banks_read"], 4 * g + b + 1)
                    act.activation(silu[:, b, :], m.bank[b][:, 0:HALF], ACT.Silu).then_inc(sig["first_banks_read"], 1)

            for k in range(KT):
                high(k, 0)
                h.high(act, k, wait=False)
            for k in range(KT):
                high(k, 1)
            for k in range(6):
                high(k, 2)
                if k >= 2:
                    t = k - 2
                    act.wait_ge(sig["first_banks_read" if t < 2 else "last_banks_read"], 4 + 2 * (t % 2) + 2)
                    norm_square(act, m, sig, t, sq[t])
            for t in range(4):
                act.wait_ge(sig["first_banks_read" if t < 2 else "last_banks_read"], 8 + 2 * (t % 2) + 2)
                norm_square(act, m, sig, 4 + t, sq[4 + t])
            high(6, 2)
            high(7, 2)
            norm_rstd(act, m, sig, rstd)
            for k in range(KT):
                h.high(act, k)
            with act.Fori(OUT, DOWN0 - 1) as g:
                for k in range(6):
                    high(k, g + 1)
                gates(g)
                for k in (6, 7):
                    high(k, g + 1)
            for e in range(6):
                high(*slot_fill(e))
            tile(0)
            gates(DOWN0 - 1)
            tile(1)
            down(high, tile, lambda g: None)

        @block.vector
        def _(dve):
            def low(s, n):
                slabs.low(dve, s, n)

            def tile(e):
                dve.wait_ge(sig["act_high"], e + 1)
                high, low = act_parts(e % FT)
                dve.tensor_tensor(low, m.act[:, e % FT], high.bitcast(F32), ALU.subtract
                                  ).then_inc(sig["act_split"], 1)

            def add(g, j):
                for b in range(8):
                    dve.wait_ge(sig["bank_done"], 8 * g + b + 1)
                    x = m.x[:, 4 * j + b // 2, HALF_OF[b % 2]]
                    dve.tensor_tensor(x, x, m.bank[b][:, 0:HALF], ALU.add
                                      ).then_inc(sig["first_banks_read" if b < 4 else "last_banks_read"], 1)

            def product(g):
                for b in range(4):
                    dve.wait_ge(sig["bank_done"], 8 * g + 4 + b + 1)
                    dve.wait_ge(sig["first_banks_read"], 4 * g + b + 5)
                    out = m.act[:, bass.ds(2 * (g - OUT) + b // 2, 1), HALF_OF[b % 2]]
                    dve.tensor_tensor(out.rearrange("p o n -> p (o n)"), silu[:, b, :], m.bank[4 + b][:, 0:HALF],
                                      ALU.mult).then_inc(sig["last_banks_read"], 1)

            slabs.all_split(dve)
            dve.sem_inc(sig["first_banks_read"], 4)
            dve.sem_inc(sig["last_banks_read"], 4)
            for k in range(KT):
                low(k, 0)
                h.low(dve, k)
            for k in range(6):
                low(k, 1)
            add(0, 0)
            for k in (6, 7):
                low(k, 1)
            for k in range(6):
                low(k, 2)
                if k >= 3:
                    norm_sum(dve, m, sig, k - 2, sq[0], sq[k - 2])
            add(1, 1)
            for t in range(4, KT):
                norm_sum(dve, m, sig, t, sq[0], sq[t])
            low(6, 2)
            low(7, 2)
            norm_apply(dve, m, sig, h, m.colw[:, 56:64], rstd, KT)
            dve.wait_ge(sig["state_stored"], STORES)
            with dve.Fori(OUT, DOWN0 - 1) as g:
                for k in range(6):
                    low(k, g + 1)
                product(g)
                for k in (6, 7):
                    low(k, g + 1)
            for e in range(6):
                low(*slot_fill(e))
            tile(0)
            product(DOWN0 - 1)
            tile(1)
            down(low, tile, lambda g: add(g, g - DOWN0))


def final_phase(nc, m, d):
    m.top = m.arena
    wrows = m.take(P)
    y = m.take(NT, D)
    sq, rstd = m.take(KT, TOK), m.take(TOK)
    with phase(nc) as (sig, block):
        @block.sync
        def _(sp):
            sp.dma_start(wrows[0:KT, :], d["final_norm_w"].rearrange("(k p) -> k p", p=P)
                         ).then_inc(sig["rows_loaded"], 16)
            for i in range(NT):
                sp.wait_ge(sig["y_even"], i + 1)
                sp.wait_ge(sig["y_odd"], i + 1)
                dst = d["y_prompt"][0, i * P:(i + 1) * P, :] if i < NT - 1 else \
                    d["y_sample"].rearrange("b t n -> (b t) n")
                sp.dma_start(dst, y[0:tile_rows(i), i, :]).then_inc(sig["y_stored"], 16)
            sp.wait_ge(sig["y_stored"], 16 * NT)

        @block.tensor
        def _(pe):
            pe.wait_ge(sig["rows_loaded"], 16)
            pe.transpose(m.bank[7][:, 0:KT], wrows[0:KT, :], m.c("ident", KT)[:, 0:KT]).then_inc(sig["rows_turned"], 1)
            norm_total(pe, m, sig, sq[:, 0])
            pe.wait_ge(sig["h_made"], KT)
            for u in range(2 * NT):
                i, g = u // 2, u % 2
                n = tile_rows(i)
                if u >= 6:
                    pe.wait_ge(sig["y_even" if g == 0 else "y_odd"], (u - 6) // 2 + 1)
                for k in range(4):
                    mm = pe.transpose(m.bank[u % 6][0:n, k * P:(k + 1) * P], m.hT[:, 4 * g + k, i * P:i * P + n],
                                      m.c("ident"))
                mm.then_inc(sig["y_turned"], 1)

        def evacuate(eng, copy, g):
            for i in range(NT):
                n = tile_rows(i)
                u = 2 * i + g
                eng.wait_ge(sig["y_turned"], u + 1)
                copy(y[0:n, i, g * 512:(g + 1) * 512], m.bank[u % 6][0:n, :]
                     ).then_inc(sig["y_even" if g == 0 else "y_odd"], 1)

        @block.scalar
        def _(act):
            for k in range(KT):
                norm_square(act, m, sig, k, sq[:, k])
            norm_rstd(act, m, sig, rstd)
            evacuate(act, act.copy, 0)

        @block.vector
        def _(dve):
            dve.wait_ge(sig["rows_turned"], 1)
            dve.tensor_copy(m.colw[:, 0:KT], m.bank[7][:, 0:KT]).then_inc(sig["colw_ready"], 1)
            for k in range(1, KT):
                norm_sum(dve, m, sig, k, sq[:, 0], sq[:, k])
            dve.wait_ge(sig["colw_ready"], 1)
            dve.wait_ge(sig["rstd"], 1)
            for k in range(KT):
                dve.scalar_tensor_tensor(out=m.hT[:, k], in0=m.x[:, k], scalar=m.colw[:, k:k + 1], in1=rstd,
                                         op0=ALU.mult, op1=ALU.mult).then_inc(sig["h_made"], 1)
            evacuate(dve, dve.tensor_copy, 1)


def build(nc, d, const_at, n_const):
    with ExitStack() as stack:
        stack.enter_context(nc.allow_non_contiguous_dma(reason="the states n and m are a few thousand words"))
        m = Memory(nc, stack, const_at, n_const)
        with m.open_area():
            setup_phase(nc, m, d)
        with nc.Fori(0, DEPTH) as l:
            input_phase(nc, m, d, l)
            with m.open_area():
                prep_phase(nc, m, d, l)
                prompt = {"S_gd": m.S_gd, "C_ml": m.C_ml, "S_hg": m.S_hg, "m_ml": m.m_ml}
                with nc.Fori(0, SEQ // P) as c:
                    chunk_phase(nc, m, prompt, 1, c)
                st = states_phase(nc, m, d, l)
                chunk_phase(nc, m, st, NSEQ, None)
            output_phase(nc, m, d, l, st)
        with m.open_area():
            final_phase(nc, m, d)


_INS = ["x_prompt", "x_sample", "state_mlstm_C", "state_mlstm_n", "state_mlstm_m", "state_gdn_S", "state_gdn_conv",
        "state_hgrn_S", "norm1_w", "w_in", "ml_i_bias", "ml_f_bias", "ml_norm_w", "gd_conv_w", "gd_A_log",
        "gd_dt_bias", "gd_norm_w", "hg_lower_bounds", "hg_norm_w", "w_out", "norm2_w", "w_gate_up", "w_down",
        "final_norm_w"]


def _states(who, b):
    return [(who + "_C", (DEPTH, b, H, DKM, DKM)), (who + "_n", (DEPTH, b, H, DKM)), (who + "_m", (DEPTH, b, H)),
            (who + "_S", (DEPTH, b, H, DKG, DKG)), (who + "_conv", (DEPTH, b, CONV - 1, 3 * H * DKG)),
            (who + "_H", (DEPTH, b, H, DKH, DKH))]


_OUTS = [("y_prompt", (1, SEQ, D)), ("y_sample", (NSEQ, DSEQ, D))] + _states("p", 1) + _states("s", NSEQ)


def kernel(**inputs):
    import concourse.bacc as bacc
    from concourse.bass_utils import run_bass_kernel_spmd as run

    nc = bacc.Bacc("TRN2", target_bir_lowering=False, num_devices=1)
    consts, const_at = constants()
    arrays, d = {"in_consts": consts}, {}
    for name in _INS:
        arrays["in_" + name] = np.ascontiguousarray(inputs[name])
    for name, a in arrays.items():
        d[name[3:]] = nc.dram_tensor(name, a.shape, mybir.dt.from_np(a.dtype), kind="ExternalInput").ap()
    for name, shape in _OUTS:
        d[name] = nc.dram_tensor("out_" + name, shape, F32, kind="ExternalOutput").ap()
    build(nc, d, const_at, consts.shape[1])
    r = run(nc, [arrays], core_ids=[0])
    return tuple(r.results[0]["out_" + name] for name, _ in _OUTS)
```

```python
from contextlib import ExitStack, contextmanager

import numpy as np

import concourse.bass as bass
from concourse import mybir

F32 = mybir.dt.float32
F32R = mybir.dt.float32r
ALU = mybir.AluOpType
ACT = mybir.ActivationFunctionType
AX = mybir.AxisListType

P = 128
D, SEQ, DEPTH, NSEQ, DSEQ = 1024, 512, 2, 8, 4
SAMP = NSEQ * DSEQ
TOK = SEQ + SAMP
HALF = TOK // 2
NT = SEQ // P + 1
H = 4
DKM, DKG, DKH = 64, 128, 64
CONV = 4
GT = 3 * H * DKG // P
KT = D // P
FF = 2816
FT = FF // P
MIX = H * (DKM + DKG + DKH)
EPS = 1e-6
LEVELS = 7
TINY = 2.0 ** -63

ML_QK, ML_VO, GD_QKV, GD_G, HG_QF, HG_IG = 0, 512, 1032, 2568, 3088, 3600
GROUP = 520
V0, O0, I0, F0 = 0, 256, 512, 516
OG1, A1, B1 = 0, 512, 516
I2, OG2 = 0, 256
LI, LF, GG, BETA = 0, 4, 8, 12

ARENA = 21240
SLOTS = 11

SEM0 = 110
EXP_LN = "natural_log_exp_and_others"


def constants():
    s, t = np.meshgrid(np.arange(P), np.arange(P), indexing="ij")
    parts, at, n = [], {}, 0

    def put(name, a):
        nonlocal n
        at[name] = (n, a.shape[1])
        parts.append(a.astype(np.float32))
        n += a.shape[1]

    put("ident", s == t)
    put("ones", np.ones((P, P)))
    put("upto", s <= t)
    put("end", np.broadcast_to(t == P - 1, (P, P)))
    for l in range(LEVELS):
        block = (s >> (l + 1)) == (t >> (l + 1))
        put(f"low{l}", block & ((s >> l) & 1 == 1) & ((t >> l) & 1 == 0))
        put(f"up{l}", block & ((t >> l) & 1 == 1) & ((s >> l) & 1 == 0))
    same = (s // DSEQ) == (t // DSEQ)
    k = SAMP
    put("upto_s", (same & (s <= t))[:, :k])
    put("same_s", same[:, :k])
    put("end_s", (same & (t % DSEQ == DSEQ - 1))[:, :k])
    b, tt = np.meshgrid(np.arange(NSEQ), np.arange(k), indexing="ij")
    put("seq_of_column", np.broadcast_to((tt // DSEQ == b).reshape(1, -1), (P, NSEQ * k)))
    put("seq_of_row", (np.arange(P)[:, None] // DSEQ) == np.arange(NSEQ)[None])
    return np.concatenate(parts, axis=1), at


class Signals:

    def __init__(self, nc):
        self.nc, self.named = nc, {}

    def __getitem__(self, name):
        if name not in self.named:
            self.named[name] = self.nc.alloc_semaphore(name, num=SEM0 + len(self.named))
        return self.named[name]


@contextmanager
def phase(nc):
    sig = Signals(nc)
    with nc.Block(no_gpsimd_drain=True) as block:
        yield sig, block
    for s in sig.named.values():
        nc.release_semaphore(s)
    nc.all_engine_barrier(sems_to_clear=range(SEM0, SEM0 + len(sig.named)))


def bc(ap, *shape):
    return ap.broadcast_to(list(shape))


def tile_rows(i):
    return SAMP if i == NT - 1 else P


class Memory:

    def __init__(self, nc, stack, const_at, n_const):
        self.nc, self.stack = nc, stack
        self.words = nc.sbuf_bytes_remaining // 4 // 8 * 8 - 8
        self.arena = self.words - ARENA
        self.all = stack.enter_context(nc.sbuf_tensor("sbuf", [P, self.arena], F32))
        self.area, self.tensors = None, 0
        self.top = 0
        self.bank = [stack.enter_context(nc.psum_tensor(f"bank{i}", [P, 512], F32)) for i in range(8)]
        self.const = self.take(n_const)
        self.const_at = const_at
        self.x = self.take(KT, TOK)
        self.hT_at = self.top
        self.hT = self.take(KT, TOK)
        work = self.top
        self.mlF = self.take(4, TOK)
        self.gdF_at = self.top
        self.gdF = self.take(GT, CONV - 1 + SEQ)
        self.gdS = self.take(GT, NSEQ, CONV - 1 + DSEQ)
        self.gdC_at = self.top
        self.gdC = self.take(GT, SAMP)
        self.hgF = self.take(4, TOK)
        self.tokp_at = self.top
        self.tokp = self.take(NT, 3, GROUP)
        self.act = self.view(work, FT, TOK)
        self.top, tokp_end = work + FT * TOK, self.top
        self.down_slab = self.take(SLOTS, 512)
        self.silu = self.take(4, HALF)
        self.rstd2 = self.take(TOK)
        assert self.top <= tokp_end
        self.top = tokp_end
        self.gates = self.take(NT, 16)
        self.colw = self.take(64)
        self.lb = self.take(DEPTH * 2)
        self.rows = self.take(16 + 64 + 64 + 128)
        self.lbl = self.take(2)
        self.mcol = self.take(4)
        self.mcol_s = self.take(4)
        self.S_gd = self.take(H, 1, DKG)
        self.C_ml = self.take(2, 1, DKM + 1)
        self.S_hg = self.take(2, 1, DKH)
        self.m_ml = self.take(H, 1)
        assert self.top <= self.arena

    @contextmanager
    def tensor(self, shape, dtype):
        self.tensors += 1
        with self.nc.sbuf_tensor(f"arena{self.tensors}", [P] + list(shape), dtype) as t:
            yield t

    @contextmanager
    def open_area(self):
        with self.tensor([ARENA], F32) as t:
            self.area = t
            yield
        self.area = None

    def view(self, at, *shape):
        n = int(np.prod(shape))
        ap = self.all[:, at:at + n] if at < self.arena else self.area[:, at - self.arena:at - self.arena + n]
        if len(shape) == 1:
            return ap
        names = "abcd"[:len(shape)]
        sizes = dict(zip(names, shape))
        return ap.rearrange(f"p ({' '.join(names)}) -> p {' '.join(names)}", **sizes)

    def take(self, *shape):
        ap = self.view(self.top, *shape)
        self.top += int(np.prod(shape))
        assert self.top <= self.words
        return ap

    def c(self, name, rows=P):
        at, n = self.const_at[name]
        return self.const[0:rows, at:at + n]


def layer_rows(m):
    r = m.rows
    return {"ibias": r[:, 0:4], "fbias": r[:, 4:8], "negA": r[:, 8:12], "dtb": r[:, 12:16],
            "mlw": r[:, 16:80], "hgw": r[:, 80:144], "gdw": r[:, 144:272]}


def setup_phase(nc, m, d):
    m.top = m.arena
    xt = m.take(NT, D)
    lbr = m.take(P)
    pr = m.take(DEPTH * 2)
    mx, sm = m.take(2), m.take(2)
    with phase(nc) as (sig, block):
        @block.sync
        def _(sp):
            sp.dma_start(m.const, d["consts"]).then_inc(sig["const_loaded"], 16)
            for i in range(NT):
                src = d["x_prompt"][0, i * P:(i + 1) * P, :] if i < NT - 1 else \
                    d["x_sample"].rearrange("b t n -> (b t) n")
                sp.dma_start(xt[0:tile_rows(i), i, :], src).then_inc(sig[f"x{i}_loaded"], 16)
            sp.dma_start(lbr[0:2 * DEPTH, :],
                         d["hg_lower_bounds"].rearrange("l (j p) -> (l j) p", p=P)).then_inc(sig["bounds_loaded"], 16)

        @block.gpsimd
        def _(pool):
            pool.memset(m.tokp[:, NT - 1], 0.0)

        @block.tensor
        def _(pe):
            pe.wait_ge(sig["const_loaded"], 16)
            pe.wait_ge(sig["bounds_loaded"], 16)
            pe.transpose(m.bank[0][:, 0:2 * DEPTH], lbr[0:2 * DEPTH, :], m.c("ident", 2 * DEPTH)[:, 0:2 * DEPTH]
                         ).then_inc(sig["bounds_turned"], 1)
            for i in range(NT):
                n = tile_rows(i)
                pe.wait_ge(sig[f"x{i}_loaded"], 16)
                for g in range(2):
                    u = 2 * i + g
                    if u >= 6:
                        pe.wait_ge(sig["x_taken"], u - 5)
                    for k in range(4):
                        kt = 4 * g + k
                        mm = pe.transpose(m.bank[1 + u % 6][:, k * n:(k + 1) * n], xt[0:n, i, kt * P:(kt + 1) * P],
                                          m.c("ident", n)[:, 0:n])
                    mm.then_inc(sig["x_turned"], 1)

        @block.vector
        def _(dve):
            b = m.bank[0][:, 0:2 * DEPTH]
            dve.wait_ge(sig["bounds_turned"], 1)
            dve.tensor_copy(pr, b).then_inc(sig["bounds"], 1)
            dve.wait_ge(sig["bounds"], 1)
            dve.tensor_tensor(mx, pr[:, 0:2], pr[:, 2:4], ALU.max).then_inc(sig["bounds"], 1)
            dve.wait_ge(sig["bounds"], 2)
            for l in range(DEPTH):
                dve.tensor_tensor(m.lb[:, 2 * l:2 * l + 2], pr[:, 2 * l:2 * l + 2], mx, ALU.subtract
                                  ).then_inc(sig["bounds_shifted"], 1)
            dve.wait_ge(sig["bounds_exp"], 1)
            dve.tensor_tensor(sm, pr[:, 0:2], pr[:, 2:4], ALU.add).then_inc(sig["bounds"], 1)
            dve.wait_ge(sig["bounds"], 3)
            dve.reciprocal(mx, sm).then_inc(sig["bounds"], 1)
            dve.wait_ge(sig["bounds"], 4)
            dve.tensor_tensor(pr[:, 0:2], pr[:, 0:2], mx, ALU.mult).then_inc(sig["bounds"], 1)
            dve.tensor_tensor(pr[:, 2:4], pr[:, 2:4], mx, ALU.mult).then_inc(sig["bounds"], 1)
            dve.wait_ge(sig["bounds"], 6)
            dve.tensor_tensor(m.lb[:, 0:2], pr[:, 0:2], pr[:, 0:2], ALU.subtract)
            dve.tensor_tensor(sm, pr[:, 0:2], pr[:, 2:4], ALU.add).then_inc(sig["bounds"], 1)
            dve.wait_ge(sig["bounds"], 7)
            dve.tensor_tensor(m.lb[:, 2:4], sm, pr[:, 0:2], ALU.subtract)

        @block.scalar
        def _(act):
            nc.scalar.preload_act_table_set(EXP_LN)
            act.wait_ge(sig["bounds_shifted"], DEPTH)
            act.activation(pr, m.lb, ACT.Exp).then_inc(sig["bounds_exp"], 1)
            for i in range(NT):
                n = tile_rows(i)
                for g in range(2):
                    u = 2 * i + g
                    act.wait_ge(sig["x_turned"], u + 1)
                    act.copy(m.x[:, 4 * g:4 * g + 4, i * P:i * P + n],
                             m.bank[1 + u % 6][:, 0:4 * n].rearrange("p (k t) -> p k t", k=4)
                             ).then_inc(sig["x_taken"], 1)




def three_passes(pe, out, wH, wL, hH, hL, first, last):
    pe.matmul(out, wH, hH, start=first, stop=False)
    pe.matmul(out, wH, hL, start=False, stop=False)
    return pe.matmul(out, wL, hH, start=False, stop=last)


def rows_of(w, one, k, cols):
    return w[one, k * P:(k + 1) * P, cols].rearrange("o p n -> (o p) n")


class Slabs:

    def __init__(self, sig, raw, high, low):
        self.sig, self.raw, self.highs, self.lows = sig, raw, high, low
        self.slots = raw.shape[1]

    def all_free(self, pe):
        for s in range(self.slots):
            pe.sem_inc(self.sig[f"slot{s}_used"], 1)

    def all_split(self, dve):
        for s in range(self.slots):
            dve.sem_inc(self.sig[f"slot{s}_split"], 1)

    def load(self, sp, s, n, src, width=512):
        sp.wait_ge(self.sig[f"slot{s}_split"], n + 1)
        dst = self.raw[:, s, 0:width]
        if len(src.shape) == 3:
            dst = dst.rearrange("p (g n) -> p g n", g=src.shape[1])
        sp.dma_start(dst, src).then_inc(self.sig[f"slot{s}_loaded"], 16)

    def high(self, act, s, n, width=512, freed=None):
        act.wait_ge(self.sig[f"slot{s}_loaded"], 16 * n + 16)
        act.wait_ge(*(freed or (self.sig[f"slot{s}_used"], n + 1)))
        act.copy(self.highs[:, s, 0:width], self.raw[:, s, 0:width]).then_inc(self.sig[f"slot{s}_high"], 1)

    def low(self, dve, s, n, width=512):
        dve.wait_ge(self.sig[f"slot{s}_high"], n + 1)
        dve.tensor_tensor(self.lows[:, s, 0:width], self.raw[:, s, 0:width],
                          self.highs[:, s, 0:width].bitcast(F32), ALU.subtract
                          ).then_inc(self.sig[f"slot{s}_split"], 1)

    def wait(self, pe, s, n):
        pe.wait_ge(self.sig[f"slot{s}_split"], n + 2)

    def used(self, s):
        return self.sig[f"slot{s}_used"]


HALF_OF = (slice(0, HALF), slice(HALF, TOK))


def norm_square(act, m, sig, k, sq):
    act.activation(sq, m.x[:, k], ACT.Square).then_inc(sig["squares"], 1)


def norm_sum(dve, m, sig, k, sq):
    if k < KT:
        dve.wait_ge(sig["squares"], k + 1)
        if k > 3:
            dve.wait_ge(sig["square_sum"], k - 3)
        total, more = sq[k % 2], sq[k]
    else:
        dve.wait_ge(sig["square_sum"], KT - 2)
        total, more = sq[0], sq[1]
    dve.tensor_tensor(total, total, more, ALU.add).then_inc(sig["square_sum"], 1)


def norm_total(pe, m, sig, total):
    pe.wait_ge(sig["square_sum"], KT - 1)
    for half in range(2):
        pe.matmul(m.bank[half][:, 0:HALF], m.c("ones"), total[:, HALF_OF[half]], start=True, stop=True
                  ).then_inc(sig["total"], 1)


def norm_rstd(act, m, sig, rstd):
    for half in range(2):
        act.wait_ge(sig["total"], half + 1)
        act.activation(rstd[:, HALF_OF[half]], m.bank[half][:, 0:HALF], ACT.Ln, scale=1.0 / D, bias=EPS
                       ).then_inc(sig["rstd_ln"], 1)
    act.wait_ge(sig["rstd_ln"], 2)
    act.activation(rstd, rstd, ACT.Exp, scale=-0.5).then_inc(sig["rstd"], 1)


class Moving:

    def __init__(self, sig, made, high, low):
        self.sig, self.made, self.highs, self.lows = sig, made, high, low

    def high(self, act, k, wait=True):
        if wait:
            act.wait_ge(self.sig["h_made"], k + 1)
        act.copy(self.highs[:, k], self.made[:, k]).then_inc(self.sig["h_high"], 1)

    def low(self, dve, k, base=0):
        dve.wait_ge(self.sig["h_high"], base + k + 1)
        dve.tensor_tensor(self.lows[:, k], self.made[:, k], self.highs[:, k].bitcast(F32), ALU.subtract
                          ).then_inc(self.sig["h_split"], 1)


def norm_apply(dve, m, sig, h, w, rstd, behind, base=0):
    dve.wait_ge(sig["rstd"], 1)
    for k in range(KT + 1):
        if k < KT:
            dve.scalar_tensor_tensor(out=h.made[:, k], in0=m.x[:, k], scalar=w[:, k:k + 1], in1=rstd,
                                     op0=ALU.mult, op1=ALU.mult).then_inc(sig["h_made"], 1)
        if k > 0:
            h.low(dve, k - 1, base)
            behind(k - 1)


def feature_group(pe, m, sig, slabs, h, n, g, h_base=None):
    for k in range(KT):
        slabs.wait(pe, k, n)
        if h_base is not None:
            pe.wait_ge(sig["h_split"], h_base + k + 1)
        for b in range(8):
            t, half = b // 2, b % 2
            if k == 0:
                pe.wait_ge(sig["first_banks_read" if b < 4 else "last_banks_read"], 4 * g + b % 4 + 1)
            tile = slice(t * P, (t + 1) * P)
            mm = three_passes(pe, m.bank[b][:, 0:HALF], slabs.highs[:, k, tile], slabs.lows[:, k, tile],
                              h.highs[:, k, HALF_OF[half]], h.lows[:, k, HALF_OF[half]], k == 0, k == KT - 1)
            if k == KT - 1:
                mm.then_inc(sig["bank_done"], 1)
            elif b == 7:
                mm.then_inc(slabs.used(k), 1)


def input_phase(nc, m, d, l):
    one = bass.ds(l, 1)
    keep, m.top = m.top, m.hT_at
    wrows = m.take(P)
    acc = [m.take(SEQ) for _ in range(2)]
    last = m.last = m.take(GT, 27)
    bufs_at = m.top
    bufs = m.take(GT * P)
    sacc, stmp = m.take(GT, NSEQ, DSEQ), m.take(GT, NSEQ, DSEQ)
    rstd = m.take(TOK)
    assert m.top <= m.hT_at + KT * TOK
    m.top = keep
    sq = [m.mlF[:, k] for k in range(4)] + [m.hgF[:, k] for k in range(4)]
    made = m.view(m.tokp_at, KT, TOK)
    rows = layer_rows(m)
    taps = m.colw[:, 0:48].rearrange("p (j t) -> p j t", j=CONV)
    OLD = NSEQ * (CONV - 1)
    NF = 5
    FLAT = ((1, GD_G, 520), (0, ML_VO, 520), (2, HG_IG, 512))
    widths = [512] * NF + [w for _, _, w in FLAT]
    PER = 5
    parts = ExitStack()
    FIRST = 4 * NF
    units, flat_units = [], [(n, i) for n in range(len(FLAT)) for i in range(NT)]
    while flat_units:
        at = len(units)
        units.append(("norm", at // 4 - 1) if at in (4, 8, 12, 16) else ("flat", flat_units.pop(0)))
    norm_sq = [m.view(bufs_at + i * SEQ, SEQ) for i in range(2)]

    def last_unit(n):
        return FIRST + units.index(("flat", (n, NT - 1)))

    def banks_read(last, n):
        return 4 + 4 * NF + 2 * len([u for u in range(FIRST, last_unit(n) + 1) if (u % 4 >= 2) == last])

    with parts, phase(nc) as (sig, block):
        def tensor(shape, dtype):
            return parts.enter_context(m.tensor(shape, dtype))

        slabs = Slabs(sig, tensor([KT, GROUP], F32), tensor([KT, GROUP], F32R), tensor([KT, GROUP], F32R))
        h = Moving(sig, made, tensor([KT, TOK], F32R), tensor([KT, TOK], F32R))

        @block.sync
        def _(sp):
            sp.dma_start(wrows[0:48, :], d["gd_conv_w"][one].rearrange("o j (t p) -> (o j t) p", p=P)
                         ).then_inc(sig["rows_loaded"], 16)
            for at, name in ((48, "norm1_w"), (56, "norm2_w")):
                sp.dma_start(wrows[at:at + KT, :], d[name][one].rearrange("o (k p) -> (o k) p", p=P)
                             ).then_inc(sig["rows_loaded"], 16)
            sp.dma_start(bufs[0:OLD, :], d["state_gdn_conv"][one].rearrange("o b j n -> (o b j) n")
                         ).then_inc(sig["stored_rows_loaded"], 16)
            w = d["w_in"]
            with sp.Fori(0, 3) as j:
                for k in range(KT):
                    slabs.load(sp, k, j, rows_of(w, one, k, bass.ds(j * 512 + GD_QKV, 512)))
            for key, name, n in (("ibias", "ml_i_bias", 4), ("fbias", "ml_f_bias", 4), ("negA", "gd_A_log", 4),
                                 ("dtb", "gd_dt_bias", 4), ("mlw", "ml_norm_w", 64), ("hgw", "hg_norm_w", 64),
                                 ("gdw", "gd_norm_w", 128)):
                sp.dma_start(rows[key], bc(d[name][one, :], P, n)).then_inc(sig["small_loaded"], 16)
            for n, c0 in enumerate((ML_QK, HG_QF) + tuple(c0 for _, c0, _ in FLAT)):
                for k in range(KT):
                    width = widths[3 + n]
                    slabs.load(sp, k, 3 + n, rows_of(w, one, k, slice(c0, c0 + width)), width)
            sp.wait_ge(sig["small_loaded"], 7 * 16)

        @block.tensor
        def _(pe):
            slabs.all_free(pe)
            pe.wait_ge(sig["rows_loaded"], 48)
            pe.transpose(m.bank[7][:, 0:64], wrows[0:64, :], m.c("ident", 64)[:, 0:64]).then_inc(sig["rows_turned"], 1)
            pe.wait_ge(sig["stored_rows_loaded"], 16)
            for t in range(GT):
                mm = pe.transpose(m.bank[6][:, t * OLD:(t + 1) * OLD], bufs[0:OLD, t * P:(t + 1) * P],
                                  m.c("ident", OLD)[:, 0:OLD])
            mm.then_inc(sig["stored_rows_turned"], 1)
            norm_total(pe, m, sig, sq[0])
            pe.wait_ge(sig["rstd_ln"], 2)
            feature_group(pe, m, sig, slabs, h, 0, 0, h_base=0)
            with pe.Fori(1, 3) as j:
                feature_group(pe, m, sig, slabs, h, j, j)
            for g in range(3, NF):
                feature_group(pe, m, sig, slabs, h, g, g)
            for u, (kind, what) in enumerate(units, FIRST):
                pe.wait_ge(sig["first_banks_read" if u % 4 < 2 else "last_banks_read"],
                           2 * (u // 4 * 2 + u % 2) + 2)
                if kind == "norm":
                    for half in range(2):
                        pe.wait_ge(sig["norm_squares"], 2 * what + half + 1)
                        pe.matmul(m.bank[2 * (u % 4) + half][:, :], m.c("ones"), norm_sq[half], start=True, stop=True
                                  ).then_inc(sig["bank_done"], 1)
                    continue
                n, i = what
                w2 = FLAT[n][2] // 2
                n_tok, tokens = tile_rows(i), slice(i * P, i * P + tile_rows(i))
                for k in range(KT):
                    if i == 0:
                        slabs.wait(pe, k, NF + n)
                    for half in range(2):
                        cols = slice(half * w2, (half + 1) * w2)
                        mm = three_passes(pe, m.bank[2 * (u % 4) + half][0:n_tok, 0:w2],
                                          h.highs[:, k, tokens], h.lows[:, k, tokens],
                                          slabs.highs[:, k, cols], slabs.lows[:, k, cols],
                                          k == 0, k == KT - 1)
                        if k == KT - 1:
                            mm.then_inc(sig["bank_done"], 1)
                        elif i == NT - 1 and half == 1:
                            mm.then_inc(slabs.used(k), 1)

        def evacuate(eng, copy, mine):
            read = sig[("first_banks_read", "last_banks_read")[mine]]

            def features(g, prompt, sample):
                for t in (2 * mine, 2 * mine + 1):
                    eng.wait_ge(sig["bank_done"], 8 * g + 2 * t + 1)
                    copy(prompt(t)[:, 0:HALF], m.bank[2 * t][:, 0:HALF]).then_inc(read, 1)
                    eng.wait_ge(sig["bank_done"], 8 * g + 2 * t + 2)
                    copy(prompt(t)[:, HALF:SEQ], m.bank[2 * t + 1][:, 0:SEQ - HALF])
                    copy(sample(t), m.bank[2 * t + 1][:, SEQ - HALF:HALF]).then_inc(read, 1)

            def conv(g):
                features(g, lambda t: m.gdF[:, bass.ds(4 * g + t, 1), CONV - 1:].rearrange("p a n -> p (a n)"),
                         lambda t: m.gdS[:, bass.ds(4 * g + t, 1), :, CONV - 1:].rearrange("p a b n -> p (a b) n"))

            def plain(g, to):
                features(g, lambda t: to[:, t, 0:SEQ], lambda t: to[:, t, SEQ:])

            def unit(u, i, place, w2):
                if (u % 4) // 2 != mine:
                    return
                n = tile_rows(i)
                for half in range(2):
                    eng.wait_ge(sig["bank_done"], 2 * u + half + 1)
                    copy(m.tokp[0:n, i, place, half * w2:(half + 1) * w2], m.bank[2 * (u % 4) + half][0:n, 0:w2]
                         ).then_inc(read, 1)

            return conv, plain, unit

        def stream(eng, split, copy, mine, convolve, norm, behind):
            conv, plain, unit = evacuate(eng, copy, mine)
            mine_behind = 1 - mine

            def step(g, evac):
                for k in range(6):
                    split(k, g + 1)
                evac(g)
                split(6, g + 1)
                split(7, g + 1, (sig["bank_done"], 8 * g + 8))

            def convolving_step(g, evac):
                width, t = widths[g + 1], (g - 3) * PER
                for k in range(6):
                    split(k, g + 1, width=width)
                    if 0 <= k - mine_behind < PER:
                        convolve(t + k - mine_behind)
                evac(g)
                split(6, g + 1, width=width)
                split(7, g + 1, (sig["bank_done"], 8 * g + 8), width)

            def deltanet():
                with eng.Fori(0, 2) as g:
                    step(g, conv)
                step(2, conv)

            def others():
                convolving_step(3, lambda g: plain(g, m.mlF))
                convolving_step(4, lambda g: plain(g, m.hgF))
                norm(None, -1)
                for u, (kind, what) in enumerate(units, FIRST):
                    if kind == "norm":
                        norm(u, what)
                        continue
                    n, i = what
                    place, _, width = FLAT[n]
                    if i == NT - 1 and n + 1 < len(FLAT):
                        for k in range(7):
                            split(k, NF + n + 1, width=widths[NF + n + 1])
                    unit(u, i, place, width // 2)
                    if 2 * PER + NT * n + i < GT:
                        convolve(2 * PER + NT * n + i)
                    behind(n, i)
                    if i == NT - 1 and n + 1 < len(FLAT):
                        split(7, NF + n + 1, (sig["bank_done"], 2 * last_unit(n) + 2), widths[NF + n + 1])

            return deltanet, others

        @block.scalar
        def _(act):
            def convolve(t):
                b = t % 2
                act.wait_ge(sig[f"conv{b}"], t // 2 * 4 + 4)
                act.activation(m.gdF[:, t, CONV - 1:], acc[b], ACT.Silu).then_inc(sig[f"conv{b}_stored"], 1)

            def norm(u, a):
                for half in range(2) if a >= 0 else ():
                    act.wait_ge(sig["bank_done"], 2 * u + half + 1)
                    act.activation(norm_sq[half], m.bank[2 * (u % 4) + half][:, :], ACT.Ln, bias=EPS
                                   ).then_inc(sig["first_banks_read"], 1)
                for half in range(2) if a >= 0 else ():
                    act.wait_ge(sig["first_banks_read"], 2 * (u // 4 * 2) + 4 + half + 1)
                    act.activation(norm_sq[half], norm_sq[half], ACT.Exp, scale=-0.5).then_inc(sig["inverse_norm"], 1)
                squares(a + 1)

            def activations(n, i):
                if (n, i) == (0, 2):
                    act.wait_ge(sig["first_banks_read"], 4 + 4 * NF)
                    act.wait_ge(sig["last_banks_read"], 4 + 4 * NF)
                    act.activation(m.hgF[:, 0:2, :], m.hgF[:, 0:2, :], ACT.Silu)
                    act.activation(m.hgF[:, 2:4, :], m.hgF[:, 2:4, :], ACT.Sigmoid)
                elif i == 1 and n > 0:
                    act.wait_ge(sig["first_banks_read"], banks_read(False, n - 1))
                    act.wait_ge(sig["last_banks_read"], banks_read(True, n - 1))
                    if n == 1:
                        x = m.tokp[:, :, 1, 0:H * DKG]
                        act.activation(x, x, ACT.Silu).then_inc(sig["gates_silu"], 1)
                    else:
                        x = m.tokp[:, :, 0, O0:O0 + H * DKM]
                        act.activation(x, x, ACT.Sigmoid)

            def squares(a):
                if 2 * a >= 2 * H:
                    return
                for half in range(2):
                    if a > 0:
                        act.wait_ge(sig["normed"], 2 * a - 1 + half)
                    act.activation(norm_sq[half], m.gdF[:, 2 * a + half, CONV - 1:], ACT.Square
                                   ).then_inc(sig["norm_squares"], 1)

            def high(k, n, freed=None, width=512):
                slabs.high(act, k, n, width, freed)

            act.sem_inc(sig["first_banks_read"], 4)
            nc.scalar.preload_act_table_set(EXP_LN)
            for k in range(KT):
                norm_square(act, m, sig, k, sq[k])
            slabs.high(act, 0, 0)
            slabs.high(act, 1, 0)
            norm_rstd(act, m, sig, rstd)
            for k in range(KT):
                h.high(act, k)
                if k + 2 < KT:
                    slabs.high(act, k + 2, 0)
            deltanet, others = stream(act, high, act.copy, 0, convolve, norm, activations)
            deltanet()
            act.wait_ge(sig["last_taken"], 2)
            others()
            act.wait_ge(sig["tap_added"], CONV - 1)
            act.activation(m.gdC.rearrange("p t n -> p (t n)"), sacc.rearrange("p t b n -> p (t b n)"), ACT.Silu)

        @block.vector
        def _(dve):
            def copy(o, i):
                if len(o.shape) == 3:
                    i = i.rearrange("p (b n) -> p b n", b=NSEQ)
                return dve.tensor_copy(o, i)

            def convolve(t):
                b = t % 2
                if t >= 2:
                    dve.wait_ge(sig[f"conv{b}_stored"], t // 2)
                for tap in range(CONV):
                    src, w = m.gdF[:, t, tap:tap + SEQ], taps[:, tap, t:t + 1]
                    if tap == 0:
                        dve.tensor_scalar(acc[b], src, w, None, ALU.mult).then_inc(sig[f"conv{b}"], 1)
                    else:
                        dve.wait_ge(sig[f"conv{b}"], t // 2 * 4 + tap)
                        dve.scalar_tensor_tensor(out=acc[b], in0=src, scalar=w, in1=acc[b],
                                                 op0=ALU.mult, op1=ALU.add).then_inc(sig[f"conv{b}"], 1)

            def norm(u, a):
                for half in range(2) if a >= 0 else ():
                    t = 2 * a + half
                    dve.wait_ge(sig["inverse_norm"], t + 1)
                    x = m.gdF[:, t, CONV - 1:]
                    dve.scalar_tensor_tensor(out=x, in0=x, scalar=DKG ** -0.5 if t < H else 1.0, in1=norm_sq[half],
                                             op0=ALU.mult, op1=ALU.mult).then_inc(sig["normed"], 1)

            def low(k, n, freed=None, width=512):
                slabs.low(dve, k, n, width)

            slabs.all_split(dve)
            dve.wait_ge(sig["rows_turned"], 1)
            dve.tensor_copy(m.colw, m.bank[7][:, 0:64]).then_inc(sig["colw_ready"], 1)
            for k in range(2, KT + 1):
                norm_sum(dve, m, sig, k, sq)
            dve.wait_ge(sig["stored_rows_turned"], 1)
            dve.tensor_copy(m.gdS[:, :, :, 0:CONV - 1],
                            m.bank[6][:, 0:GT * OLD].rearrange("p (t b j) -> p t b j", t=GT, b=NSEQ)
                            ).then_inc(sig["rows_placed"], 1)
            dve.wait_ge(sig["rows_placed"], 1)
            dve.sem_inc(sig["last_banks_read"], 4)
            slabs.low(dve, 0, 0)
            slabs.low(dve, 1, 0)
            dve.wait_ge(sig["colw_ready"], 1)
            norm_apply(dve, m, sig, h, m.colw[:, 48:56], rstd, lambda k: slabs.low(dve, k + 2, 0) if k + 2 < KT else None)
            deltanet, others = stream(dve, low, copy, 1, convolve, norm, lambda n, i: None)
            deltanet()
            dve.wait_ge(sig["first_banks_read"], 16)
            dve.wait_ge(sig["last_banks_read"], 16)
            dve.wait_ge(sig["window_empty"], 1)
            others()

        @block.gpsimd
        def _(pool):
            pool.memset(m.gdF[:, :, 0:CONV - 1], 0.0).then_inc(sig["window_empty"], 1)
            pool.wait_ge(sig["first_banks_read"], 16)
            pool.wait_ge(sig["last_banks_read"], 16)
            pool.tensor_copy(last[:, :, 0:3], m.gdF[:, :, SEQ:SEQ + 3]).then_inc(sig["last_taken"], 1)
            for t in range(GT):
                cp = pool.tensor_copy(last[:, t, 3:27].rearrange("p (b j) -> p b j", b=NSEQ), m.gdS[:, t, :, DSEQ:])
            cp.then_inc(sig["last_taken"], 1)
            pool.wait_ge(sig["rows_placed"], 1)
            for j in range(CONV):
                wj = bc(taps[:, j, :].unsqueeze(2).unsqueeze(3), P, GT, NSEQ, DSEQ)
                dst = sacc if j == 0 else stmp
                if j > 1:
                    pool.wait_ge(sig["tap_added"], j - 1)
                pool.tensor_tensor(dst, m.gdS[:, :, :, j:j + DSEQ], wj, ALU.mult).then_inc(sig["tap_scaled"], 1)
                if j > 0:
                    pool.wait_ge(sig["tap_scaled"], j + 1)
                    if j > 1:
                        pool.wait_ge(sig["tap_added"], j - 1)
                    pool.tensor_tensor(sacc, sacc, stmp, ALU.add).then_inc(sig["tap_added"], 1)
            pool.wait_ge(sig["small_loaded"], 7 * 16)
            pool.wait_ge(sig["gates_silu"], 1)
            for i in range(NT):
                g = m.tokp[:, i, 1, 0:H * DKG].rearrange("p (h n) -> p h n", h=H)
                pool.tensor_tensor(g, g, bc(rows["gdw"].unsqueeze(1), P, H, DKG), ALU.mult)


def prep_phase(nc, m, d, l):
    one = bass.ds(l, 1)
    last = m.last
    m.top = m.arena + 6 * H * P
    fy, ab = m.take(NT, 8), m.take(NT, 8)
    pos = m.take(NT, 4)
    lastT = m.take(GT * P)
    rows = layer_rows(m)
    with phase(nc) as (sig, block):
        @block.sync
        def _(sp):
            sp.wait_ge(sig["last_ready"], 3)
            sp.dma_start(d["p_conv"][one].rearrange("o b j n -> (o b j) n"), lastT[0:3, :]
                         ).then_inc(sig["last_stored"], 16)
            sp.dma_start(d["s_conv"][one].rearrange("o b j n -> (o b j) n"), lastT[3:27, :]
                         ).then_inc(sig["last_stored"], 16)
            sp.wait_ge(sig["last_stored"], 32)

        @block.tensor
        def _(pe):
            for t in range(GT):
                mm = pe.transpose(m.bank[1 + t // 4][0:27, (t % 4) * P:(t % 4 + 1) * P], last[:, t, :], m.c("ident"))
                if t % 4 == 3:
                    mm.then_inc(sig["last_turned"], 1)

        @block.gpsimd
        def _(pool):
            pool.tensor_copy(m.lbl, m.lb[:, bass.ds(l * 2, 2)])
            for s in (m.S_gd, m.C_ml, m.S_hg, m.m_ml):
                pool.memset(s, 0.0)
            pool.memset(m.view(m.arena, 6 * H * P), 0.0)
            pool.wait_ge(sig["gates_silu"], 1)
            for i in range(0, NT, 2):
                g = m.tokp[:, i, 2, OG2:OG2 + H * DKH].rearrange("p (h n) -> p h n", h=H)
                pool.tensor_tensor(g, g, bc(rows["hgw"].unsqueeze(1), P, H, DKH), ALU.mult)

        @block.vector
        def _(dve):
            t0 = m.tokp
            dve.tensor_tensor(m.gates[:, :, LI:LI + 4], t0[:, :, 0, I0:I0 + 4],
                              bc(rows["ibias"].unsqueeze(1), P, NT, 4), ALU.add)
            dve.tensor_tensor(fy[:, :, 0:4], t0[:, :, 0, F0:F0 + 4], bc(rows["fbias"].unsqueeze(1), P, NT, 4),
                              ALU.add).then_inc(sig["fy_ready"], 1)
            dve.tensor_tensor(fy[:, :, 4:8], t0[:, :, 1, A1:A1 + 4], bc(rows["dtb"].unsqueeze(1), P, NT, 4),
                              ALU.add).then_inc(sig["fy_ready"], 1)
            dve.wait_ge(sig["fy_ready"], 2)
            dve.scalar_tensor_tensor(out=ab, in0=fy, scalar=-1.0, in1=fy, op0=ALU.mult, op1=ALU.max
                                     ).then_inc(sig["fy_abs"], 1)
            dve.tensor_scalar(m.gates[:, :, LF:LF + 4], fy[:, :, 0:4], 0.0, None, ALU.min).then_inc(sig["fy_clipped"], 1)
            dve.tensor_scalar(pos, fy[:, :, 4:8], 0.0, None, ALU.max).then_inc(sig["fy_clipped"], 1)
            for g in range(3):
                dve.wait_ge(sig["last_turned"], g + 1)
                dve.tensor_copy(lastT[0:27, g * 512:(g + 1) * 512], m.bank[1 + g][0:27, :]
                                ).then_inc(sig["last_ready"], 1)
            for i in range(1, NT, 2):
                dve.wait_ge(sig["gates_silu"], 1)
                g = m.tokp[:, i, 2, OG2:OG2 + H * DKH].rearrange("p (h n) -> p h n", h=H)
                dve.tensor_tensor(g, g, bc(rows["hgw"].unsqueeze(1), P, H, DKH), ALU.mult)
            dve.wait_ge(sig["decay_rates"], 1)
            dve.tensor_scalar(rows["negA"], rows["negA"], -1.0, None, ALU.mult).then_inc(sig["rates_negated"], 1)
            dve.wait_ge(sig["fy_ln"], 2)
            dve.wait_ge(sig["fy_clipped"], 2)
            dve.tensor_tensor(m.gates[:, :, LF:LF + 4], m.gates[:, :, LF:LF + 4], ab[:, :, 0:4], ALU.subtract)
            dve.tensor_tensor(pos, pos, ab[:, :, 4:8], ALU.add).then_inc(sig["softplus"], 1)
            dve.wait_ge(sig["softplus"], 1)
            dve.wait_ge(sig["rates_negated"], 1)
            dve.tensor_tensor(m.gates[:, :, GG:GG + 4], pos, bc(rows["negA"].unsqueeze(1), P, NT, 4), ALU.mult)

        @block.scalar
        def _(act):
            g2 = m.tokp[:, :, 2, OG2:OG2 + H * DKH]
            act.activation(g2, g2, ACT.Silu).then_inc(sig["gates_silu"], 1)
            act.activation(m.gates[:, :, BETA:BETA + 4], m.tokp[:, :, 1, B1:B1 + 4], ACT.Sigmoid)
            nc.scalar.preload_act_table_set(EXP_LN)
            act.activation(rows["negA"], rows["negA"], ACT.Exp).then_inc(sig["decay_rates"], 1)
            act.wait_ge(sig["fy_abs"], 1)
            act.activation(ab, ab, ACT.Exp, scale=-1.0).then_inc(sig["fy_ln"], 1)
            act.wait_ge(sig["fy_ln"], 1)
            act.activation(ab, ab, ACT.Ln, bias=1.0).then_inc(sig["fy_ln"], 1)


def sample_states(m):
    m.top = m.gdF_at
    st = {"S_gd": m.take(H, NSEQ, DKG), "C_ml": m.take(2, NSEQ, DKM + 1), "S_hg": m.take(2, NSEQ, DKH),
          "m_ml": m.take(H, NSEQ)}
    assert m.top <= m.gdC_at
    return st


def load_states(sp, m, d, l, st, sig):
    one = bass.ds(l, 1)
    for h in range(H):
        sp.dma_start(st["m_ml"][:, h, :], bc(d["state_mlstm_m"][one, :, h], P, NSEQ)
                     ).then_inc(sig["m_loaded"], 16)
    for h in range(H):
        sp.dma_start(st["S_gd"][:, h], d["state_gdn_S"][one, :, h].rearrange("o b k v -> k (o b) v")
                     ).then_inc(sig["S_gd_loaded"], 16)
    for h in range(H):
        half, pair = slice(64 * (h % 2), 64 * (h % 2) + 64), h // 2
        sp.dma_start(st["C_ml"][half, pair, :, 0:DKM], d["state_mlstm_C"][one, :, h].rearrange("o b k v -> k (o b) v")
                     ).then_inc(sig["C_loaded"], 16)
        sp.dma_start(st["C_ml"][half, pair, :, DKM:],
                     d["state_mlstm_n"][one, :, h].rearrange("o b (k x) -> k (o b) x", x=1)
                     ).then_inc(sig["C_loaded"], 16)
        sp.dma_start(st["S_hg"][half, pair], d["state_hgrn_S"][one, :, h].rearrange("o b k v -> k (o b) v")
                     ).then_inc(sig["S_hg_loaded"], 16)


STORES = 16 * (4 * H + 1)


def store_states(sp, m, d, l, st, who, last_m, sig):
    one = bass.ds(l, 1)
    for h in range(H):
        half, pair = slice(64 * (h % 2), 64 * (h % 2) + 64), h // 2
        sp.dma_start(d[who + "_S"][one, :, h].rearrange("o b k v -> k (o b) v"), st["S_gd"][:, h]
                     ).then_inc(sig["state_stored"], 16)
        sp.dma_start(d[who + "_C"][one, :, h].rearrange("o b k v -> k (o b) v"),
                     st["C_ml"][half, pair, :, 0:DKM]).then_inc(sig["state_stored"], 16)
        sp.dma_start(d[who + "_n"][one, :, h].rearrange("o b (k x) -> k (o b) x", x=1),
                     st["C_ml"][half, pair, :, DKM:]).then_inc(sig["state_stored"], 16)
        sp.dma_start(d[who + "_H"][one, :, h].rearrange("o b k v -> k (o b) v"), st["S_hg"][half, pair]
                     ).then_inc(sig["state_stored"], 16)
    sp.dma_start(d[who + "_m"][one].rearrange("o b h -> (o b) h"), last_m
                 ).then_inc(sig["state_stored"], 16)


HALVES = tuple((odd, slice(64 * odd, 64 * odd + 64)) for odd in range(2))


def chunk_phase(nc, m, st, nseq, c, d=None, l=None, prompt=None):
    sample = c is None
    L = DSEQ if sample else P
    T = nseq * L
    nl = 2 if sample else LEVELS
    W = H * T
    tile = NT - 1 if sample else None
    upto = m.c("upto_s" if sample else "upto", T)[:, 0:T]
    same = m.c("same_s" if sample else "ones", T)[:, 0:T]
    endsel = m.c("end_s" if sample else "end", T)[:, 0:T]
    ident = m.c("ident", T)[:, 0:T]
    ones = m.c("ones")
    rows = layer_rows(m)

    def low(lv):
        return m.c(f"low{lv}", T)[:, 0:T]

    def up(lv):
        return m.c(f"up{lv}", T)[:, 0:T]

    def heads(ap, n=None):
        return ap.rearrange("p (h n) -> p h n", h=H)

    def over_heads(mask):
        return bc(mask.unsqueeze(1), mask.shape[0], H, mask.shape[1])

    def per_head(col, n):
        return bc(col.unsqueeze(2), col.shape[0], H, n)

    m.top = m.arena
    padded = m.take(6, H, T)
    mq, mqw, hq, hqe = (padded[:, i] for i in range(4))
    lq = [padded[:, 4], padded[:, 5]]
    t4 = lambda: m.take(H, T)
    tv = lambda: m.take(H, DKG)
    kn, qn, EA, EB, X, Y, kd, qd, edb = (t4() for _ in range(9))
    A = EA
    at = m.top
    AM = [t4(), t4()]
    first = m.top
    m.take(5, H * DKG)
    spot = lambda i, n: m.view(first + i * H * DKG, H, n)
    sqk, r = spot(0, T), spot(0, DKG)
    sqq, u = spot(1, T), spot(1, DKG)
    p1 = spot(2, T)
    ug, og = spot(3, T), m.view(first + 3 * H * DKG, H * DKG)
    Dg, kdec = spot(4, T), spot(4, DKG)
    vS = t4()
    gates = m.take(16)
    dcol, ddc, kfac, msg, nbeta = m.take(12), m.take(4), m.take(4), m.take(4), m.take(4)
    hk, bH, hlf, hkd, mk = (m.take(2, T) for _ in range(5))
    hkdT, mks = (m.take(2 * P), m.take(2 * P)) if sample else \
        (a.rearrange("p x t -> p (x t)") for a in (hkd, mk))
    lev = m.take(nl, 2, T)
    lk = [m.take(2, T) for _ in range(2)]
    hacc, htmp = t4(), [t4(), t4()]
    hms, hog = m.take(4), m.take(H * DKH)
    vext = m.take(H, DKM + 1)
    ua, ma, M, mW = t4(), t4(), t4(), t4()
    wexp = t4()
    bcol, acol, gend, emt, den, mms, kw = (m.take(12 if i == 0 else 4) for i in range(7))
    mog = m.take(H * DKM)
    m_sq = m.take(H * DKM) if sample else hlf.rearrange("p x t -> p (x t)")
    lbm, lbn = m.take(2), m.take(2)
    mix = m.take(MIX) if sample else m.view(at, MIX)
    if sample:
        kx, qx = m.take(H, nseq, T), m.take(H, nseq, T)
        hqx, mqx = m.take(H, nseq, T), m.take(H, nseq, T)
        ux = [m.take(nseq, DKG) for _ in range(H)]
        hx = m.view(m.tokp_at + 2 * nseq * DKG, H, nseq, DKH)
        vx = m.view(m.tokp_at + 2 * nseq * DKG + H * nseq * DKH, H, nseq, DKM + 1)
        seqcol = m.c("seq_of_column").rearrange("p (b t) -> p b t", b=nseq)
        seqrow = m.c("seq_of_row", T)
    else:
        kx, qx, hqx, mqx = kd, qd, hqe, mqw
    M0, M1, H0, H1, G0, G1, G2, G3 = m.bank

    if sample:
        gt = lambda a, z: m.gdC[:, a:z, :]
        mlF, hgF = (lambda a, z: m.mlF[:, a:z, SEQ:]), (lambda a, z: m.hgF[:, a:z, SEQ:])
        tk = lambda g, a, z: m.tokp[0:T, tile, g, a:z]
        gates_src = m.gates[0:T, tile, :]
        hTc = m.hT[:, :, SEQ:]
    else:
        gt = lambda a, z: m.gdF[:, a:z, bass.ds(c * P + (CONV - 1), P)]
        mlF = lambda a, z: m.mlF[:, a:z, bass.ds(c * P, P)]
        hgF = lambda a, z: m.hgF[:, a:z, bass.ds(c * P, P)]
        tk = lambda g, a, z: m.tokp[:, bass.ds(c, 1), g, a:z].rearrange("p o n -> p (o n)")
        gates_src = m.gates[:, bass.ds(c, 1), :].rearrange("p o n -> p (o n)")
        hTc = m.hT[:, :, bass.ds(c * P, P)]
    if not sample:
        qn = gt(0, 4)
    li, lf, gg, beta = (gates[0:T, a:a + 4] for a in (LI, LF, GG, BETA))
    pair_of = lambda h: (slice(64 * (h % 2), 64 * (h % 2) + 64), h // 2)

    def flat(ap):
        return ap.rearrange("p h t -> p (h t)")

    def seqs(ap):
        return ap.rearrange("p x (b j) -> p x b j", b=nseq)

    mcol = m.mcol_s if sample else m.mcol
    with phase(nc) as (sig, block):
        if sample:
            @block.sync
            def _(sp):
                load_states(sp, m, d, l, st, sig)
                store_states(sp, m, d, l, prompt, "p", m.mcol[P - 1:P, :], sig)
                sp.wait_ge(sig["state_stored"], STORES)

        @block.scalar
        def _(act):
            def rstd(ms, n, ready, name):
                act.wait_ge(sig[ready], H)
                act.activation(ms, ms, ACT.Ln, scale=1.0 / n, bias=EPS).then_inc(sig[name], 1)
                act.wait_ge(sig[name], 1)
                act.activation(ms, ms, ACT.Exp, scale=-0.5).then_inc(sig[name], 1)

            def head_squares(sq, src, ms, name):
                for h in range(H):
                    act.activation(sq[:, h], src[:, h], ACT.Square, accum_out=ms[:, h:h + 1]
                                   ).then_inc(sig[name + "_ms"], 1)

            def norm(i):
                b, sq = ((G0, sqk), (G1, sqq))[i]
                act.wait_ge(sig["norm_sums"], i + 1)
                act.activation(flat(sq), b[:, 0:W], ACT.Ln, bias=EPS).then_inc(sig["norm_ln"], 1)
                act.wait_ge(sig["norm_ln"], i + 1)
                act.activation(flat(sq), flat(sq), ACT.Exp, scale=-0.5).then_inc(sig["norm_ready"], 1)

            act.copy(gates[0:T, :], gates_src).then_inc(sig["gates_taken"], 1)
            if sample:
                act.activation(sqk, gt(4, 8), ACT.Square).then_inc(sig["squares"], 1)
                act.activation(sqq, gt(0, 4), ACT.Square).then_inc(sig["squares"], 1)
            else:
                act.copy(kn, gt(4, 8)).then_inc(sig["gd_kn"], 1)
            act.wait_ge(sig["f_ready"], 1)
            act.activation(hlf, hlf, ACT.Ln).then_inc(sig["logf"], 1)
            if sample:
                norm(0)
            act.wait_ge(sig["gd_Dmax"], 1)
            act.activation(EA[0:T], EA[0:T], ACT.Exp, scale=-1.0).then_inc(sig["gd_EA"], 1)
            act.wait_ge(sig["gd_Dmin"], 1)
            act.activation(EB[0:T], EB[0:T], ACT.Exp).then_inc(sig["gd_EB"], 1)
            if sample:
                norm(1)
            act.activation(flat(edb), G2[:, 0:W], ACT.Exp).then_inc(sig["gd_edb"], 1)
            act.wait_ge(sig["gd_dd"], 1)
            act.activation(kfac[0:T], ddc[0:T], ACT.Exp).then_inc(sig["gd_kfac"], 1)
            if sample:
                act.wait_ge(sig["padding"], 1)
            for odd, half in HALVES:
                act.copy(hq[half, odd::2, :], hgF(0, 2)[half]).then_inc(sig["hg_q"], 1)
            act.wait_ge(sig["ml_arows"], 1)
            act.copy(flat(ma), M0[:, 0:W]).then_inc(sig["ml_a_taken"], 1)
            act.wait_ge(sig["gd_X0"], 1)
            act.copy(flat(X[0:T]), G2[0:T, 0:W]).then_inc(sig["X_ready"], 1)
            act.mul(mk, mlF(2, 4), DKM ** -0.5).then_inc(sig["ml_k"], 1)
            for odd, half in HALVES:
                act.copy(mq[half, odd::2, :], mlF(0, 2)[half]).then_inc(sig["ml_q"], 1)
            def inverse(lv):
                if lv > 1:
                    act.wait_ge(sig["X_turned"], lv - 1)
                    act.copy(flat(Y[0:T]), G2[0:T, 0:W]).then_inc(sig["Y_taken"], 1)
                act.wait_ge(sig["inv_p1"], lv)
                act.copy(flat(p1[0:T]), G0[0:T, 0:W]).then_inc(sig["inv_p1_taken"], 1)

            def hg_decays():
                act.wait_ge(sig["lev"], 2 * nl)
                act.activation(lev, lev, ACT.Exp).then_inc(sig["lev_ready"], 1)
                act.wait_ge(sig["hg_dl"], 1)
                act.activation(bH, bH, ACT.Exp).then_inc(sig["hg_eb"], 1)
                act.activation(hkd, hkd, ACT.Exp, scale=-1.0).then_inc(sig["hg_ekd"], 1)
                act.mul(vS, gt(8, 12), -1.0).then_inc(sig["v_taken"], 1)

            def decayed_keys():
                act.wait_ge(sig["k_turned"], 1)
                act.wait_ge(sig["gd_kfac"], 1)
                for h in range(H):
                    act.activation(kdec[0:T, h], G3[0:T, h * DKG:(h + 1) * DKG], ACT.Copy, scale=kfac[0:T, h:h + 1]
                                   ).then_inc(sig["gd_kdec"], 1)

            def ml_weights():
                act.wait_ge(sig["ml_D"], 2)
                act.activation(mW[0:T], mW[0:T], ACT.Exp, scale=-1.0).then_inc(sig["ml_E"], 1)
                act.wait_ge(sig["ml_wD"], 1)
                act.activation(wexp, wexp, ACT.Exp, scale=-1.0).then_inc(sig["ml_wexp"], 1)

            inverse(1)
            hg_decays()
            if nl > 2:
                inverse(2)
            decayed_keys()
            ml_weights()
            for lv in range(3, nl):
                inverse(lv)
            act.wait_ge(sig["ml_kwD"], 1)
            act.activation(kw[0:T], kw[0:T], ACT.Exp).then_inc(sig["ml_kw"], 1)
            act.wait_ge(sig["ml_mt"], 1)
            act.activation(emt[0:T], mcol[0:T, :], ACT.Exp, scale=-1.0).then_inc(sig["ml_emt"], 1)
            act.wait_ge(sig["gd_u"], 1)
            act.copy(flat(u[0:T]), G1[0:T, :]).then_inc(sig["u_ready"], 1)
            act.wait_ge(sig["hg_k_turned"], 1)
            act.copy(hkdT[0:T, :], H1[0:T, 0:2 * P]).then_inc(sig["hg_kT"], 1)
            act.wait_ge(sig["ml_h"], H)
            head_squares(heads(m_sq[0:T, :]), heads(mog[0:T, :]), mms[0:T], "ml")
            rstd(mms[0:T], DKM, "ml_ms", "ml_rstd")
            act.wait_ge(sig["gd_o"], 1)
            head_squares(heads(og[0:T, :]), heads(G2[0:T, :]), msg[0:T], "gd")
            rstd(msg[0:T], DKG, "gd_ms", "gd_rstd")
            act.wait_ge(sig["hg_o"], 1)
            head_squares(heads(hog[0:T, :]), heads(H0[0:T, 0:H * DKH]), hms[0:T], "hg")
            rstd(hms[0:T], DKH, "hg_ms", "hg_rstd")
            act.wait_ge(sig["mix_turned"], 1)
            act.copy(hTc[:, 2:6, :], M1[:, 0:W].rearrange("p (k t) -> p k t", k=4))

        @block.gpsimd
        def _(pool):
            def mul(out, a, b):
                return pool.tensor_tensor(out, a, b, ALU.mult)

            def blocks(lv):
                pool.wait_ge(sig["gd_A"], H)
                if lv > 2:
                    pool.wait_ge(sig["inv_p1"], lv - 2)
                mul(AM[lv % 2][0:T], A[0:T], over_heads(low(lv))).then_inc(sig["AM_ready"], 1)

            if sample:
                pool.memset(padded, 0.0).then_inc(sig["padding"], 1)
                pool.wait_ge(sig["padding"], 1)
            pool.wait_ge(sig["gates_taken"], 1)
            mul(ug[0:T], over_heads(upto), per_head(gg, T)).then_inc(sig["gd_ug"], 1)
            pool.wait_ge(sig["ml_acol"], 1)
            mul(ua[0:T], over_heads(ident), per_head(acol[0:T], T)).then_inc(sig["ml_ua_ready"], 1)
            pool.wait_ge(sig["gd_EB"], 1)
            mul(EB[0:T], EB[0:T], over_heads(upto)).then_inc(sig["gd_EBm"], 1)
            blocks(1)
            if nl > 2:
                blocks(2)
            pool.tensor_copy(vext[0:T, :, 0:DKM], heads(tk(0, V0, V0 + H * DKM))).then_inc(sig["ml_v"], 1)
            pool.memset(vext[0:T, :, DKM:], 1.0).then_inc(sig["ml_v"], 1)
            if sample:
                pool.wait_ge(sig["ml_v"], 2)
            pool.wait_ge(sig["gd_edb"], 1)
            pool.wait_ge(sig["gd_kn"], 1)
            mul(kd, kn, edb).then_inc(sig["gd_kd"], 1)
            if sample:
                pool.wait_ge(sig["gd_qn"], 1)
            mul(qd, qn, edb).then_inc(sig["gd_qd"], 1)
            if sample:
                pool.wait_ge(sig["gd_kd"], 1)
                pool.wait_ge(sig["gd_qd"], 1)
                for h in range(H):
                    mul(kx[:, h], bc(kd[:, h].unsqueeze(1), P, nseq, T), seqcol)
                    x = mul(qx[:, h], bc(qd[:, h].unsqueeze(1), P, nseq, T), seqcol)
                x.then_inc(sig["gd_x"], 1)
                pool.wait_ge(sig["gd_x"], 1)

            def ml_mask():
                pool.wait_ge(sig["ml_E"], 1)
                mul(mW[0:T], mW[0:T], over_heads(upto)).then_inc(sig["ml_W"], 1)

            for s in range(1, nl + 1):
                if 2 < s + 2 < nl:
                    blocks(s + 2)
                pool.wait_ge(sig["hg_masked"], s + 1)
                if s > 1:
                    pool.wait_ge(sig["hg_sum"], s - 1)
                pool.tensor_tensor(hacc[0:T], hacc[0:T], htmp[s % 2][0:T], ALU.add).then_inc(sig["hg_sum"], 1)
                if s == 2:
                    ml_mask()
            if sample:
                pool.wait_ge(sig["ml_W"], 1)
                pool.wait_ge(sig["hg_qe"], 2)
                pool.wait_ge(sig["ml_qw"], 2)
                for j in range(H):
                    mul(hqx[:, j], bc(hqe[:, j].unsqueeze(1), P, nseq, T), seqcol)
                    x = mul(mqx[:, j], bc(mqw[:, j].unsqueeze(1), P, nseq, T), seqcol)
                x.then_inc(sig["qx_ready"], 1)
                pool.wait_ge(sig["qx_ready"], 1)
                for h in range(H):
                    mul(hx[0:T, h], bc(tk(2, I2 + h * DKH, I2 + (h + 1) * DKH).unsqueeze(1), T, nseq, DKH),
                        bc(seqrow.unsqueeze(2), T, nseq, DKH))
                    x = mul(vx[0:T, h], bc(vext[0:T, h].unsqueeze(1), T, nseq, DKM + 1),
                            bc(seqrow.unsqueeze(2), T, nseq, DKM + 1))
                x.then_inc(sig["values_spread"], 1)

                pool.wait_ge(sig["u_ready"], 1)
                for h in range(H):
                    mul(ux[h][0:T], bc(u[0:T, h].unsqueeze(1), T, nseq, DKG),
                        bc(seqrow.unsqueeze(2), T, nseq, DKG)).then_inc(sig["u_spread"], 1)

        @block.vector
        def _(dve):
            def tt(out, a, b, op):
                return dve.tensor_tensor(out, a, b, op)

            def mul(out, a, b):
                return dve.tensor_tensor(out, a, b, ALU.mult)

            dve.tensor_scalar(lbm, m.lbl, -1.0, 1.0, ALU.mult, ALU.add).then_inc(sig["lb_rest"], 1)
            dve.tensor_scalar(lbn, m.lbl, 1.0, None, ALU.subtract).then_inc(sig["lb_rest"], 1)
            dve.wait_ge(sig["lb_rest"], 2)
            for j in range(2):
                z = hgF(2 + j, 3 + j).rearrange("p a t -> p (a t)")
                dve.tensor_scalar(hlf[:, j], z, lbm[:, j:j + 1], m.lbl[:, j:j + 1], ALU.mult, ALU.add
                                  ).then_inc(sig["f_raw"], 1)
            dve.wait_ge(sig["f_raw"], 2)
            dve.tensor_scalar(hlf, hlf, TINY, None, ALU.max).then_inc(sig["f_ready"], 1)
            dve.wait_ge(sig["ml_bcols"], 1)
            dve.tensor_copy(bcol[0:T, 0:4], M1[0:T, 0:4]).then_inc(sig["ml_b"], 1)
            dve.tensor_copy(bcol[:, 8:12], M1[:, 8:12]).then_inc(sig["ml_b"], 1)
            dve.wait_ge(sig["ml_b"], 2)
            tt(acol[0:T], li, bcol[0:T, 0:4], ALU.subtract).then_inc(sig["ml_acol"], 1)
            dve.tensor_scalar(nbeta[0:T], beta, -1.0, None, ALU.mult).then_inc(sig["nbeta"], 1)
            dve.wait_ge(sig["gd_dcols"], 1)
            dve.tensor_copy(dcol[0:T, 0:8], G3[0:T, 0:8]).then_inc(sig["dcol_taken"], 1)
            for j in range(2):
                z = hgF(2 + j, 3 + j).rearrange("p a t -> p (a t)")
                dve.tensor_scalar(hk[:, j], z, lbn[:, j:j + 1], lbm[:, j:j + 1], ALU.mult, ALU.add
                                  ).then_inc(sig["hg_k"], 1)
            dve.wait_ge(sig["dcol_taken"], 1)
            tt(ddc[0:T], dcol[0:T, 4:8], dcol[0:T, 0:4], ALU.subtract).then_inc(sig["gd_dd"], 1)
            if sample:
                dve.wait_ge(sig["norm_ready"], 1)
                mul(kn, gt(4, 8), sqk).then_inc(sig["gd_kn"], 1)
            dve.wait_ge(sig["gd_drows"], 1)
            tt(Dg[0:T], G2[0:T, 0:W].rearrange("p (h t) -> p h t", h=H), per_head(dcol[0:T, 0:4], T), ALU.subtract
               ).then_inc(sig["gd_D"], 1)
            dve.wait_ge(sig["gd_D"], 1)
            dve.tensor_scalar(EA[0:T], Dg[0:T], 0.0, None, ALU.max).then_inc(sig["gd_Dmax"], 1)
            dve.tensor_scalar(EB[0:T], Dg[0:T], 0.0, None, ALU.min).then_inc(sig["gd_Dmin"], 1)
            dve.wait_ge(sig["logf"], 1)
            if sample:
                dve.tensor_copy(seqs(bH)[:, :, :, 0], seqs(hlf)[:, :, :, 0]).then_inc(sig["hg_b"], 1)
                for t in range(1, L):
                    dve.wait_ge(sig["hg_b"], t)
                    tt(seqs(bH)[:, :, :, t], seqs(bH)[:, :, :, t - 1], seqs(hlf)[:, :, :, t], ALU.add
                       ).then_inc(sig["hg_b"], 1)
            else:
                for j in range(2):
                    dve.tensor_tensor_scan(bH[:, j], ones[:, 0:T], hlf[:, j], 0.0, ALU.mult, ALU.add
                                           ).then_inc(sig["hg_b"], 1)
            dve.wait_ge(sig["gd_kk"], 1)
            dve.wait_ge(sig["gd_EA"], 1)
            for h in range(H):
                dve.scalar_tensor_tensor(out=A[0:T, h], in0=G0[0:T, h * T:(h + 1) * T], scalar=beta[:, h:h + 1],
                                         in1=EA[0:T, h], op0=ALU.mult, op1=ALU.mult).then_inc(sig["gd_A"], 1)
            dve.wait_ge(sig["gd_A"], H)
            mul(Dg[0:T], A[0:T], over_heads(low(0))).then_inc(sig["gd_A0"], 1)
            dve.wait_ge(sig["gd_A0"], 1)
            tt(Y[0:T], over_heads(ident), Dg[0:T], ALU.subtract).then_inc(sig["Y_ready"], 1)
            if sample:
                dve.wait_ge(sig["norm_ready"], 2)
                dve.scalar_tensor_tensor(out=qn, in0=gt(0, 4), scalar=DKG ** -0.5, in1=sqq, op0=ALU.mult, op1=ALU.mult
                                         ).then_inc(sig["gd_qn"], 1)
            dve.wait_ge(sig["hg_b"], L if sample else 2)
            for lv in range(nl):
                if lv == nl // 2:
                    dve.wait_ge(sig["gd_kq"], 1)
                    dve.wait_ge(sig["gd_EBm"], 1)
                    mul(EB[0:T], heads(G1[0:T, 0:W]), EB[0:T]).then_inc(sig["gd_att"], 1)
                n = 1 << (lv + 1)
                v = bH.rearrange("p x (k n) -> p x k n", n=n)
                o = lev[:, lv].rearrange("p x (k n) -> p x k n", n=n)
                mid = bc(v[:, :, :, n // 2 - 1:n // 2], P, 2, T // n, n // 2)
                tt(o[:, :, :, 0:n // 2], mid, v[:, :, :, 0:n // 2], ALU.subtract).then_inc(sig["lev"], 1)
                tt(o[:, :, :, n // 2:], v[:, :, :, n // 2:], mid, ALU.subtract).then_inc(sig["lev"], 1)
            tt(seqs(hkd), seqs(bH), bc(seqs(bH)[:, :, :, L - 1:L], P, 2, nseq, L), ALU.subtract
               ).then_inc(sig["hg_dl"], 1)
            mp = st["m_ml"]

            def ml_maxima():
                dve.wait_ge(sig["ml_a_taken"], 1)
                if sample:
                    dve.wait_ge(sig["m_loaded"], 16 * H)
                    tt(seqs(M)[:, :, :, 0], seqs(ma)[:, :, :, 0], mp, ALU.max).then_inc(sig["ml_M"], 1)
                    for t in range(1, L):
                        dve.wait_ge(sig["ml_M"], t)
                        tt(seqs(M)[:, :, :, t], seqs(M)[:, :, :, t - 1], seqs(ma)[:, :, :, t], ALU.max
                           ).then_inc(sig["ml_M"], 1)
                else:
                    for h in range(H):
                        dve.tensor_tensor_scan(M[:, h], ma[:, h], ma[:, h], mp[:, h], ALU.max, ALU.max
                                               ).then_inc(sig["ml_M"], 1)
                dve.wait_ge(sig["ml_M"], 4)
                tt(mW[0:T], M[0:T], per_head(acol[0:T], T), ALU.subtract).then_inc(sig["ml_D"], 1)
                dve.wait_ge(sig["ml_D"], 1)
                dve.tensor_scalar(mW[0:T], mW[0:T], 0.0, None, ALU.max).then_inc(sig["ml_D"], 1)
                tt(seqs(wexp), seqs(M), bc(mp.unsqueeze(3), P, H, nseq, L), ALU.subtract).then_inc(sig["ml_wD"], 1)

            def ml_columns():
                last_M = M[:, :, T - 1]
                if sample:
                    mul(ma[0:T], M[0:T], over_heads(endsel)).then_inc(sig["ml_pick"], 1)
                    dve.wait_ge(sig["ml_pick"], 1)
                    dve.tensor_reduce(gend[0:T], ma[0:T], AX.X, ALU.add).then_inc(sig["ml_pick"], 1)
                    dve.wait_ge(sig["ml_pick"], 2)
                    last_M = gend[0:T]
                tt(kw[0:T], acol[0:T], last_M, ALU.subtract).then_inc(sig["ml_kwD"], 1)
                dve.wait_ge(sig["ml_Mcols"], 1)
                tt(mcol[0:T, :], M1[0:T, 16:20], bcol[0:T, 0:4], ALU.add).then_inc(sig["ml_mt"], 1)
                if not sample:
                    dve.wait_ge(sig["ml_wD"], 1)
                    tt(mp.rearrange("p h b -> p (h b)"), bcol[:, 8:12], last_M, ALU.add).then_inc(sig["m_next"], 1)

            def hg_decayed():
                dve.wait_ge(sig["hg_eb"], 1)
                for odd, half in HALVES:
                    mul(hqe[half, odd::2, :], hq[half, odd::2, :], bH[half]).then_inc(sig["hg_qe"], 1)
                dve.wait_ge(sig["hg_ekd"], 1)
                mul(hkd, hk, hkd).then_inc(sig["hg_kd"], 1)

            def ml_decayed():
                dve.wait_ge(sig["ml_wexp"], 1)
                for odd, half in HALVES:
                    mul(mqw[half, odd::2, :], mq[half, odd::2, :], wexp[half, odd::2, :]).then_inc(sig["ml_qw"], 1)

            def ml_scores():
                dve.wait_ge(sig["ml_scores"], 1)
                dve.wait_ge(sig["ml_W"], 1)
                mul(mW[0:T], heads(M0[0:T, 0:W]), mW[0:T]).then_inc(sig["ml_P"], 1)

            def delta_targets():
                dve.wait_ge(sig["gd_kS"], 1)
                mul(r[0:T], heads(G3[0:T, :]), per_head(nbeta[0:T], DKG)).then_inc(sig["gd_r"], 1)

            def ml_keys():
                dve.wait_ge(sig["ml_k_turned"], 1)
                dve.wait_ge(sig["ml_kw"], 1)
                mul(heads(mks[0:T, :]), heads(M0[0:T, 0:2 * P]), per_head(kw[0:T], DKM)).then_inc(sig["ml_ks"], 1)

            def inverse(lv):
                dve.wait_ge(sig["inv_p2"], lv)
                tt(X[0:T], X[0:T], heads(G1[0:T, 0:W]), ALU.subtract).then_inc(sig["X_ready"], 1)

            def masked(s):
                dve.wait_ge(sig["hg_scores"], s + 1)
                dst = hacc if s == 0 else htmp[s % 2]
                if s > 2:
                    dve.wait_ge(sig["hg_sum"], s - 2)
                mul(dst[0:T], heads((H0, H1)[s % 2][0:T, 0:W]), over_heads(ident if s == 0 else up(s - 1))
                    ).then_inc(sig["hg_masked"], 1)

            def level_operands(lv):
                dve.wait_ge(sig["lev_ready"], 1)
                if lv >= 2:
                    dve.wait_ge(sig["hg_scores"], lv)
                for odd, half in HALVES:
                    mul(lq[lv % 2][half, odd::2, :], hq[half, odd::2, :], lev[half, lv]).then_inc(sig["lq"], 1)
                mul(lk[lv % 2], hk, lev[:, lv]).then_inc(sig["lq"], 1)

            masked(0)
            if sample:
                inverse(1)
                level_operands(0)
                level_operands(1)
                masked(1)
                masked(2)
                ml_maxima()
                ml_columns()
                hg_decayed()
                ml_decayed()
                ml_scores()
                delta_targets()
            else:
                inverse(1)
                level_operands(0)
                ml_maxima()
                inverse(2)
                level_operands(1)
                masked(1)
                ml_columns()
                hg_decayed()
                inverse(3)
                level_operands(2)
                masked(2)
                level_operands(3)
                ml_decayed()
                inverse(4)
                masked(3)
                level_operands(4)
                masked(4)
                level_operands(5)
                inverse(5)
                masked(5)
                level_operands(6)
                delta_targets()
                masked(6)
                ml_scores()
                inverse(6)
                masked(7)
            ml_keys()
            dve.wait_ge(sig["ml_num"], 1)
            num = M1[0:T, 0:H * (DKM + 1)].rearrange("p (h n) -> p h n", h=H)
            dve.tensor_copy(den[0:T], num[:, :, DKM]).then_inc(sig["ml_den"], 1)
            dve.wait_ge(sig["ml_den"], 1)
            dve.scalar_tensor_tensor(out=den[0:T], in0=den[0:T], scalar=-1.0, in1=den[0:T], op0=ALU.mult, op1=ALU.max
                                     ).then_inc(sig["ml_den"], 1)
            dve.wait_ge(sig["ml_den"], 2)
            dve.wait_ge(sig["ml_emt"], 1)
            tt(den[0:T], den[0:T], emt[0:T], ALU.max).then_inc(sig["ml_den"], 1)
            dve.wait_ge(sig["ml_den"], 3)
            dve.reciprocal(den[0:T], den[0:T]).then_inc(sig["ml_den"], 1)
            dve.wait_ge(sig["ml_den"], 4)
            og4 = heads(tk(0, O0, O0 + H * DKM))
            for h in range(H):
                dve.scalar_tensor_tensor(out=heads(mog[0:T, :])[:, h], in0=num[:, h, 0:DKM], scalar=den[0:T, h:h + 1],
                                         in1=og4[:, h], op0=ALU.mult, op1=ALU.mult).then_inc(sig["ml_h"], 1)
            C = st["C_ml"]
            if not sample:
                dve.wait_ge(sig["ml_delta"], 1)
                for h in range(H):
                    half, j = pair_of(h)
                    dve.scalar_tensor_tensor(out=C[half, j, 0], in0=C[half, j, 0], scalar=wexp[half, h, T - 1:T],
                                             in1=M0[half, h * (DKM + 1):(h + 1) * (DKM + 1)],
                                             op0=ALU.mult, op1=ALU.add).then_inc(sig["ml_state"], 1)
            else:
                for h in range(H):
                    half, j = pair_of(h)
                    e = seqs(wexp)[half, h, :, L - 1]
                    mul(C[half, j], C[half, j], bc(e.unsqueeze(2), 64, nseq, DKM + 1)
                        ).then_inc(sig["ml_decayed"], 1)
                for h in range(H):
                    half, j = pair_of(h)
                    dve.wait_ge(sig["ml_decayed"], h + 1)
                    for q in range(2):
                        i = 2 * h + q
                        dve.wait_ge(sig["ml_delta"], i + 1)
                        b = (M0, H1)[i % 2]
                        tt(C[half, j, 4 * q:4 * q + 4], C[half, j, 4 * q:4 * q + 4],
                           b[half, 0:4 * (DKM + 1)].rearrange("p (b n) -> p b n", b=4), ALU.add
                           ).then_inc(sig["ml_state"], 1)
            def hg_state():
                Sh = st["S_hg"]
                for h in range(H):
                    half, j = pair_of(h)
                    if not sample:
                        dve.wait_ge(sig["hg_delta"], 1)
                        dve.scalar_tensor_tensor(out=Sh[half, j, 0], in0=Sh[half, j, 0], scalar=bH[half, j, T - 1:T],
                                                 in1=H1[half, h * DKH:(h + 1) * DKH], op0=ALU.mult, op1=ALU.add
                                                 ).then_inc(sig["hg_state"], 1)
                    else:
                        dve.wait_ge(sig["hg_decayed"], h + 1)
                        dve.wait_ge(sig["hg_delta"], h + 1)
                        tt(Sh[half, j], Sh[half, j], (H1, M0)[h % 2][half, :].rearrange("p (b n) -> p b n", b=nseq),
                           ALU.add).then_inc(sig["hg_state"], 1)

            if sample:
                dve.wait_ge(sig["gd_o"], 1)
                for h in range(H):
                    e = seqs(edb)[:, h, :, L - 1]
                    mul(st["S_gd"][:, h], st["S_gd"][:, h], bc(e.unsqueeze(2), P, nseq, DKG)
                        ).then_inc(sig["gd_decayed"], 1)
                S = st["S_gd"]
                for h in range(H):
                    dve.wait_ge(sig["gd_decayed"], h + 1)
                    for q in range(2):
                        i = 2 * h + q
                        dve.wait_ge(sig["gd_delta"], i + 1)
                        tt(S[:, h, 4 * q:4 * q + 4], S[:, h, 4 * q:4 * q + 4],
                           (G3, G0, G1)[i % 3][:, :].rearrange("p (b n) -> p b n", b=4), ALU.add
                           ).then_inc(sig["gd_state"], 1)
                dve.wait_ge(sig["hg_o"], 1)
                for h in range(H):
                    half, j = pair_of(h)
                    e = seqs(bH)[half, j, :, L - 1]
                    mul(st["S_hg"][half, j], st["S_hg"][half, j], bc(e.unsqueeze(2), 64, nseq, DKH)
                        ).then_inc(sig["hg_decayed"], 1)
                hg_state()

            def normed(out, src, ms, weight, name):
                dve.wait_ge(sig[name + "_rstd"], 2)
                for h in range(H):
                    dve.scalar_tensor_tensor(out=out[:, h], in0=src[:, h], scalar=ms[0:T, h:h + 1], in1=weight(h),
                                             op0=ALU.mult, op1=ALU.mult).then_inc(sig["mix"], 1)

            normed(heads(mix[0:T, 0:H * DKM]), heads(mog[0:T, :]), mms, lambda h: rows["mlw"][0:T], "ml")
            gate1 = heads(tk(1, OG1, OG1 + H * DKG))
            normed(heads(mix[0:T, H * DKM:H * (DKM + DKG)]), heads(G2[0:T, :]), msg, lambda h: gate1[:, h], "gd")
            if not sample:
                hg_state()
            gate = heads(tk(2, OG2, OG2 + H * DKH))
            normed(heads(mix[0:T, H * (DKM + DKG):]), heads(H0[0:T, 0:H * DKH]), hms, lambda h: gate[:, h], "hg")
            S = st["S_gd"]
            if not sample:
                dve.wait_ge(sig["gd_delta"], 1)
                for h in range(H):
                    dve.scalar_tensor_tensor(out=S[:, h, 0], in0=S[:, h, 0], scalar=edb[:, h, T - 1:T],
                                             in1=G3[:, h * DKG:(h + 1) * DKG], op0=ALU.mult, op1=ALU.add)
            dve.wait_ge(sig["mix_turned"], 2)
            src = M0[:, 0:W].rearrange("p (k t) -> p k t", k=4)
            dve.tensor_copy(hTc[:, 0:2, :], src[:, 0:2])
            dve.tensor_copy(hTc[:, 6:8, :], src[:, 2:4])

        @block.tensor
        def _(pe):
            def per_h(bank, width, lhs, rhs, done, n=T):
                for h in range(H):
                    mm = pe.matmul(bank[0:n, h * width:(h + 1) * width], lhs(h), rhs(h), start=True, stop=True)
                return mm.then_inc(sig[done], 1)

            def turn(bank, src, n, done):
                for k in range(n):
                    mm = pe.transpose(bank[0:T, k * P:(k + 1) * P], src[:, k, :], m.c("ident"))
                mm.then_inc(sig[done], 1)

            def turn_square(src, done):
                for h in range(H):
                    mm = pe.transpose(G2[0:T, h * T:(h + 1) * T], src[0:T, h], ident)
                mm.then_inc(sig[done], 1)

            def pairs(bank, a, b, done):
                for h in range(H):
                    mm = pe.matmul(bank[0:T, h * T:(h + 1) * T], a[:, h // 2], b[:, h], start=True, stop=True)
                mm.then_inc(sig[done], 1)

            n1 = DKM + 1
            pe.wait_ge(sig["gates_taken"], 1)
            pe.matmul(M1[:, 8:12], ones[0:T, :], lf, start=True, stop=True)
            pe.matmul(M1[0:T, 0:4], upto, lf, start=True, stop=True).then_inc(sig["ml_bcols"], 1)
            pe.matmul(G3[0:T, 0:4], upto, gg, start=True, stop=True)
            pe.matmul(G3[0:T, 4:8], same, gg, start=True, stop=True).then_inc(sig["gd_dcols"], 1)
            if sample:
                pe.wait_ge(sig["squares"], 1)
                pe.matmul(G0[:, 0:W], ones, flat(sqk), start=True, stop=True).then_inc(sig["norm_sums"], 1)
            pe.wait_ge(sig["gd_ug"], 1)
            pe.matmul(G2[:, 0:W], ones[0:T, :], flat(ug[0:T]), start=True, stop=True).then_inc(sig["gd_drows"], 1)
            if sample:
                pe.wait_ge(sig["squares"], 2)
                pe.matmul(G1[:, 0:W], ones, flat(sqq), start=True, stop=True).then_inc(sig["norm_sums"], 1)
            pe.wait_ge(sig["gd_kn"], 1)
            per_h(G0, T, lambda h: kn[:, h], lambda h: kn[:, h], "gd_kk")
            pe.wait_ge(sig["ml_ua_ready"], 1)
            pe.matmul(M0[:, 0:W], ones[0:T, :], flat(ua[0:T]), start=True, stop=True).then_inc(sig["ml_arows"], 1)
            pe.wait_ge(sig["dcol_taken"], 1)
            turn(G3, kn, H, "k_turned")
            pe.wait_ge(sig["gd_edb"], 1)
            if not sample:
                per_h(G1, T, lambda h: kn[:, h], lambda h: qn[:, h], "gd_kq")
            pe.wait_ge(sig["Y_ready"], 1)
            turn_square(Y, "gd_X0")
            if sample:
                pe.wait_ge(sig["gd_qn"], 1)
                per_h(G1, T, lambda h: kn[:, h], lambda h: qn[:, h], "gd_kq")

            def scores(s):
                if s == 0:
                    pe.wait_ge(sig["hg_q"], 2)
                    pe.wait_ge(sig["hg_k"], 2)
                else:
                    pe.wait_ge(sig["lq"], 3 * s)
                if s >= 2:
                    pe.wait_ge(sig["hg_masked"], s - 1)
                a, b = (hk, hq) if s == 0 else (lk[(s - 1) % 2], lq[(s - 1) % 2])
                pairs((H0, H1)[s % 2], a, b, "hg_scores")

            def ml_products():
                pe.wait_ge(sig["ml_a_taken"], 1)
                pe.wait_ge(sig["ml_q"], 2)
                pe.wait_ge(sig["ml_k"], 1)
                pairs(M0, mk, mq, "ml_scores")

            def ml_max_columns():
                pe.wait_ge(sig["ml_M"], 4)
                for h in range(H):
                    mm = pe.matmul(M1[0:T, 16 + h:17 + h], M[:, h], m.c("ident")[:, 0:1], start=True, stop=True)
                mm.then_inc(sig["ml_Mcols"], 1)

            def ml_key_turn():
                pe.wait_ge(sig["ml_P"], 1)
                turn(M0, mk, 2, "ml_k_turned")

            def ml_output():
                pe.wait_ge(sig["ml_P"], 1)
                pe.wait_ge(sig["ml_qw"], 2)
                pe.wait_ge(sig["ml_v"], 2)
                pe.wait_ge(sig["ml_mt"], 1)
                if sample:
                    pe.wait_ge(sig["qx_ready"], 1)
                    pe.wait_ge(sig["C_loaded"], 2 * 16 * H)
                for h in range(H):
                    out = M1[0:T, h * n1:(h + 1) * n1]
                    for b in range(nseq):
                        lhs = mqx[:, h, b] if sample else mqw[:, h]
                        pe.matmul(out, lhs, st["C_ml"][:, h // 2, b], start=(b == 0), stop=False)
                    mm = pe.matmul(out, mW[0:T, h], vext[0:T, h], start=False, stop=True)
                mm.then_inc(sig["ml_num"], 1)

            def delta_products():
                pe.wait_ge(sig["gd_kdec"], H)
                pe.wait_ge(sig["gd_kd"], 1)
                pe.wait_ge(sig["v_taken"], 1)
                if sample:
                    pe.wait_ge(sig["gd_x"], 1)
                    pe.wait_ge(sig["S_gd_loaded"], 16 * H)
                for h in range(H):
                    out = G3[0:T, h * DKG:(h + 1) * DKG]
                    pe.matmul(out, vS[:, h], m.c("ident"), start=True, stop=False)
                    for b in range(nseq):
                        lhs = kx[:, h, b] if sample else kd[:, h]
                        mm = pe.matmul(out, lhs, st["S_gd"][:, h, b], start=False, stop=(b == nseq - 1))
                mm.then_inc(sig["gd_kS"], 1)

            def inverse(lv, *between):
                if lv > 1:
                    pe.wait_ge(sig["X_ready"], lv)
                    turn_square(X, "X_turned")
                pe.wait_ge(sig["AM_ready"], lv)
                pe.wait_ge(sig["X_ready"], lv)
                if lv == 1:
                    pe.wait_ge(sig["gd_A"], H)
                per_h(G0, T, lambda h: AM[lv % 2][0:T, h], lambda h: X[0:T, h], "inv_p1")
                for s in between:
                    scores(s)
                pe.wait_ge(sig["inv_p1_taken"], lv)
                if lv == 1:
                    pe.wait_ge(sig["gd_att"], 1)
                else:
                    pe.wait_ge(sig["Y_taken"], lv - 1)
                per_h(G1, T, lambda h: Y[0:T, h], lambda h: p1[0:T, h], "inv_p2")

            def hg_key_turn():
                pe.wait_ge(sig["hg_kd"], 1)
                pe.wait_ge(sig["hg_masked"], nl + 1)
                turn(H1, hkd, 2, "hg_k_turned")

            def hg_output():
                pe.wait_ge(sig["hg_qe"], 2)
                pe.wait_ge(sig["hg_sum"], nl)
                if sample:
                    pe.wait_ge(sig["S_hg_loaded"], 16 * H)
                for h in range(H):
                    out = H0[0:T, h * DKH:(h + 1) * DKH]
                    for b in range(nseq):
                        lhs = hqx[:, h, b] if sample else hqe[:, h]
                        pe.matmul(out, lhs, st["S_hg"][:, h // 2, b], start=(b == 0), stop=False)
                    mm = pe.matmul(out, hacc[0:T, h], tk(2, I2 + h * DKH, I2 + (h + 1) * DKH), start=False, stop=True)
                mm.then_inc(sig["hg_o"], 1)

            def delta_values():
                pe.wait_ge(sig["gd_r"], 1)
                pe.wait_ge(sig["X_ready"], nl)
                per_h(G1, DKG, lambda h: X[0:T, h], lambda h: r[0:T, h], "gd_u")

            inverse(1, 0)
            if sample:
                scores(1)
                scores(2)
                ml_products()
                ml_max_columns()
                delta_products()
                ml_key_turn()
                ml_output()
                delta_values()
                hg_key_turn()
                pe.wait_ge(sig["ml_ks"], 1)
                pe.wait_ge(sig["hg_kT"], 1)
                pe.wait_ge(sig["values_spread"], 1)
                for i in range(2 * H):
                    h, q = i // 2, i % 2
                    half, j = pair_of(h)
                    if i >= 2:
                        pe.wait_ge(sig["ml_state"], i - 1)
                    pe.matmul((M0, H1)[i % 2][:, 0:4 * n1], mks[0:T, j * P:(j + 1) * P],
                              vx[0:T, h, 4 * q:4 * q + 4].rearrange("p b n -> p (b n)"), start=True, stop=True
                              ).then_inc(sig["ml_delta"], 1)
            else:
                ml_products()
                inverse(2, 1)
                ml_max_columns()
                inverse(3, 2)
                delta_products()
                inverse(4, 3)
                scores(4)
                inverse(5, 5)
                scores(6)
                inverse(6, 7)
                ml_key_turn()
                delta_values()
                ml_output()
                pe.wait_ge(sig["ml_ks"], 1)
                for h in range(H):
                    half, j = pair_of(h)
                    mm = pe.matmul(M0[:, h * n1:(h + 1) * n1], mks[0:T, j * P:(j + 1) * P], vext[0:T, h],
                                   start=True, stop=True)
                mm.then_inc(sig["ml_delta"], 1)
            pe.wait_ge(sig["gd_qd"], 1)
            pe.wait_ge(sig["u_ready"], 1)
            if nl > 2:
                pe.wait_ge(sig["Y_taken"], nl - 2)
            for h in range(H):
                out = G2[0:T, h * DKG:(h + 1) * DKG]
                for b in range(nseq):
                    lhs = qx[:, h, b] if sample else qd[:, h]
                    pe.matmul(out, lhs, st["S_gd"][:, h, b], start=(b == 0), stop=False)
                mm = pe.matmul(out, EB[0:T, h], u[0:T, h], start=False, stop=True)
            mm.then_inc(sig["gd_o"], 1)
            if sample:
                def delta_additions(units):
                    for i in units:
                        h, q = i // 2, i % 2
                        pe.wait_ge(sig["u_spread"], h + 1)
                        if i >= 3:
                            pe.wait_ge(sig["gd_state"], i - 2)
                        pe.matmul((G3, G0, G1)[i % 3][:, :], kdec[0:T, h],
                                  ux[h][0:T, 4 * q:4 * q + 4].rearrange("p b n -> p (b n)"), start=True, stop=True
                                  ).then_inc(sig["gd_delta"], 1)

                delta_additions(range(3))
                hg_output()
                delta_additions(range(3, 2 * H))
            else:
                hg_key_turn()
                hg_output()
            pe.wait_ge(sig["hg_kT"], 1)
            if not sample:
                for h in range(H):
                    half, j = pair_of(h)
                    mm = pe.matmul(H1[:, h * DKH:(h + 1) * DKH], hkdT[0:T, j * P:(j + 1) * P],
                                   tk(2, I2 + h * DKH, I2 + (h + 1) * DKH), start=True, stop=True)
                mm.then_inc(sig["hg_delta"], 1)
            else:
                pe.wait_ge(sig["ml_state"], 2 * H)
                for h in range(H):
                    half, j = pair_of(h)
                    if h >= 2:
                        pe.wait_ge(sig["hg_state"], h - 1)
                    pe.matmul((H1, M0)[h % 2][:, :], hkdT[0:T, j * P:(j + 1) * P],
                              hx[0:T, h].rearrange("p b n -> p (b n)"), start=True, stop=True
                              ).then_inc(sig["hg_delta"], 1)
            if not sample:
                per_h(G3, DKG, lambda h: kdec[0:T, h], lambda h: u[0:T, h], "gd_delta", n=P)
            pe.wait_ge(sig["ml_mt"], 1)
            pe.wait_ge(sig["ml_h"], H)
            pe.wait_ge(sig["mix"], 2 * H)
            for k, kt in enumerate((2, 3, 4, 5)):
                mm = pe.transpose(M1[:, k * T:(k + 1) * T], mix[0:T, kt * P:(kt + 1) * P], ident)
            mm.then_inc(sig["mix_turned"], 1)
            pe.wait_ge(sig["mix"], 3 * H)
            if sample:
                pe.wait_ge(sig["hg_state"], H)
            else:
                pe.wait_ge(sig["ml_state"], H)
            for k, kt in enumerate((0, 1, 6, 7)):
                mm = pe.transpose(M0[:, k * T:(k + 1) * T], mix[0:T, kt * P:(kt + 1) * P], ident)
            mm.then_inc(sig["mix_turned"], 1)


def output_phase(nc, m, d, l, st):
    one = bass.ds(l, 1)
    OUT, UP = D // 512, FF // 256
    DOWN0 = OUT + UP
    silu, rstd = m.silu, m.rstd2
    spare = silu.rearrange("p (k x) n -> p k (x n)", k=2)
    sq = [m.act[:, FT - 6 + k] for k in range(6)] + [spare[:, 0], spare[:, 1]]

    def slot_fill(e):
        return e % SLOTS, (DOWN0 if e % SLOTS < KT else 0) + e // SLOTS

    def spent(sig, e):
        if e % FT == FT - 1:
            return sig["bank_done"], 8 * (DOWN0 + e // FT + 1)
        s = e % SLOTS
        told = len([x for x in range(s, e + 1, SLOTS) if x % FT != FT - 1])
        return sig[f"slot{s}_used"], (DOWN0 if s < KT - 1 else 0) + 1 + told

    def freed(sig, e):
        if e >= SLOTS:
            return spent(sig, e - SLOTS)
        return (sig["bank_done"], 8 * DOWN0) if e == KT - 1 else None

    parts = ExitStack()
    with parts, phase(nc) as (sig, block):
        def tensor(shape, dtype):
            return parts.enter_context(m.tensor(shape, dtype))

        slabs = Slabs(sig, m.down_slab, tensor([SLOTS, 512], F32R), tensor([SLOTS, 512], F32R))
        h = Moving(sig, m.hT, tensor([KT, TOK], F32R), tensor([KT, TOK], F32R))
        first = (tensor([TOK], F32R), tensor([TOK], F32R))

        def act_parts(k):
            return (first[0][:, :], first[1][:, :]) if k == 0 else (h.highs[:, k % KT], h.lows[:, k % KT])

        @block.sync
        def _(sp):
            with sp.Fori(0, OUT) as j:
                for k in range(KT):
                    slabs.load(sp, k, j, rows_of(d["w_out"], one, k, bass.ds(j * 512, 512)))
            store_states(sp, m, d, l, st, "s", m.mcol_s[DSEQ - 1:SAMP:DSEQ, :], sig)
            w = d["w_gate_up"].rearrange("l p (g n) -> l p g n", g=2)
            with sp.Fori(0, UP) as j:
                for k in range(KT):
                    slabs.load(sp, k, OUT + j, w[one, k * P:(k + 1) * P, :, bass.ds(j * 256, 256)]
                               .rearrange("o p g n -> (o p) g n"))
            with sp.Fori(0, 2) as j:
                for k in range(FT):
                    s, n = slot_fill(k)
                    slabs.load(sp, s, n + 2 * j, rows_of(d["w_down"], one, k, bass.ds(j * 512, 512)))
            sp.wait_ge(sig["state_stored"], STORES)

        @block.tensor
        def _(pe):
            slabs.all_free(pe)
            feature_group(pe, m, sig, slabs, h, 0, 0, h_base=0)
            feature_group(pe, m, sig, slabs, h, 1, 1)
            pe.wait_ge(sig["first_banks_read"], 4 + 4 * OUT)
            norm_total(pe, m, sig, sq[0])
            pe.wait_ge(sig["rstd_ln"], 2)
            feature_group(pe, m, sig, slabs, h, OUT, OUT, h_base=KT)
            with pe.Fori(OUT + 1, DOWN0) as g:
                feature_group(pe, m, sig, slabs, h, g, g)
            with pe.Fori(0, 2) as j:
                for k in range(FT):
                    s, n = slot_fill(k)
                    slabs.wait(pe, s, n + 2 * j)
                    pe.wait_ge(sig["act_split"], FT * j + k + 1)
                    for b in range(8):
                        t, half = b // 2, b % 2
                        if k == 0:
                            pe.wait_ge(sig["first_banks_read" if b < 4 else "last_banks_read"],
                                       4 * j + 4 * DOWN0 + b % 4 + 1)
                        tile = slice(t * P, (t + 1) * P)
                        high, low = (x[:, HALF_OF[half]] for x in act_parts(k))
                        mm = three_passes(pe, m.bank[b][:, 0:HALF], slabs.highs[:, s, tile], slabs.lows[:, s, tile],
                                          high, low, k == 0, k == FT - 1)
                        if k == FT - 1:
                            mm.then_inc(sig["bank_done"], 1)
                        elif b == 7:
                            mm.then_inc(slabs.used(s), 1)

        def down(split, tile, evac):
            for e in range(2 * FT):
                if e + 6 < 2 * FT:
                    split(e + 6)
                if e % FT == FT - 1:
                    evac(DOWN0 + e // FT)
                if e + 2 < 2 * FT:
                    tile(e + 2)

        @block.scalar
        def _(act):
            def high(k, n):
                first = isinstance(n, int) and n == 0
                slabs.high(act, k, n, freed=(sig["bank_done"], 8 * n) if k == KT - 1 and not first else None)

            def high_down(e):
                slabs.high(act, *slot_fill(e), freed=freed(sig, e))

            def tile(e):
                if e == 0:
                    act.wait_ge(sig["last_banks_read"], 4 + 4 * (OUT + 1))
                elif e <= FT:
                    act.wait_ge(sig["last_banks_read"], 4 + 4 * DOWN0)
                if e >= KT:
                    act.wait_ge(*spent(sig, e - 2))
                act.copy(act_parts(e % FT)[0], m.act[:, e % FT]).then_inc(sig["act_high"], 1)

            def gates(g):
                for b in range(4):
                    act.wait_ge(sig["bank_done"], 8 * g + b + 1)
                    act.wait_ge(sig["last_banks_read"], 4 * g + b + 1)
                    act.activation(silu[:, b, :], m.bank[b][:, 0:HALF], ACT.Silu).then_inc(sig["first_banks_read"], 1)

            for k in range(3):
                h.high(act, k, wait=False)
            for k in range(KT):
                high(k, 0)
                if k + 3 < KT:
                    h.high(act, k + 3, wait=False)
            for k in range(KT):
                high(k, 1)
            for k in range(6):
                high(k, 2)
                if k >= 2:
                    t = k - 2
                    act.wait_ge(sig["first_banks_read" if t < 2 else "last_banks_read"], 4 + 2 * (t % 2) + 2)
                    norm_square(act, m, sig, t, sq[t])
            for t in range(4):
                act.wait_ge(sig["first_banks_read" if t < 2 else "last_banks_read"], 8 + 2 * (t % 2) + 2)
                norm_square(act, m, sig, 4 + t, sq[4 + t])
            nc.scalar.preload_act_table_set(EXP_LN)
            norm_rstd(act, m, sig, rstd)
            for k in range(KT):
                h.high(act, k)
                if k < 2:
                    high(6 + k, 2)
            with act.Fori(OUT, DOWN0 - 1) as g:
                for k in range(6):
                    high(k, g + 1)
                gates(g)
                for k in (6, 7):
                    high(k, g + 1)
            for e in range(6):
                high_down(e)
            tile(0)
            gates(DOWN0 - 1)
            tile(1)
            down(high_down, tile, lambda g: None)

        @block.vector
        def _(dve):
            def low(s, n):
                slabs.low(dve, s, n)

            def low_down(e):
                slabs.low(dve, *slot_fill(e))

            def tile(e):
                dve.wait_ge(sig["act_high"], e + 1)
                high, low = act_parts(e % FT)
                dve.tensor_tensor(low, m.act[:, e % FT], high.bitcast(F32), ALU.subtract
                                  ).then_inc(sig["act_split"], 1)

            def add(g, j):
                for b in range(8):
                    dve.wait_ge(sig["bank_done"], 8 * g + b + 1)
                    x = m.x[:, 4 * j + b // 2, HALF_OF[b % 2]]
                    dve.tensor_tensor(x, x, m.bank[b][:, 0:HALF], ALU.add
                                      ).then_inc(sig["first_banks_read" if b < 4 else "last_banks_read"], 1)

            def product(g):
                for b in range(4):
                    dve.wait_ge(sig["bank_done"], 8 * g + 4 + b + 1)
                    dve.wait_ge(sig["first_banks_read"], 4 * g + b + 5)
                    out = m.act[:, bass.ds(2 * (g - OUT) + b // 2, 1), HALF_OF[b % 2]]
                    dve.tensor_tensor(out.rearrange("p o n -> p (o n)"), silu[:, b, :], m.bank[4 + b][:, 0:HALF],
                                      ALU.mult).then_inc(sig["last_banks_read"], 1)

            slabs.all_split(dve)
            dve.sem_inc(sig["first_banks_read"], 4)
            dve.sem_inc(sig["last_banks_read"], 4)
            for k in range(3):
                h.low(dve, k)
            for k in range(KT):
                low(k, 0)
                if k + 3 < KT:
                    h.low(dve, k + 3)
            for k in range(6):
                low(k, 1)
            add(0, 0)
            for k in (6, 7):
                low(k, 1)
            for k in range(6):
                low(k, 2)
                if k >= 4:
                    norm_sum(dve, m, sig, k - 2, sq)
            add(1, 1)
            for t in range(4, KT + 1):
                norm_sum(dve, m, sig, t, sq)
            norm_apply(dve, m, sig, h, m.colw[:, 56:64], rstd, lambda k: low(6 + k, 2) if k < 2 else None, KT)
            dve.wait_ge(sig["state_stored"], STORES)
            with dve.Fori(OUT, DOWN0 - 1) as g:
                for k in range(6):
                    low(k, g + 1)
                product(g)
                for k in (6, 7):
                    low(k, g + 1)
            for e in range(6):
                low_down(e)
            tile(0)
            product(DOWN0 - 1)
            tile(1)
            down(low_down, tile, lambda g: add(g, g - DOWN0))


def final_phase(nc, m, d):
    m.top = m.arena
    wrows = m.take(P)
    y = m.take(NT, D)
    sq, rstd = m.take(KT, TOK), m.take(TOK)
    with phase(nc) as (sig, block):
        @block.sync
        def _(sp):
            sp.dma_start(wrows[0:KT, :], d["final_norm_w"].rearrange("(k p) -> k p", p=P)
                         ).then_inc(sig["rows_loaded"], 16)
            for i in range(NT):
                sp.wait_ge(sig["y_even"], i + 1)
                sp.wait_ge(sig["y_odd"], i + 1)
                dst = d["y_prompt"][0, i * P:(i + 1) * P, :] if i < NT - 1 else \
                    d["y_sample"].rearrange("b t n -> (b t) n")
                sp.dma_start(dst, y[0:tile_rows(i), i, :]).then_inc(sig["y_stored"], 16)
            sp.wait_ge(sig["y_stored"], 16 * NT)

        @block.tensor
        def _(pe):
            pe.wait_ge(sig["rows_loaded"], 16)
            pe.transpose(m.bank[7][:, 0:KT], wrows[0:KT, :], m.c("ident", KT)[:, 0:KT]).then_inc(sig["rows_turned"], 1)
            norm_total(pe, m, sig, sq[:, 0])
            pe.wait_ge(sig["h_made"], KT)
            for u in range(2 * NT):
                i, g = u // 2, u % 2
                n = tile_rows(i)
                if u >= 6:
                    pe.wait_ge(sig["y_even" if g == 0 else "y_odd"], (u - 6) // 2 + 1)
                for k in range(4):
                    mm = pe.transpose(m.bank[u % 6][0:n, k * P:(k + 1) * P], m.hT[:, 4 * g + k, i * P:i * P + n],
                                      m.c("ident"))
                mm.then_inc(sig["y_turned"], 1)

        def evacuate(eng, copy, g):
            for i in range(NT):
                n = tile_rows(i)
                u = 2 * i + g
                eng.wait_ge(sig["y_turned"], u + 1)
                copy(y[0:n, i, g * 512:(g + 1) * 512], m.bank[u % 6][0:n, :]
                     ).then_inc(sig["y_even" if g == 0 else "y_odd"], 1)

        @block.scalar
        def _(act):
            for k in range(KT):
                norm_square(act, m, sig, k, sq[:, k])
            norm_rstd(act, m, sig, rstd)
            evacuate(act, act.copy, 0)

        @block.vector
        def _(dve):
            dve.wait_ge(sig["rows_turned"], 1)
            dve.tensor_copy(m.colw[:, 0:KT], m.bank[7][:, 0:KT]).then_inc(sig["colw_ready"], 1)
            for k in range(2, KT + 1):
                norm_sum(dve, m, sig, k, [sq[:, k] for k in range(KT)])
            dve.wait_ge(sig["colw_ready"], 1)
            dve.wait_ge(sig["rstd"], 1)
            for k in range(KT):
                dve.scalar_tensor_tensor(out=m.hT[:, k], in0=m.x[:, k], scalar=m.colw[:, k:k + 1], in1=rstd,
                                         op0=ALU.mult, op1=ALU.mult).then_inc(sig["h_made"], 1)
            evacuate(dve, dve.tensor_copy, 1)


def build(nc, d, const_at, n_const):
    with ExitStack() as stack:
        stack.enter_context(nc.allow_non_contiguous_dma(reason="the states n and m are a few thousand words"))
        m = Memory(nc, stack, const_at, n_const)
        with m.open_area():
            setup_phase(nc, m, d)
        with nc.Fori(0, DEPTH) as l:
            input_phase(nc, m, d, l)
            with m.open_area():
                prep_phase(nc, m, d, l)
                prompt = {"S_gd": m.S_gd, "C_ml": m.C_ml, "S_hg": m.S_hg, "m_ml": m.m_ml}
                with nc.Fori(0, SEQ // P) as c:
                    chunk_phase(nc, m, prompt, 1, c)
                st = sample_states(m)
                chunk_phase(nc, m, st, NSEQ, None, d, l, prompt)
            output_phase(nc, m, d, l, st)
        with m.open_area():
            final_phase(nc, m, d)


_INS = ["x_prompt", "x_sample", "state_mlstm_C", "state_mlstm_n", "state_mlstm_m", "state_gdn_S", "state_gdn_conv",
        "state_hgrn_S", "norm1_w", "w_in", "ml_i_bias", "ml_f_bias", "ml_norm_w", "gd_conv_w", "gd_A_log",
        "gd_dt_bias", "gd_norm_w", "hg_lower_bounds", "hg_norm_w", "w_out", "norm2_w", "w_gate_up", "w_down",
        "final_norm_w"]


def _states(who, b):
    return [(who + "_C", (DEPTH, b, H, DKM, DKM)), (who + "_n", (DEPTH, b, H, DKM)), (who + "_m", (DEPTH, b, H)),
            (who + "_S", (DEPTH, b, H, DKG, DKG)), (who + "_conv", (DEPTH, b, CONV - 1, 3 * H * DKG)),
            (who + "_H", (DEPTH, b, H, DKH, DKH))]


_OUTS = [("y_prompt", (1, SEQ, D)), ("y_sample", (NSEQ, DSEQ, D))] + _states("p", 1) + _states("s", NSEQ)


def kernel(**inputs):
    import concourse.bacc as bacc
    from concourse.bass_utils import run_bass_kernel_spmd as run

    nc = bacc.Bacc("TRN2", target_bir_lowering=False, num_devices=1)
    consts, const_at = constants()
    arrays, d = {"in_consts": consts}, {}
    for name in _INS:
        arrays["in_" + name] = np.ascontiguousarray(inputs[name])
    for name, a in arrays.items():
        d[name[3:]] = nc.dram_tensor(name, a.shape, mybir.dt.from_np(a.dtype), kind="ExternalInput").ap()
    for name, shape in _OUTS:
        d[name] = nc.dram_tensor("out_" + name, shape, F32, kind="ExternalOutput").ap()
    build(nc, d, const_at, consts.shape[1])
    r = run(nc, [arrays], core_ids=[0])
    return tuple(r.results[0]["out_" + name] for name, _ in _OUTS)
```
